# Optimizing a Trainium2 kernel written in Bass

```python
import math
import jax, jax.numpy as jnp
from jax import lax
import numpy as np

D_MODEL = 1024
BATCH = 1
SEQ = 1024
DEPTH = 1
DEC_BATCH = 1
DEC_SEQ = 32
PAST_LEN = 128

CHUNK = 64
Q_BLOCK = 128
T_BLOCK = 256
N_MEM = 256
EPS = 1e-6
NEG_INF = -1e30
MLA_HEADS = 8
MLA_Q_LORA = 384
MLA_KV_LORA = 256
MLA_NOPE = 64
MLA_ROPE = 32
MLA_V = 64
ROPE_THETA = 10000.0
MLA_SCALE = (MLA_NOPE + MLA_ROPE) ** -0.5
DIFF_HEADS = 8
DIFF_DH = 32
DIFF_V = 2 * DIFF_DH
DIFF_SCALE = DIFF_DH ** -0.5
MEM_HEADS = 4
MEM_DH = 128
MEM_SCALE = MEM_DH ** -0.5
PEER_HEADS = 8
PEER_NKEYS = 128
PEER_EXPERTS = PEER_NKEYS * PEER_NKEYS
PEER_DKEY = 256
PEER_HALF = PEER_DKEY // 2
PEER_TOPK = 16
BR_A = MLA_HEADS * MLA_V
BR_B = DIFF_HEADS * DIFF_V
BR_M = MEM_HEADS * MEM_DH
IN_SIZES = (MLA_Q_LORA, MLA_KV_LORA, MLA_ROPE, DIFF_HEADS * 2 * DIFF_DH, DIFF_HEADS * 2 * DIFF_DH, BR_B, BR_M)
IN_WIDTH = MLA_Q_LORA + MLA_KV_LORA + MLA_ROPE + 3 * DIFF_HEADS * 2 * DIFF_DH + BR_M
IN_OFFSETS = [MLA_Q_LORA,
              MLA_Q_LORA + MLA_KV_LORA,
              MLA_Q_LORA + MLA_KV_LORA + MLA_ROPE,
              MLA_Q_LORA + MLA_KV_LORA + MLA_ROPE + DIFF_HEADS * 2 * DIFF_DH,
              MLA_Q_LORA + MLA_KV_LORA + MLA_ROPE + 2 * DIFF_HEADS * 2 * DIFF_DH,
              MLA_Q_LORA + MLA_KV_LORA + MLA_ROPE + 3 * DIFF_HEADS * 2 * DIFF_DH]

kernel_name = "streaming_hybrid_mla_diffattn_peer_step"

def _rmsnorm(x, g):
    xf = x.astype(jnp.float32)
    y = xf * lax.rsqrt(jnp.mean(xf * xf, axis=-1, keepdims=True) + EPS)
    return (y * g.astype(jnp.float32)).astype(x.dtype)

def _rope(x, pos):
    half = MLA_ROPE // 2
    inv = 1.0 / (ROPE_THETA ** (jnp.arange(half, dtype=jnp.float32) / half))
    ang = pos.astype(jnp.float32)[:, None] * inv[None, :]
    shp = (1, ang.shape[0]) + (1,) * (x.ndim - 3) + (half,)
    cos = jnp.cos(ang).reshape(shp)
    sin = jnp.sin(ang).reshape(shp)
    x1 = x[..., :half].astype(jnp.float32)
    x2 = x[..., half:].astype(jnp.float32)
    return jnp.concatenate([x1 * cos - x2 * sin, x2 * cos + x1 * sin], axis=-1).astype(x.dtype)

def _chunk_mask(q_pos, k_pos):
    return (k_pos[None, :] // CHUNK) <= (q_pos[:, None] // CHUNK)

def _sweep_queries(fn, q_args, q_pos):
    s = q_pos.shape[0]
    if s <= Q_BLOCK or s % Q_BLOCK:
        return fn(*q_args, q_pos)
    nb = s // Q_BLOCK

    def split(a):
        return jnp.moveaxis(a.reshape((a.shape[0], nb, Q_BLOCK) + a.shape[2:]), 1, 0)

    blocks = tuple(split(a) for a in q_args) + (q_pos.reshape(nb, Q_BLOCK),)
    out = lax.map(lambda a: fn(*a), blocks)
    out = jnp.moveaxis(out, 0, 1)
    return out.reshape((out.shape[0], s) + out.shape[3:])

def _mla_attend(q_nope, q_rope, q_pos, k_nope, k_rope, v, k_pos):
    def blk(qn, qr, qp):
        s = (jnp.einsum("bqhd,bkhd->bhqk", qn, k_nope)
             + jnp.einsum("bqhd,bkd->bhqk", qr, k_rope)).astype(jnp.float32) * MLA_SCALE
        s = jnp.where(_chunk_mask(qp, k_pos)[None, None], s, NEG_INF)
        p = jax.nn.softmax(s, axis=-1).astype(v.dtype)
        return jnp.einsum("bhqk,bkhd->bqhd", p, v)
    return _sweep_queries(blk, (q_nope, q_rope), q_pos)

def _diff_attend(q, q_pos, k, v, k_pos, lam):
    slopes = jnp.exp2(-8.0 * jnp.arange(1, DIFF_HEADS + 1, dtype=jnp.float32) / DIFF_HEADS)

    def blk(qb, qp):
        s = jnp.einsum("bqhjd,bkhjd->bhjqk", qb, k).astype(jnp.float32) * DIFF_SCALE
        dist = jnp.abs(qp[:, None] - k_pos[None, :]).astype(jnp.float32)
        s = s - (slopes[:, None, None] * dist[None])[None, :, None]
        s = jnp.where(_chunk_mask(qp, k_pos)[None, None, None], s, NEG_INF)
        p = jax.nn.softmax(s, axis=-1)
        a = (p[:, :, 0] - lam * p[:, :, 1]).astype(v.dtype)
        return jnp.einsum("bhqk,bkhd->bqhd", a, v)
    return _sweep_queries(blk, (q,), q_pos)

def _mem_kv(mem, g, w):
    b, m, _ = mem.shape
    kv = jnp.einsum("bmd,de->bme", _rmsnorm(mem, g), w)
    k, v = jnp.split(kv, 2, axis=-1)
    return k.reshape(b, m, MEM_HEADS, MEM_DH), v.reshape(b, m, MEM_HEADS, MEM_DH)

def _mem_attend(q, mem_k, mem_v):
    s = jnp.einsum("bqhd,bmhd->bhqm", q, mem_k).astype(jnp.float32) * MEM_SCALE
    p = jax.nn.softmax(s, axis=-1).astype(mem_v.dtype)
    return jnp.einsum("bhqm,bmhd->bqhd", p, mem_v)

def _peer(h, wq, subkeys, u, v):
    b, s, d = h.shape
    n = b * s
    n_pad = -(-n // T_BLOCK) * T_BLOCK
    t = jnp.pad(h.reshape(n, d), ((0, n_pad - n), (0, 0)))

    def blk(tb):
        q = jnp.einsum("td,de->te", tb, wq).reshape(-1, PEER_HEADS, 2, PEER_HALF)
        sc = jnp.einsum("thjd,hjnd->thjn", q, subkeys).astype(jnp.float32)
        s1, i1 = lax.top_k(sc[:, :, 0], PEER_TOPK)
        s2, i2 = lax.top_k(sc[:, :, 1], PEER_TOPK)
        cand = (s1[..., :, None] + s2[..., None, :]).reshape(-1, PEER_HEADS, PEER_TOPK * PEER_TOPK)
        cidx = (i1[..., :, None] * PEER_NKEYS + i2[..., None, :]).reshape(-1, PEER_HEADS, PEER_TOPK * PEER_TOPK)
        best, sel = lax.top_k(cand, PEER_TOPK)
        idx = jnp.take_along_axis(cidx, sel, axis=-1)
        g = jax.nn.softmax(best, axis=-1).astype(tb.dtype)
        ue = jnp.take(u, idx, axis=0)
        ve = jnp.take(v, idx, axis=0)
        a = jax.nn.gelu(jnp.einsum("thkd,td->thk", ue, tb), approximate=False)
        return jnp.einsum("thk,thkd->td", g * a, ve)

    if n_pad == T_BLOCK:
        out = blk(t)
    else:
        out = lax.map(blk, t.reshape(-1, T_BLOCK, d)).reshape(n_pad, d)
    return out[:n].reshape(b, s, d)

def _layer(x, pos, past, mem_k, mem_v, p, layer):
    b, s, _ = x.shape
    h = _rmsnorm(x, p["norm_mix"])
    z = jnp.einsum("bsd,de->bse", h, p["w_in"])
    c_q, c_kv, k_r, d_q, d_k, d_v, m_q = jnp.split(z, IN_OFFSETS, axis=-1)

    q = jnp.einsum("bsr,re->bse", _rmsnorm(c_q, p["mla_q_norm"]), p["w_uq"])
    q = q.reshape(b, s, MLA_HEADS, MLA_NOPE + MLA_ROPE)
    q_nope = q[..., :MLA_NOPE]
    q_rope = _rope(q[..., MLA_NOPE:], pos)
    c_kv = _rmsnorm(c_kv, p["mla_kv_norm"])
    k_r = _rope(k_r, pos)
    d_k = d_k.reshape(b, s, DIFF_HEADS, DIFF_V)
    d_v = d_v.reshape(b, s, DIFF_HEADS, DIFF_V)
    new_rows = (c_kv, k_r, d_k, d_v)
    if past is None:
        ckv_all, kr_all, dk_all, dv_all = new_rows
        k_pos = pos
    else:
        ckv_all, kr_all, dk_all, dv_all = [jnp.concatenate([c, r], axis=1) for c, r in zip(past, new_rows)]
        k_pos = jnp.arange(past[0].shape[1] + s, dtype=jnp.int32)
    kk = ckv_all.shape[1]
    k_nope = jnp.einsum("bkr,re->bke", ckv_all, p["w_uk"]).reshape(b, kk, MLA_HEADS, MLA_NOPE)
    v_mla = jnp.einsum("bkr,re->bke", ckv_all, p["w_uv"]).reshape(b, kk, MLA_HEADS, MLA_V)
    o_a = _mla_attend(q_nope, q_rope, pos, k_nope, kr_all, v_mla, k_pos).reshape(b, s, BR_A)

    lam_init = 0.8 - 0.6 * math.exp(-0.3 * layer)
    lam = (jnp.exp(jnp.sum(p["diff_lq1"].astype(jnp.float32) * p["diff_lk1"].astype(jnp.float32)))
           - jnp.exp(jnp.sum(p["diff_lq2"].astype(jnp.float32) * p["diff_lk2"].astype(jnp.float32)))
           + lam_init)
    o_b = _diff_attend(d_q.reshape(b, s, DIFF_HEADS, 2, DIFF_DH), pos,
                       dk_all.reshape(b, kk, DIFF_HEADS, 2, DIFF_DH), dv_all, k_pos, lam)
    o_b = (_rmsnorm(o_b, p["diff_subln"]) * (1.0 - lam_init)).reshape(b, s, BR_B)

    o_m = _mem_attend(m_q.reshape(b, s, MEM_HEADS, MEM_DH), mem_k, mem_v).reshape(b, s, BR_M)

    gates = jax.nn.sigmoid((jnp.einsum("bsd,de->bse", h, p["w_gate"]) + p["b_gate"]).astype(jnp.float32)).astype(x.dtype)
    g_a, g_b, g_m = jnp.split(gates, 3, axis=-1)
    merged = (g_a * jnp.einsum("bse,ed->bsd", o_a, p["w_br_a"])
              + g_b * jnp.einsum("bse,ed->bsd", o_b, p["w_br_b"])
              + g_m * jnp.einsum("bse,ed->bsd", o_m, p["w_br_m"]))
    x = x + jnp.einsum("bsd,de->bse", merged, p["w_o"])

    x = x + _peer(_rmsnorm(x, p["norm_ffn"]), p["peer_wq"], p["peer_subkeys"], p["peer_u"], p["peer_v"])
    return x, new_rows

def setup_inputs(seed: int = 0) -> dict:
    key = jax.random.key(seed)
    ks = jax.random.split(key, 40)
    f32 = jnp.float32

    def nrm(k, shape, scale=1.0):
        return jax.random.normal(k, shape, f32) * scale

    def gain(k, shape):
        return 1.0 + 0.01 * jax.random.normal(k, shape, f32)

    L = DEPTH
    return {
        "x_prompt": nrm(ks[0], (BATCH, SEQ, D_MODEL)),
        "x_sample": nrm(ks[1], (DEC_BATCH, DEC_SEQ, D_MODEL)),
        "cache_mla_ckv": nrm(ks[2], (L, DEC_BATCH, PAST_LEN, MLA_KV_LORA)),
        "cache_mla_krope": nrm(ks[3], (L, DEC_BATCH, PAST_LEN, MLA_ROPE)),
        "cache_diff_k": nrm(ks[4], (L, DEC_BATCH, PAST_LEN, DIFF_HEADS, DIFF_V)),
        "cache_diff_v": nrm(ks[5], (L, DEC_BATCH, PAST_LEN, DIFF_HEADS, DIFF_V)),
        "cache_mem_k": nrm(ks[6], (L, DEC_BATCH, N_MEM, MEM_HEADS, MEM_DH)),
        "cache_mem_v": nrm(ks[7], (L, DEC_BATCH, N_MEM, MEM_HEADS, MEM_DH)),
        "mem_prompt": nrm(ks[8], (BATCH, N_MEM, D_MODEL)),
        "norm_mix": gain(ks[9], (L, D_MODEL)),
        "w_in": nrm(ks[10], (L, D_MODEL, IN_WIDTH), D_MODEL ** -0.5),
        "mla_q_norm": gain(ks[11], (L, MLA_Q_LORA)),
        "w_uq": nrm(ks[12], (L, MLA_Q_LORA, MLA_HEADS * (MLA_NOPE + MLA_ROPE)), MLA_Q_LORA ** -0.5),
        "mla_kv_norm": gain(ks[13], (L, MLA_KV_LORA)),
        "w_uk": nrm(ks[14], (L, MLA_KV_LORA, MLA_HEADS * MLA_NOPE), MLA_KV_LORA ** -0.5),
        "w_uv": nrm(ks[15], (L, MLA_KV_LORA, MLA_HEADS * MLA_V), MLA_KV_LORA ** -0.5),
        "diff_lq1": nrm(ks[16], (L, DIFF_DH), 0.1),
        "diff_lk1": nrm(ks[17], (L, DIFF_DH), 0.1),
        "diff_lq2": nrm(ks[18], (L, DIFF_DH), 0.1),
        "diff_lk2": nrm(ks[19], (L, DIFF_DH), 0.1),
        "diff_subln": gain(ks[20], (L, DIFF_V)),
        "norm_mem": gain(ks[21], (L, D_MODEL)),
        "w_mem_kv": nrm(ks[22], (L, D_MODEL, 2 * MEM_HEADS * MEM_DH), D_MODEL ** -0.5),
        "w_br_a": nrm(ks[23], (L, BR_A, D_MODEL), BR_A ** -0.5),
        "w_br_b": nrm(ks[24], (L, BR_B, D_MODEL), BR_B ** -0.5),
        "w_br_m": nrm(ks[25], (L, BR_M, D_MODEL), BR_M ** -0.5),
        "w_gate": nrm(ks[26], (L, D_MODEL, 3 * D_MODEL), D_MODEL ** -0.5),
        "b_gate": nrm(ks[27], (L, 3 * D_MODEL), 0.01),
        "w_o": nrm(ks[28], (L, D_MODEL, D_MODEL), D_MODEL ** -0.5),
        "norm_ffn": gain(ks[29], (L, D_MODEL)),
        "peer_wq": nrm(ks[30], (L, D_MODEL, PEER_HEADS * PEER_DKEY), D_MODEL ** -0.5),
        "peer_subkeys": nrm(ks[31], (L, PEER_HEADS, 2, PEER_NKEYS, PEER_HALF), PEER_HALF ** -0.5),
        "peer_u": nrm(ks[32], (L, PEER_EXPERTS, D_MODEL), D_MODEL ** -0.5),
        "peer_v": nrm(ks[33], (L, PEER_EXPERTS, D_MODEL), 0.5),
        "norm_final": gain(ks[34], (D_MODEL,)),
    }

def reference(x_prompt, x_sample, cache_mla_ckv, cache_mla_krope, cache_diff_k, cache_diff_v,
              cache_mem_k, cache_mem_v, mem_prompt, norm_mix, w_in, mla_q_norm, w_uq, mla_kv_norm,
              w_uk, w_uv, diff_lq1, diff_lk1, diff_lq2, diff_lk2, diff_subln, norm_mem, w_mem_kv,
              w_br_a, w_br_b, w_br_m, w_gate, b_gate, w_o, norm_ffn, peer_wq, peer_subkeys,
              peer_u, peer_v, norm_final):
    pos_p = jnp.arange(x_prompt.shape[1], dtype=jnp.int32)
    past_len = cache_mla_ckv.shape[2]
    pos_s = past_len + jnp.arange(x_sample.shape[1], dtype=jnp.int32)
    xp, xs = x_prompt, x_sample
    p_ckv, p_kr, p_dk, p_dv, p_mk, p_mv = [], [], [], [], [], []
    s_ckv, s_kr, s_dk, s_dv = [], [], [], []
    for l in range(DEPTH):
        prm = {
            "norm_mix": norm_mix[l], "w_in": w_in[l], "mla_q_norm": mla_q_norm[l], "w_uq": w_uq[l],
            "mla_kv_norm": mla_kv_norm[l], "w_uk": w_uk[l], "w_uv": w_uv[l],
            "diff_lq1": diff_lq1[l], "diff_lk1": diff_lk1[l], "diff_lq2": diff_lq2[l],
            "diff_lk2": diff_lk2[l], "diff_subln": diff_subln[l],
            "w_br_a": w_br_a[l], "w_br_b": w_br_b[l], "w_br_m": w_br_m[l],
            "w_gate": w_gate[l], "b_gate": b_gate[l], "w_o": w_o[l], "norm_ffn": norm_ffn[l],
            "peer_wq": peer_wq[l], "peer_subkeys": peer_subkeys[l], "peer_u": peer_u[l], "peer_v": peer_v[l],
        }
        mk, mv = _mem_kv(mem_prompt, norm_mem[l], w_mem_kv[l])
        xp, rows_p = _layer(xp, pos_p, None, mk, mv, prm, l)
        past = (cache_mla_ckv[l], cache_mla_krope[l], cache_diff_k[l], cache_diff_v[l])
        xs, rows_s = _layer(xs, pos_s, past, cache_mem_k[l], cache_mem_v[l], prm, l)
        p_ckv.append(rows_p[0]); p_kr.append(rows_p[1]); p_dk.append(rows_p[2]); p_dv.append(rows_p[3])
        p_mk.append(mk); p_mv.append(mv)
        s_ckv.append(rows_s[0]); s_kr.append(rows_s[1]); s_dk.append(rows_s[2]); s_dv.append(rows_s[3])
    y_prompt = _rmsnorm(xp, norm_final)
    y_sample = _rmsnorm(xs, norm_final)
    return (y_prompt, y_sample,
            jnp.stack(p_ckv), jnp.stack(p_kr), jnp.stack(p_dk), jnp.stack(p_dv),
            jnp.stack(p_mk), jnp.stack(p_mv),
            jnp.stack(s_ckv), jnp.stack(s_kr), jnp.stack(s_dk), jnp.stack(s_dv))


_drawn_inputs = setup_inputs


def setup_inputs(seed=0):
    import zlib

    import numpy as np

    out = dict(_drawn_inputs(seed))
    spreads = {}
    factors = {'mla_q_norm': 8.0,
     'mla_kv_norm': 21.951,
     'diff_lq1': 9.608,
     'diff_subln': 110.124,
     'norm_mem': 19.509,
     'b_gate': 5.854,
     'norm_final': 185.591,
     'cache_mla_ckv': 8.0,
     'cache_mla_krope': 8.0,
     'cache_mem_k': 3.715,
     'cache_mem_v': 3.054,
     'diff_lk2': 3.713,
     'norm_ffn': 36.925}
    for name, (base, spread) in spreads.items():
        noise = np.random.default_rng([zlib.crc32(name.encode()), seed]).standard_normal(out[name].shape)
        drawn = base * np.exp(spread * noise) if base else spread * noise
        out[name] = __import__('jax').numpy.asarray(drawn.astype(out[name].dtype))
    for name, factor in factors.items():
        out[name] = (out[name] * factor).astype(out[name].dtype)
    return out
```

```python
from contextlib import ExitStack

import numpy as np

import concourse.bass as bass
from concourse import mybir

F32 = mybir.dt.float32
I32 = mybir.dt.int32
U32 = mybir.dt.uint32
ALU = mybir.AluOpType
ACT = mybir.ActivationFunctionType
AX = mybir.AxisListType.X

P = 128
D = 1024
DC = D // P
SEQ, DEC, PAST = 1024, 32, 128
TOK = SEQ + DEC
TILES = -(-TOK // P)
ROWS = TILES * P
PAD_ROWS = ROWS + 2 * P
CACHE = ROWS
KEYS = ROWS + PAST
MEM = 256
EPS = 1e-6
HEADS = 8
NOPE, ROPE, VD = 64, 32, 64
QK = NOPE + ROPE
Q_LORA, KV_LORA = 384, 256
BR = 512
DDH = 32
MEM_HEADS, MDH = 4, 128
MLA_SCALE = QK ** -0.5
DIFF_SCALE = DDH ** -0.5
MEM_SCALE = MDH ** -0.5
CHUNK = 64
TOPK = 16
ATOMS = HEADS * TOPK
Z_CUTS = [0, Q_LORA, Q_LORA + KV_LORA + ROPE]
Z_CUTS += [Z_CUTS[-1] + BR * (i + 1) for i in range(4)]
Z_COLS = list(zip(Z_CUTS[:-1], Z_CUTS[1:]))
IN_W = Z_CUTS[-1]


def until(eng, sem, value, passed):
    eng.wait_ge(sem, value)
    if not isinstance(value, int):
        eng.sem_inc(passed, 1)


def clear(nc, sems):
    with nc.Block() as block:
        @block.gpsimd
        def _(pool):
            nc.clear_and_free_semaphores(sems)


def tools(nc, ctx, tag):
    sems = []
    ctx.callback(clear, nc, sems)

    def sb(name, shape, dt=F32):
        return ctx.enter_context(nc.sbuf_tensor(f"{tag}_{name}", shape, dt))

    def psum(name, shape):
        return ctx.enter_context(nc.psum_tensor(f"{tag}_{name}", shape, F32))

    def sem(name):
        sems.append(nc.alloc_semaphore(name=f"{tag}_{name}"))
        return sems[-1]
    return sb, psum, sem


def beside(ex, kind, eng, tile, steps, i, of, half=None):
    if ex:
        groups = len(steps) // TOPK
        q = next(q for q in range(groups) if i < of * (q + 1) // groups)
        first, last = of * q // groups, of * (q + 1) // groups
        share = range(TOPK * (i - first) // (last - first), TOPK * (i - first + 1) // (last - first))
        if half is not None:
            share = (share[:len(share) // 2], share[len(share) // 2:])[half]
        for c in share:
            ex.atom(kind, eng, tile, steps.start + q * TOPK + c)


def make_identity(pool, ident, made):
    pool.memset(ident[:, :], 0.0).then_inc(made, 1)
    pool.wait_ge(made, 1)
    pool.affine_select(out=ident[:, :], in_=ident[:, :], compare_op=ALU.not_equal, fill=1.0, base=0,
                       pattern=[[-1, P]], channel_multiplier=1).then_inc(made, 1)


def project_inputs(nc, a, s):
    MMS, TURNS = 10, 11
    with ExitStack() as ctx:
        sb, psum, sem = tools(nc, ctx, "A")
        ident = sb("ident", [P, P])
        w_in = sb("w_in", [P, DC, IN_W])
        w_uq = sb("w_uq", [P, Q_LORA // P, HEADS * QK])
        w_uk = sb("w_uk", [P, KV_LORA // P, BR])
        w_uv = sb("w_uv", [P, KV_LORA // P, BR])
        g_mix, g_q, g_kv = sb("g_mix", [P, D]), sb("g_q", [P, Q_LORA]), sb("g_kv", [P, KV_LORA])
        xt = [sb(f"xt{i}", [P, D]) for i in range(2)]
        cs = [sb(f"cs{i}", [P, ROPE]) for i in range(2)]
        junk = sb("junk", [P, D])
        xn = sb("xn", [P, D])
        hT = [sb(f"hT{i}", [P, DC, P]) for i in range(2)]
        ms, root, rs = sb("ms", [P, 4]), sb("root", [P, 4]), sb("rs", [P, 4])
        cq, kv = sb("cq", [P, Q_LORA]), sb("kv", [P, KV_LORA + ROPE])
        cqn, kvn, krr = sb("cqn", [P, Q_LORA]), sb("kvn", [P, KV_LORA]), sb("krr", [P, ROPE])
        cqT, kvT = sb("cqT", [P, Q_LORA]), sb("kvT", [P, KV_LORA])
        dq = [sb(f"dq{i}", [P, BR]) for i in range(2)]
        dk = [sb(f"dk{i}", [P, BR]) for i in range(2)]
        dv = [sb(f"dv{i}", [P, BR]) for i in range(2)]
        mq = [sb(f"mq{i}", [P, BR]) for i in range(2)]
        q_sb, k_sb, v_sb = sb("q_sb", [P, HEADS, QK]), sb("k_sb", [P, HEADS, QK]), sb("v_sb", [P, BR])
        rot = sb("rot", [P, 4, HEADS, ROPE // 2])
        kT, qT = sb("kT", [P, HEADS, P]), sb("qT", [P, HEADS, P])
        dkT, dqT, mqT = sb("dkT", [P, 4, P]), sb("dqT", [P, 4, P]), sb("mqT", [P, 4, P])
        ps_t = [psum(f"turn{i}", [P, 512]) for i in range(2)]
        ps_m = [psum(f"mm{i}", [P, 512]) for i in range(4)]

        made, passed = sem("identity"), sem("loop_waits")
        w_z = [sem(f"w_in{i}") for i in range(6)]
        w_up, gains = sem("w_up"), sem("gains")
        x_in = [sem(f"x_in{i}") for i in range(2)]
        cs_in = [sem(f"cs_in{i}") for i in range(2)]
        squares, roots, normed = sem("squares"), sem("roots"), sem("normed")
        turned, t_copied = sem("turned"), sem("t_copied")
        mm_done, m_copied = sem("mm_done"), sem("m_copied")
        heads_ready, latents_done, roped = sem("heads_ready"), sem("latents_done"), sem("q_roped")
        v_out, kv_out = sem("v_out"), sem("kv_out")
        h_out = [sem(f"h_out{i}") for i in range(2)]
        d_out = [sem(f"d_out{i}") for i in range(2)]
        t_out = {k: sem(f"{k}_out") for k in ("kT", "qT", "dkT", "dqT", "mqT")}
        block = ctx.enter_context(nc.Block())

        @block.gpsimd
        def _(pool):
            make_identity(pool, ident, made)
            for j in range(2):
                pool.dma_start(xt[j][:, :], a["x_all"][j * P:(j + 1) * P, :]).then_inc(x_in[j], 16)
                pool.dma_start(cs[j][:, :], a["cos_sin"][j * P:(j + 1) * P, :]).then_inc(cs_in[j], 16)
            until(pool, normed, 1, passed)
            pool.dma_start(xt[0][:, :], a["x_all"][2 * P:3 * P, :]).then_inc(x_in[0], 16)
            with pool.Fori(0, TILES // 2) as g:
                for par in range(2):
                    j = g * 2 + par
                    until(pool, roped, j + 1, passed)
                    pool.dma_start(cs[par][:, :], a["cos_sin"][bass.ds(j * P + 2 * P, P), :]).then_inc(cs_in[par], 16)
                    until(pool, normed, j + 2, passed)
                    pool.dma_start(xt[1 - par][:, :], a["x_all"][bass.ds(j * P + 3 * P, P), :]).then_inc(x_in[1 - par], 16)

        @block.sync
        def _(sp):
            for w, name in ((g_mix, "norm_mix"), (g_q, "mla_q_norm"), (g_kv, "mla_kv_norm")):
                sp.dma_start(w[:, :], a[name].to_broadcast(list(w.shape))).then_inc(gains, 16)
            w_view = a["w_in"].rearrange("(c p) n -> p c n", p=P)
            for i, (lo, hi) in enumerate(Z_COLS):
                sp.dma_start(w_in[:, :, lo:hi], w_view[:, :, lo:hi]).then_inc(w_z[i], 16)
            for w, name in ((w_uq, "w_uq"), (w_uk, "w_uk"), (w_uv, "w_uv")):
                sp.dma_start(w[:, :, :], a[name].rearrange("(c p) n -> p c n", p=P)).then_inc(w_up, 16)

            def rows(t):
                return slice(t * P, (t + 1) * P) if isinstance(t, int) else bass.ds(t * P, P)

            def store_projected(t, par, mm0, tn0):
                until(sp, t_copied, tn0 + 2, passed)
                sp.dma_start(s["hT"].rearrange("c p n -> p c n")[:, :, rows(t)], hT[par][:, :, :]).then_inc(h_out[par], 16)
                until(sp, latents_done, t + 1, passed)
                sp.dma_start(s["ckv"][rows(t), :], kvn[:, :]).then_inc(kv_out, 16)
                sp.dma_start(s["krope"][rows(t), :], krr[:, :]).then_inc(kv_out, 16)
                until(sp, m_copied, mm0 + 5, passed)
                sp.dma_start(s["dk"][rows(t), :], dk[par][:, :]).then_inc(d_out[par], 16)
                sp.dma_start(s["dv"][rows(t), :], dv[par][:, :]).then_inc(d_out[par], 16)

            def store_values(t):
                until(sp, m_copied, t * MMS + 10, passed)
                sp.dma_start(s["vm"][rows(t), :], v_sb[:, :]).then_inc(v_out, 16)

            def store_turned(t):
                for n, (name, buf, top) in {5: ("kT", kT, QK), 7: ("qT", qT, QK), 8: ("dkT", dkT, P),
                                            9: ("dqT", dqT, P), 10: ("mqT", mqT, P)}.items():
                    until(sp, t_copied, t * TURNS + (2 + n + 1), passed)
                    sp.dma_start(s[name].rearrange("c p n -> p c n")[:, :, rows(t)], buf[0:top, :, :]).then_inc(t_out[name], 16)

            store_projected(0, 0, 0, 0)
            with sp.Fori(0, TILES // 2) as g:
                for par in range(2):
                    j = g * 2 + par
                    store_values(j)
                    store_projected(j + 1, 1 - par, j * MMS + 10, j * TURNS + 4)
                    store_turned(j)
            store_values(TILES - 1)
            store_turned(TILES - 1)
            sp.wait_ge(v_out, 16 * TILES)
            sp.wait_ge(kv_out, 32 * TILES)
            for i in range(2):
                sp.wait_ge(h_out[i], 16 * ((TILES + 1 - i) // 2))
                sp.wait_ge(d_out[i], 32 * ((TILES + 1 - i) // 2))
            for q in t_out.values():
                sp.wait_ge(q, 16 * TILES)

        @block.tensor
        def _(pe):
            def turn(n, bank, blocks, top):
                if not (isinstance(n, int) and n < 2):
                    until(pe, t_copied, n - 1, passed)
                for b, src in enumerate(blocks):
                    last = pe.transpose(ps_t[bank][0:top, b * P:(b + 1) * P], src, ident[:, :])
                last.then_inc(turned, 1)

            def product(n, bank, lhs, w, lo, hi):
                if not (isinstance(n, int) and n < 4):
                    until(pe, m_copied, n - 3, passed)
                for c in range(len(lhs)):
                    last = pe.matmul(ps_m[bank][:, 0:hi - lo], lhs[c], w[:, c, lo:hi], start=(c == 0),
                                     stop=(c == len(lhs) - 1))
                last.then_inc(mm_done, 1)

            def chunks(buf, lo, hi):
                return [buf[:, c * P:(c + 1) * P] for c in range(lo, hi)]

            def turn_h(n, bank):
                turn(n, bank, chunks(xn, 0, 4), P)
                turn(n + 1, 1 - bank, chunks(xn, 4, 8), P)

            def project(n, bank, par, first):
                for i, (lo, hi) in enumerate(Z_COLS):
                    if first:
                        pe.wait_ge(w_z[i], 16)
                    product(n + i, (bank + i) % 4, [hT[par][:, c, :] for c in range(DC)], w_in, lo, hi)

            def latents(j, par):
                until(pe, normed, j + 2, passed)
                turn(j * TURNS + 2, par, chunks(cqn, 0, 3), P)
                turn(j * TURNS + 3, 1 - par, chunks(kvn, 0, 2), P)

            def ups(j, par):
                n, bank = j * MMS + 6, (2 + 2 * par) % 4
                until(pe, t_copied, j * TURNS + 4, passed)
                product(n, bank, chunks(cqT, 0, 3), w_uq, 0, 512)
                product(n + 1, (bank + 1) % 4, chunks(cqT, 0, 3), w_uq, 512, HEADS * QK)
                product(n + 2, (bank + 2) % 4, chunks(kvT, 0, 2), w_uk, 0, BR)
                product(n + 3, (bank + 3) % 4, chunks(kvT, 0, 2), w_uv, 0, BR)

            def turn_heads(j, par):
                until(pe, heads_ready, j + 1, passed)
                n, bank = j * TURNS + 6, par
                for i, (buf, h) in enumerate(((k_sb, 0), (k_sb, 4), (q_sb, 0), (q_sb, 4))):
                    turn(n + i, (bank + i) % 2, [buf[:, h + b, :] for b in range(4)], QK)
                for i, buf in enumerate((dk[par], dq[par], mq[par])):
                    turn(n + 4 + i, (bank + i) % 2, chunks(buf, 0, 4), P)

            pe.wait_ge(made, 2)
            pe.wait_ge(normed, 1)
            turn_h(0, 0)
            pe.wait_ge(t_copied, 2)
            project(0, 0, 0, True)
            pe.wait_ge(w_up, 48)
            with pe.Fori(0, TILES // 2) as g:
                for par in range(2):
                    j = g * 2 + par
                    latents(j, par)
                    turn_h(j * TURNS + 4, par)
                    ups(j, par)
                    until(pe, t_copied, j * TURNS + 6, passed)
                    project(j * MMS + 10, (2 + 2 * par) % 4, 1 - par, False)
                    turn_heads(j, par)
            j = TILES - 1
            latents(j, 0)
            turn_h(j * TURNS + 4, 0)
            ups(j, 0)
            turn_heads(j, 0)

        @block.scalar
        def _(act):
            def copy(n, bank, dst, width, top, guard=None):
                until(act, turned, n + 1, passed)
                if guard is not None and not (isinstance(guard[1], int) and guard[1] <= 0):
                    until(act, guard[0], guard[1], passed)
                act.activation(dst, ps_t[bank][0:top, 0:width], ACT.Copy).then_inc(t_copied, 1)

            def take_root(n):
                until(act, squares, n, passed)
                act.activation(root[:, :], ms[:, :], ACT.Sqrt).then_inc(roots, 1)

            def flat(buf, lo, hi, top):
                return buf[0:top, lo:hi, :].rearrange("p c n -> p (c n)")

            def copy_h(n, bank, par, guard=None):
                copy(n, bank, flat(hT[par], 0, 4, P), 512, P, guard)
                copy(n + 1, 1 - bank, flat(hT[par], 4, 8, P), 512, P)

            def copy_heads(j, par):
                n, w = j * TURNS + 6, j * 16
                for i, (buf, h, name) in enumerate(((kT, 0, "kT"), (kT, 4, "kT"), (qT, 0, "qT"), (qT, 4, "qT"))):
                    copy(n + i, (par + i) % 2, flat(buf, h, h + 4, QK), 512, QK, (t_out[name], w))
                for i, (buf, name) in enumerate(((dkT, "dkT"), (dqT, "dqT"), (mqT, "mqT"))):
                    copy(n + 4 + i, (par + i) % 2, flat(buf, 0, 4, P), 512, P, (t_out[name], w))

            take_root(1)
            copy_h(0, 0, 0)
            take_root(2)

            def step(g, par, follow, guard=True):
                j = g * 2 + par
                copy(j * TURNS + 2, par, cqT[:, :], Q_LORA, P)
                copy(j * TURNS + 3, 1 - par, kvT[:, :], KV_LORA, P)
                copy_h(j * TURNS + 4, par, 1 - par, (h_out[1 - par], (g + par) * 16))
                if follow:
                    take_root(j + 3)
                copy_heads(j, par)

            for par in range(2):
                step(0, par, True)
            with act.Fori(0, TILES // 2 - 1) as g:
                for par in range(2):
                    step(g + 1, par, True)
            step(TILES // 2, 0, False)

        @block.vector
        def _(dve):
            def evacuate(n, bank, dst, width, scale=None):
                until(dve, mm_done, n + 1, passed)
                src = ps_m[bank][:, 0:width]
                if scale is None:
                    dve.tensor_copy(dst, src).then_inc(m_copied, 1)
                else:
                    dve.tensor_scalar(dst, src, scale, None, ALU.mult).then_inc(m_copied, 1)

            def square(col, src, width):
                dve.tensor_tensor_reduce(out=junk[:, 0:width], in0=src, in1=src, scale=1.0 / width, scalar=EPS,
                                         op0=ALU.mult, op1=ALU.add, accum_out=ms[:, col:col + 1])

            def rotate(x, x_out, table, heads):
                half = ROPE // 2
                x1, x2 = x[:, :, 0:half], x[:, :, half:ROPE]
                cos = table[:, 0:half].unsqueeze(1).to_broadcast([P, heads, half])
                sin = table[:, half:ROPE].unsqueeze(1).to_broadcast([P, heads, half])
                for i, (u, w) in enumerate(((x1, cos), (x2, sin), (x2, cos), (x1, sin))):
                    dve.tensor_tensor(rot[:, i, 0:heads, :], u, w, ALU.mult)
                dve.drain()
                dve.tensor_tensor(x_out[:, :, 0:half], rot[:, 0, 0:heads, :], rot[:, 1, 0:heads, :], ALU.subtract)
                dve.tensor_tensor(x_out[:, :, half:ROPE], rot[:, 2, 0:heads, :], rot[:, 3, 0:heads, :], ALU.add)
                dve.drain()

            def norm_x(src):
                dve.scalar_tensor_tensor(out=xn[:, :], in0=src[:, :], scalar=rs[:, 2:3], in1=g_mix[:, :],
                                         op0=ALU.mult, op1=ALU.mult).then_inc(normed, 1)

            def take_z(n, bank, t, par, cs_count, x_count, d_guard, kv_guard):
                evacuate(n, bank, cq[:, :], Q_LORA)
                evacuate(n + 1, (bank + 1) % 4, kv[:, :], KV_LORA + ROPE)
                until(dve, x_in[1 - par], x_count, passed)
                dve.drain()
                square(0, cq[:, :], Q_LORA)
                dve.drain()
                square(1, kv[:, 0:KV_LORA], KV_LORA)
                dve.drain()
                square(2, xt[1 - par][:, :], D)
                dve.drain().then_inc(squares, 1)
                until(dve, cs_in[par], cs_count, passed)
                if kv_guard is not None:
                    until(dve, kv_out, kv_guard, passed)
                rotate(kv[:, KV_LORA:].unsqueeze(1), krr[:, :].unsqueeze(1), cs[par], 1)
                until(dve, roots, t + 2, passed)
                dve.reciprocal(rs[:, :], root[:, :])
                dve.drain()
                dve.scalar_tensor_tensor(out=cqn[:, :], in0=cq[:, :], scalar=rs[:, 0:1], in1=g_q[:, :],
                                         op0=ALU.mult, op1=ALU.mult)
                dve.scalar_tensor_tensor(out=kvn[:, :], in0=kv[:, 0:KV_LORA], scalar=rs[:, 1:2], in1=g_kv[:, :],
                                         op0=ALU.mult, op1=ALU.mult).then_inc(latents_done, 1)
                norm_x(xt[1 - par])
                if d_guard is not None:
                    until(dve, d_out[par], d_guard, passed)
                evacuate(n + 2, (bank + 2) % 4, dq[par][:, :], BR, DIFF_SCALE)
                evacuate(n + 3, (bank + 3) % 4, dk[par][:, :], BR)
                evacuate(n + 4, bank, dv[par][:, :], BR)
                evacuate(n + 5, (bank + 1) % 4, mq[par][:, :], BR, MEM_SCALE)

            def take_heads(j, par, guard):
                n, bank = j * MMS + 6, (2 + 2 * par) % 4
                q_flat = q_sb[:, :, :].rearrange("p h d -> p (h d)")
                evacuate(n, bank, q_flat[:, 0:512], 512, MLA_SCALE)
                evacuate(n + 1, (bank + 1) % 4, q_flat[:, 512:], HEADS * QK - 512, MLA_SCALE)
                until(dve, mm_done, n + 3, passed)
                dve.tensor_copy(k_sb[:, :, 0:NOPE],
                                ps_m[(bank + 2) % 4][:, :].rearrange("p (h d) -> p h d", d=NOPE)).then_inc(m_copied, 1)
                if guard:
                    until(dve, v_out, j * 16, passed)
                evacuate(n + 3, (bank + 3) % 4, v_sb[:, :], BR)
                dve.tensor_copy(k_sb[:, :, NOPE:], krr[:, :].unsqueeze(1).to_broadcast([P, HEADS, ROPE]))
                dve.drain()
                rotate(q_sb[:, :, NOPE:], q_sb[:, :, NOPE:], cs[par], HEADS)
                dve.sem_inc(roped, 1)
                dve.sem_inc(heads_ready, 1)

            dve.memset(ms[:, :], 1.0)
            dve.memset(junk[:, :], 0.0)
            dve.drain()
            dve.wait_ge(gains, 48)
            dve.wait_ge(x_in[0], 16)
            square(2, xt[0][:, :], D)
            dve.drain().then_inc(squares, 1)
            dve.wait_ge(roots, 1)
            dve.reciprocal(rs[:, :], root[:, :])
            dve.drain()
            norm_x(xt[0])
            take_z(0, 0, 0, 0, 16, 16, None, None)

            def step(g, par, first):
                j = g * 2 + par
                take_heads(j, par, not (first and par == 0))
                take_z(j * MMS + 10, (2 + 2 * par) % 4, j + 1, 1 - par, (g + par) * 16 + 16, (g * 16) + 32,
                       None if first and par == 0 else (g + par) * 32, j * 32 + 32)

            for par in range(2):
                step(0, par, True)
            with dve.Fori(0, TILES // 2 - 1) as g:
                for par in range(2):
                    step(g + 1, par, False)
            take_heads(TILES - 1, 0, True)


def cached_and_memory_keys(nc, a, s):
    with ExitStack() as ctx:
        sb, psum, sem = tools(nc, ctx, "B")
        ident = sb("ident", [P, P])
        w_uk, w_uv = sb("w_uk", [P, KV_LORA // P, BR]), sb("w_uv", [P, KV_LORA // P, BR])
        w_kv = sb("w_kv", [P, DC, 2 * BR])
        g_mem = sb("g_mem", [P, D])
        cmk = sb("cmk", [P, 2, BR])
        cdk, ckv, ckr = sb("cdk", [P, BR]), sb("ckv", [P, KV_LORA]), sb("ckr", [P, ROPE])
        sub = sb("sub", [P, 2 * HEADS, P])
        mem, mn = sb("mem", [P, 2, D]), sb("mn", [P, 2, D])
        ms, root, rs = sb("ms", [P, 2]), sb("root", [P, 2]), sb("rs", [P, 2])
        memT = sb("memT", [P, 2, DC, P])
        ckvT = sb("ckvT", [P, KV_LORA])
        cmkT, mkT = sb("cmkT", [P, MEM_HEADS, MEM]), sb("mkT", [P, MEM_HEADS, MEM])
        cdkT, subT = sb("cdkT", [P, 4, P]), sb("subT", [P, 2 * HEADS, P])
        k_sb, v_sb, kT = sb("k_sb", [P, HEADS, QK]), sb("v_sb", [P, BR]), sb("kT", [P, HEADS, P])
        mk, mv = sb("mk", [P, 2, BR]), sb("mv", [P, 2, BR])
        ps_t = [psum(f"turn{i}", [P, 512]) for i in range(2)]
        ps_m = [psum(f"mm{i}", [P, 512]) for i in range(4)]
        made = sem("identity")
        small_in, mem_in, w_in_sem, sub_in = sem("small_in"), sem("mem_in"), sem("w_in"), sem("sub_in")
        squares, roots, normed = sem("squares"), sem("roots"), sem("normed")
        turned, t_copied, mm_done, m_copied = sem("turned"), sem("t_copied"), sem("mm_done"), sem("m_copied")
        keys_ready, stored = sem("keys_ready"), sem("stored")
        block = ctx.enter_context(nc.Block())

        @block.gpsimd
        def _(pool):
            make_identity(pool, ident, made)

        @block.sync
        def _(sp):
            two = "(m p) n -> p m n"
            sp.dma_start(cmk[:, :, :], a["cache_mem_k"].rearrange(two, p=P)).then_inc(small_in, 16)
            sp.dma_start(cdk[:, :], a["cache_diff_k"]).then_inc(small_in, 16)
            sp.dma_start(ckv[:, :], a["cache_mla_ckv"]).then_inc(small_in, 16)
            sp.dma_start(ckr[:, :], a["cache_mla_krope"]).then_inc(small_in, 16)
            sp.dma_start(w_uk[:, :, :], a["w_uk"].rearrange("(c p) n -> p c n", p=P)).then_inc(small_in, 16)
            sp.dma_start(w_uv[:, :, :], a["w_uv"].rearrange("(c p) n -> p c n", p=P)).then_inc(small_in, 16)
            sp.dma_start(mem[:, :, :], a["mem_prompt"].rearrange(two, p=P)).then_inc(mem_in, 16)
            sp.dma_start(g_mem[:, :], a["norm_mem"].to_broadcast([P, D])).then_inc(mem_in, 16)
            sp.dma_start(sub[:, :, :], a["peer_subkeys"].rearrange("(b n) d -> n b d", n=P)).then_inc(sub_in, 16)
            sp.dma_start(w_kv[:, :, :], a["w_mem_kv"].rearrange("(c p) n -> p c n", p=P)).then_inc(w_in_sem, 16)
            cache = slice(CACHE, CACHE + PAST)
            sp.wait_ge(t_copied, 3)
            sp.dma_start(s["mkT"][1].rearrange("h p n -> p h n"), cmkT[:, :, :]).then_inc(stored, 16)
            sp.dma_start(s["dkT"].rearrange("c p n -> p c n")[:, :, cache], cdkT[:, :, :]).then_inc(stored, 16)
            sp.wait_ge(m_copied, 2)
            sp.dma_start(s["vm"][cache, :], v_sb[:, :]).then_inc(stored, 16)
            sp.wait_ge(t_copied, 14)
            sp.dma_start(s["kT"].rearrange("c p n -> p c n")[:, :, cache], kT[0:QK, :, :]).then_inc(stored, 16)
            sp.wait_ge(m_copied, 6)
            sp.dma_start(s["mk"].rearrange(two, p=P), mk[:, :, :]).then_inc(stored, 16)
            sp.dma_start(s["mv"].rearrange(two, p=P), mv[:, :, :]).then_inc(stored, 16)
            sp.wait_ge(t_copied, 16)
            sp.dma_start(s["mkT"][0].rearrange("h p n -> p h n"), mkT[:, :, :]).then_inc(stored, 16)
            sp.dma_start(s["skT"].rearrange("b d n -> d b n"), subT[:, :, :]).then_inc(stored, 16)
            sp.wait_ge(stored, 16 * 8)

        @block.tensor
        def _(pe):
            count = {"turn": 0, "mm": 0}

            def turn(blocks, top=P):
                n = count["turn"]
                if n >= 2:
                    pe.wait_ge(t_copied, n - 1)
                for b, src in enumerate(blocks):
                    last = pe.transpose(ps_t[n % 2][0:top, b * P:(b + 1) * P], src, ident[:, :])
                last.then_inc(turned, 1)
                count["turn"] += 1

            def product(lhs, w, lo):
                n = count["mm"]
                if n >= 4:
                    pe.wait_ge(m_copied, n - 3)
                for c in range(len(lhs)):
                    last = pe.matmul(ps_m[n % 4][:, :], lhs[c], w[:, c, lo:lo + BR], start=(c == 0),
                                     stop=(c == len(lhs) - 1))
                last.then_inc(mm_done, 1)
                count["mm"] += 1

            pe.wait_ge(made, 2)
            pe.wait_ge(small_in, 96)
            for m in range(2):
                turn([cmk[:, m, h * P:(h + 1) * P] for h in range(4)])
            turn([cdk[:, h * P:(h + 1) * P] for h in range(4)])
            turn([ckv[:, c * P:(c + 1) * P] for c in range(2)])
            pe.wait_ge(sub_in, 16)
            for i in range(4):
                turn([sub[:, 4 * i + b, :] for b in range(4)])
            latent = [ckvT[:, c * P:(c + 1) * P] for c in range(2)]
            product(latent, w_uk, 0)
            product(latent, w_uv, 0)
            pe.wait_ge(normed, 2)
            for m in range(2):
                for i in range(2):
                    turn([mn[:, m, (4 * i + b) * P:(4 * i + b + 1) * P] for b in range(4)])
            pe.wait_ge(keys_ready, 1)
            for i in range(2):
                turn([k_sb[:, 4 * i + b, :] for b in range(4)], QK)
            pe.wait_ge(w_in_sem, 16)
            for m in range(2):
                pe.wait_ge(t_copied, 10 + 2 * m)
                for i in range(2):
                    product([memT[:, m, c, :] for c in range(DC)], w_kv, i * BR)
            for m in range(2):
                pe.wait_ge(m_copied, 3 + 2 * m)
                turn([mk[:, m, h * P:(h + 1) * P] for h in range(4)])

        @block.scalar
        def _(act):
            act.wait_ge(squares, 1)
            act.activation(root[:, :], ms[:, :], ACT.Sqrt).then_inc(roots, 1)
            count = [0]

            def copy(dst, width, top=P):
                n = count[0]
                act.wait_ge(turned, n + 1)
                src = ps_t[n % 2][0:top, 0:width]
                if len(dst.shape) == 3:
                    src = src.rearrange("p (c n) -> p c n", n=P)
                act.activation(dst, src, ACT.Copy).then_inc(t_copied, 1)
                count[0] += 1

            for m in range(2):
                copy(cmkT[:, :, m * P:(m + 1) * P], 512)
            copy(cdkT[:, :, :], 512)
            copy(ckvT[:, :], KV_LORA)
            for i in range(4):
                copy(subT[:, 4 * i:4 * i + 4, :], 512)
            for m in range(2):
                for i in range(2):
                    copy(memT[:, m, 4 * i:4 * i + 4, :], 512)
            for i in range(2):
                copy(kT[0:QK, 4 * i:4 * i + 4, :], 512, QK)
            for m in range(2):
                copy(mkT[:, :, m * P:(m + 1) * P], 512)

        @block.vector
        def _(dve):
            dve.wait_ge(mem_in, 32)
            for m in range(2):
                dve.tensor_tensor_reduce(out=mn[:, m, :], in0=mem[:, m, :], in1=mem[:, m, :], scale=1.0 / D, scalar=EPS,
                                         op0=ALU.mult, op1=ALU.add, accum_out=ms[:, m:m + 1])
            dve.drain().then_inc(squares, 1)
            dve.wait_ge(roots, 1)
            dve.reciprocal(rs[:, :], root[:, :])
            dve.drain()
            for m in range(2):
                dve.scalar_tensor_tensor(out=mn[:, m, :], in0=mem[:, m, :], scalar=rs[:, m:m + 1], in1=g_mem[:, :],
                                         op0=ALU.mult, op1=ALU.mult).then_inc(normed, 1)
            dve.wait_ge(mm_done, 1)
            dve.tensor_copy(k_sb[:, :, 0:NOPE], ps_m[0][:, :].rearrange("p (h d) -> p h d", d=NOPE)).then_inc(m_copied, 1)
            dve.wait_ge(small_in, 96)
            dve.tensor_copy(k_sb[:, :, NOPE:], ckr[:, :].unsqueeze(1).to_broadcast([P, HEADS, ROPE]))
            dve.drain().then_inc(keys_ready, 1)
            for n, dst in enumerate((v_sb[:, :], mk[:, 0, :], mv[:, 0, :], mk[:, 1, :], mv[:, 1, :])):
                dve.wait_ge(mm_done, n + 2)
                dve.tensor_copy(dst, ps_m[(n + 1) % 4][:, :]).then_inc(m_copied, 1)


KEY_TILES = SEQ // P
SAMPLE_KEYS = PAST + DEC
LAM_INIT = 0.8 - 0.6
PAIRS = HEADS // 2
ALIBI_STEP = 2.0 ** (-8.0 * 2 / HEADS)


class Span:

    def __init__(self, tiles, groups):
        self.tiles = tiles
        self.lo = tiles[0] * P
        self.hi = min(TOK, (tiles[-1] + 1) * P)
        self.n = self.hi - self.lo
        self.groups = groups
        self.width = self.n // groups
        self.sample = self.hi == TOK
        self.keys = SEQ if self.sample else self.hi
        self.rows = [min(P, TOK - t * P) for t in tiles]


FIRST = Span(list(range(KEY_TILES // 2)), 1)
SECOND = Span(list(range(KEY_TILES // 2, TILES)), 2)


def attention_jobs(span, blocks):
    jobs, slot, group = [], 0, 0
    for kind, heads in (("mla", 2), ("diff", 2), ("mem", 1)):
        for u in range(heads):
            for t in span.tiles:
                keys = MEM if kind == "mem" else (t + 1) * P if t < KEY_TILES else SAMPLE_KEYS
                jobs.append((kind, u, t, keys, slot, group))
                slot += 2 if kind == "diff" else 1
                group += -(-keys // (blocks * P))
    return jobs, slot, group


def attention(nc, a, s, span, tag, ex=None):
    BLOCKS = 4
    BANKS = 1 if ex else 2
    jobs, SLOTS, GROUPS = attention_jobs(span, BLOCKS)
    JOBS = len(jobs)
    NT = len(span.tiles)
    O_GROUPS = -(-NT // BLOCKS)
    TURNS = GROUPS + 3 * O_GROUPS
    MIXES = 2 * NT
    LAST = {k: max(i for i, j in enumerate(jobs) if j[0] == k) for k in ("mla", "diff", "mem")}
    WIDTH = {"mla": VD, "diff": VD, "mem": MDH}

    def done(g, per, n):
        return g * per + (per + n + 1)

    with ExitStack() as ctx:
        sb, psum, sem = tools(nc, ctx, tag)
        ident = sb("ident", [P, P])
        MEMS = 1 + span.sample
        KW = span.keys + (SAMPLE_KEYS if span.sample else 0)
        VT = span.keys // P + (2 if span.sample else 0)
        bias = [sb(f"bias{u}", [P, D]) for u in range(2)]
        q_mla = [sb(f"q_mla{u}", [P, NT * P]) for u in range(2)]
        k_mla = [sb(f"k_mla{u}", [P, KW]) for u in range(2)]
        v_mla = sb("v_mla", [P, VT, P])
        q_diff, k_diff = sb("q_diff", [P, NT * P]), sb("k_diff", [P, KW])
        v_diff = sb("v_diff", [P, VT, P])
        q_mem, k_mem, v_mem = sb("q_mem", [P, NT * P]), sb("k_mem", [P, 2, MEM]), sb("v_mem", [P, 2, 2, P])
        shifted_s = [sb(f"shifted{i}", [P, D]) for i in range(2)]
        probs = [sb(f"probs{i}", [P, D]) for i in range(2)]
        pT = [sb(f"pT{i}", [P, D]) for i in range(2)]
        o = {k: sb(f"o_{k}", [P, NT, P]) for k in ("mla", "diff", "mem")}
        o_sq = sb("o_sq", [P, NT * 2, VD])
        oT = {k: sb(f"oT_{k}", [P, NT, P]) for k in ("mla", "diff", "mem")}
        o_ms, o_root, o_rs = (sb(n, [P, 2 * NT]) for n in ("o_ms", "o_root", "o_rs"))
        top = sb("top", [P, 8])
        ntop = sb("ntop", [P, 8])
        sums = sb("sums", [P, 8])
        inv, coef = sb("inv", [P, 8]), sb("coef", [P, 8])
        lam_in = sb("lam_in", [P, 4, DDH])
        lam_junk, lam_sum, lam_exp = sb("lam_junk", [P, 2, DDH]), sb("lam_sum", [P, 2]), sb("lam_exp", [P, 2])
        neg_lam = sb("neg_lam", [P, 1])
        subln, g_o = sb("subln", [P, VD]), sb("g_o", [P, VD])
        ps_s = [psum(f"scores{i}", [P, D]) for i in range(2)]
        ps_t = [psum(f"turn{i}", [P, 512]) for i in range(BANKS)]
        ps_o = [psum(f"o{i}", [P, 512]) for i in range(BANKS)]
        steps, dist = shifted_s[0][:, :].bitcast(I32), probs[0]

        K_IN = 48 if span.sample else 16
        made, passed = sem("identity"), sem("loop_waits")
        iota_done, dist_done, small_in, lam_summed, lam_exped = (sem(n) for n in (
            "iota_done", "dist_done", "small_in", "lam_summed", "lam_exped"))
        in_mla = [sem(f"in_mla{u}") for u in range(2)]
        in_vmla, in_diff, in_mem = sem("in_vmla"), sem("in_diff"), sem("in_mem")
        scored, maxed, shifted, exped = sem("scored"), sem("maxed"), sem("shifted"), sem("exped")
        mixed, turned, t_copied = sem("mixed"), sem("turned"), sem("t_copied")
        pv_done, o_taken = sem("pv_done"), sem("o_taken")
        o_squares, o_roots, o_normed, oT_out = sem("o_squares"), sem("o_roots"), sem("o_normed"), sem("oT_out")
        def loop(eng, body):
            if ex:
                with eng.Fori(0, PAIRS // 2) as t:
                    for half in range(2):
                        body(t * 2 + half, t, half)
            else:
                with eng.Fori(0, PAIRS) as g:
                    body(g, None, None)

        def experts_beside(kind, eng, t, half, i, share=None):
            if ex:
                beside(ex, kind, eng, t, range(half * (ATOMS // 2), (half + 1) * (ATOMS // 2)), i, JOBS, share)

        block = ctx.enter_context(nc.Block())

        @block.sync
        def _(sp):
            for i, name in enumerate(("diff_lq1", "diff_lk1", "diff_lq2", "diff_lk2")):
                sp.dma_start(lam_in[:, i, :], a[name].to_broadcast([P, DDH])).then_inc(small_in, 16)
            sp.dma_start(subln[:, :], a["diff_subln"].to_broadcast([P, VD])).then_inc(small_in, 16)

            def tiles(src):
                return src.rearrange("(t p) n -> p t n", p=P)

            def load_keys(buf, top_row, src, c, signal):
                view = src.rearrange("c p n -> p c n")[:, bass.ds(c, 1), :]
                parts = [(0, 0, span.keys)] + [(SEQ, CACHE, PAST), (SEQ + PAST, SEQ, DEC)] * span.sample
                for lo, src_lo, n in parts:
                    sp.dma_start(buf[0:top_row, lo:lo + n].unsqueeze(1), view[:, :, src_lo:src_lo + n]).then_inc(signal, 16)

            def load_values(buf, rows, cache, g, signal):
                cols = bass.ds(g * P, P)
                sp.dma_start(buf[:, 0:span.keys // P, :], tiles(rows[0:span.keys, :])[:, :, cols]).then_inc(signal, 16)
                if span.sample:
                    sp.dma_start(buf[:, KEY_TILES, :], cache[:, cols]).then_inc(signal, 16)
                    sp.dma_start(buf[0:DEC, KEY_TILES + 1, :], rows[SEQ:TOK, cols]).then_inc(signal, 16)

            q_cols = slice(span.lo, span.lo + NT * P)

            def loads(g, t, half):
                for u in range(2):
                    last = max(j[4] for j in jobs if j[0] == "mla" and j[1] == u)
                    until(sp, scored, done(g, SLOTS, last - SLOTS), passed)
                    view = s["qT"].rearrange("c p n -> p c n")[:, bass.ds(g * 2 + u, 1), q_cols]
                    sp.dma_start(q_mla[u][0:QK, :].unsqueeze(1), view).then_inc(in_mla[u], 16)
                    load_keys(k_mla[u], QK, s["kT"], g * 2 + u, in_mla[u])
                until(sp, pv_done, done(g, JOBS, LAST["mla"] - JOBS), passed)
                load_values(v_mla, s["vm"], s["vm"][CACHE:CACHE + PAST, :], g, in_vmla)
                until(sp, pv_done, done(g, JOBS, LAST["diff"] - JOBS), passed)
                sp.dma_start(q_diff[:, :].unsqueeze(1), s["dqT"].rearrange("c p n -> p c n")[:, bass.ds(g, 1), q_cols]).then_inc(in_diff, 16)
                load_keys(k_diff, P, s["dkT"], g, in_diff)
                load_values(v_diff, s["dv"], a["cache_diff_v"], g, in_diff)
                until(sp, pv_done, done(g, JOBS, LAST["mem"] - JOBS), passed)
                sp.dma_start(q_mem[:, :].unsqueeze(1), s["mqT"].rearrange("c p n -> p c n")[:, bass.ds(g, 1), q_cols]).then_inc(in_mem, 16)
                for m, v in enumerate((s["mv"], a["cache_mem_v"])[0:MEMS]):
                    sp.dma_start(k_mem[:, m, :].unsqueeze(1), s["mkT"][m].rearrange("h p n -> p h n")[:, bass.ds(g, 1), :]).then_inc(in_mem, 16)
                    sp.dma_start(v_mem[:, m, :, :], tiles(v)[:, :, bass.ds(g * P, P)]).then_inc(in_mem, 16)

            loop(sp, loads)

        @block.gpsimd
        def _(pool):
            make_identity(pool, ident, made)
            pool.iota(steps, pattern=[[1, D]], base=P - D, channel_multiplier=-1).then_inc(iota_done, 1)
            if ex:
                ex.pool_start(pool)
                with pool.Fori(0, PAIRS // 2) as t:
                    ex.pool_tile(pool, t, range(HEADS))

        @block.tensor
        def _(pe):
            def free_slot(g, k):
                if k < 2:
                    until(pe, exped, done(g, SLOTS, -1), passed)
                elif 2 * NT <= k - 2 < 6 * NT:
                    until(pe, shifted, done(g, 2 * MIXES, k - 2 - 2 * NT), passed)
                else:
                    until(pe, exped, done(g, SLOTS, k - 2), passed)

            def scores(g, i):
                kind, u, t, keys, slot, _ = jobs[i]
                if t == span.tiles[0]:
                    per, signal = {"mla": (16 + K_IN, in_mla[u]), "diff": (16 + K_IN + K_IN, in_diff),
                                   "mem": (16 + 32 * MEMS, in_mem)}[kind]
                    until(pe, signal, g * per + per, passed)
                q = slice(t * P - span.lo, (t + 1) * P - span.lo)
                lo = 0 if t < KEY_TILES else SEQ
                for m in range(2 if kind == "diff" else 1):
                    free_slot(g, slot + m)
                    out = ps_s[(slot + m) % 2]
                    for c in range(0, keys, 512):
                        n = min(512, keys - c)
                        if kind == "mla":
                            lhs, rhs = q_mla[u][0:QK, q], k_mla[u][0:QK, lo + c:lo + c + n]
                        elif kind == "diff":
                            part = slice(DDH * (2 * u + m), DDH * (2 * u + m + 1))
                            lhs, rhs = q_diff[part, q], k_diff[part, lo + c:lo + c + n]
                        else:
                            lhs, rhs = q_mem[:, q], k_mem[:, int(t == TILES - 1), :]
                        last = pe.matmul(out[:, c:c + n], lhs, rhs, start=True, stop=True)
                    last.then_inc(scored, 1)

            def bank_free(g, n):
                until(pe, t_copied, done(g, TURNS, n - BANKS if n >= BANKS else -1), passed)

            def turn(g, i):
                kind, u, t, keys, slot, group = jobs[i]
                if kind == "diff":
                    until(pe, mixed, done(g, MIXES, i - 2 * NT), passed)
                else:
                    until(pe, exped, done(g, SLOTS, slot), passed)
                for n, c in enumerate(range(0, keys, BLOCKS * P)):
                    bank_free(g, group + n)
                    for b in range(c, min(keys, c + BLOCKS * P), P):
                        w = min(P, keys - b)
                        last = pe.transpose(ps_t[(group + n) % BANKS][0:w, b - c:b - c + P], probs[slot % 2][:, b:b + w], ident[:, :])
                    last.then_inc(turned, 1)

            def weigh(g, i):
                kind, u, t, keys, _, group = jobs[i]
                if kind == "mla" and i == 0:
                    until(pe, in_vmla, g * K_IN + K_IN, passed)
                until(pe, t_copied, done(g, TURNS, group + (keys - 1) // (BLOCKS * P)), passed)
                until(pe, o_taken, done(g, JOBS, i - BANKS if i >= BANKS else -1), passed)
                blocks = -(-keys // P)
                for b in range(blocks):
                    w = min(P, keys - b * P)
                    if kind == "mem":
                        v = v_mem[:, int(t == TILES - 1), b, :]
                    else:
                        tile = b if t < KEY_TILES else KEY_TILES + b
                        v = (v_mla if kind == "mla" else v_diff)[0:w, tile, VD * u:VD * (u + 1)]
                    last = pe.matmul(ps_o[i % BANKS][:, 0:WIDTH[kind]], pT[i % 2][0:w, b * P:(b + 1) * P], v,
                                     start=(b == 0), stop=(b == blocks - 1))
                last.then_inc(pv_done, 1)

            def turn_o(g):
                for n, kind in enumerate(("mla", "diff", "mem")):
                    if kind == "diff":
                        until(pe, o_normed, g + 2, passed)
                    else:
                        until(pe, o_taken, done(g, JOBS, LAST[kind]), passed)
                    for c in range(O_GROUPS):
                        group = GROUPS + O_GROUPS * n + c
                        bank_free(g, group)
                        for b in range(BLOCKS * c, min(BLOCKS * c + BLOCKS, NT)):
                            last = pe.transpose(ps_t[group % BANKS][:, (b - BLOCKS * c) * P:(b - BLOCKS * c + 1) * P], o[kind][:, b, :], ident[:, :])
                        last.then_inc(turned, 1)

            pe.wait_ge(made, 2)
            pe.sem_inc(scored, SLOTS)
            pe.sem_inc(turned, TURNS)
            pe.sem_inc(pv_done, JOBS)
            if ex:
                ex.pe_start(pe)

            def pair(g, tile, half):
                scores(g, 0)
                for i in range(JOBS):
                    if i + 1 < JOBS:
                        scores(g, i + 1)
                    experts_beside("pe", pe, tile, half, i, 0)
                    turn(g, i)
                    experts_beside("pe", pe, tile, half, i, 1)
                    if i >= 1:
                        weigh(g, i - 1)
                weigh(g, JOBS - 1)
                turn_o(g)

            loop(pe, pair)

        @block.scalar
        def _(act):
            def exp(g, i):
                kind, _, _, keys, slot, _ = jobs[i]
                until(act, maxed, done(g, JOBS, i), passed)
                for m in range(2 if kind == "diff" else 1):
                    col = 2 * (i % 4) + m
                    src = shifted_s[m] if kind == "diff" else ps_s[slot % 2]
                    act.activation(probs[(slot + m) % 2][:, 0:keys], src[:, 0:keys], ACT.Exp, bias=ntop[:, col:col + 1],
                                   accum_out=sums[:, col:col + 1]).then_inc(exped, 1)

            def copy(g, i):
                _, _, _, keys, _, group = jobs[i]
                until(act, pv_done, done(g, JOBS, i - 2 if i >= 2 else -1), passed)
                for n, c in enumerate(range(0, keys, BLOCKS * P)):
                    until(act, turned, done(g, TURNS, group + n), passed)
                    full = min(keys, c + BLOCKS * P) // P * P - c
                    bank = ps_t[(group + n) % BANKS]
                    if full:
                        last = act.activation(pT[i % 2][:, c:c + full], bank[:, 0:full], ACT.Copy)
                    if (keys - c) % P and keys - c < BLOCKS * P:
                        w = (keys - c) % P
                        last = act.activation(pT[i % 2][0:w, c + full:c + full + P], bank[0:w, full:full + P], ACT.Copy)
                    last.then_inc(t_copied, 1)

            act.wait_ge(iota_done, 1)
            act.activation(dist[:, :], steps, ACT.Abs).then_inc(dist_done, 1)
            act.wait_ge(lam_summed, 1)
            act.activation(lam_exp[:, :], lam_sum[:, :], ACT.Exp).then_inc(lam_exped, 1)
            act.sem_inc(exped, SLOTS)
            act.sem_inc(t_copied, TURNS)
            act.sem_inc(o_roots, 1)
            act.sem_inc(oT_out, 48)
            if ex:
                ex.act_start(act)

            def pair(g, tile, half):
                exp(g, 0)
                for i in range(JOBS):
                    experts_beside("act_diag", act, tile, half, i)
                    copy(g, i)
                    if i + 1 < JOBS:
                        exp(g, i + 1)
                    if i == LAST["diff"] + 2:
                        until(act, o_squares, g + 2, passed)
                        act.activation(o_root[:, :], o_ms[:, :], ACT.Sqrt).then_inc(o_roots, 1)
                    experts_beside("act_rest", act, tile, half, i)
                until(act, oT_out, g * 48 + 48, passed)
                for n, kind in enumerate(("mla", "diff", "mem")):
                    for c in range(O_GROUPS):
                        group = GROUPS + O_GROUPS * n + c
                        until(act, turned, done(g, TURNS, group), passed)
                        k = min(BLOCKS, NT - BLOCKS * c)
                        act.activation(oT[kind][:, BLOCKS * c:BLOCKS * c + k, :].rearrange("p t n -> p (t n)"),
                                       ps_t[group % BANKS][:, 0:k * P], ACT.Copy).then_inc(t_copied, 1)
                    until(act, t_copied, done(g, TURNS, group), passed)
                    view = s["oT"].rearrange("c p n -> p c n")[:, bass.ds(g + PAIRS * n, 1), span.lo:span.lo + NT * P]
                    act.dma_start(view, oT[kind][:, :, :].rearrange("p t n -> p (t n)").unsqueeze(1)).then_inc(oT_out, 16)

            loop(act, pair)
            act.wait_ge(oT_out, 48 * (PAIRS + 1))

        @block.vector
        def _(dve):
            def maximum(g, i):
                kind, u, t, keys, slot, _ = jobs[i]
                col = 2 * (i % 4)
                until(dve, scored, done(g, SLOTS, slot), passed)
                if kind == "diff":
                    for m in range(2):
                        if m:
                            until(dve, scored, done(g, SLOTS, slot + 1), passed)
                        lo = D - P - t * P if t < KEY_TILES else D - P - PAST
                        dve.tensor_tensor_reduce(out=shifted_s[m][:, 0:keys], in0=ps_s[m][:, 0:keys],
                                                 in1=bias[u][:, lo:lo + keys], scale=1.0, scalar=-3.0e38,
                                                 op0=ALU.add, op1=ALU.max, accum_out=top[:, col + m:col + m + 1]).then_inc(shifted, 1)
                    dve.drain()
                    dve.tensor_scalar(ntop[:, col:col + 2], top[:, col:col + 2], -1.0, None, ALU.mult).then_inc(maxed, 1)
                    return
                if kind == "mla" and t < KEY_TILES:
                    dve.memset(ps_s[slot % 2][0:CHUNK, keys - CHUNK:keys], -1e30)
                    dve.drain()
                dve.tensor_reduce(ntop[:, col:col + 1], ps_s[slot % 2][:, 0:keys], AX, ALU.max, negate=True).then_inc(maxed, 1)

            def mix(g, i):
                col, slot = 2 * (i % 4), jobs[i][4]
                until(dve, exped, done(g, SLOTS, slot + 1), passed)
                dve.reciprocal(inv[:, col:col + 2], sums[:, col:col + 2])
                dve.drain()
                dve.tensor_scalar(coef[:, col:col + 1], inv[:, col + 1:col + 2], sums[:, col:col + 1], neg_lam[:, 0:1], ALU.mult, ALU.mult)
                dve.drain()
                keys = jobs[i][3]
                dve.scalar_tensor_tensor(out=probs[0][:, 0:keys], in0=probs[1][:, 0:keys], scalar=coef[:, col:col + 1],
                                         in1=probs[0][:, 0:keys], op0=ALU.mult, op1=ALU.add).then_inc(mixed, 1)

            def take_o(g, i):
                kind, u, t, _, _, _ = jobs[i]
                col = 2 * (i % 4)
                until(dve, pv_done, done(g, JOBS, i), passed)
                if kind != "diff":
                    dve.reciprocal(inv[:, col:col + 1], sums[:, col:col + 1])
                    dve.drain()
                lo = 0 if kind == "mem" else VD * u
                dve.tensor_scalar(o[kind][:, t - span.tiles[0], lo:lo + WIDTH[kind]], ps_o[i % BANKS][:, 0:WIDTH[kind]],
                                  inv[:, col:col + 1], None, ALU.mult).then_inc(o_taken, 1)

            heads_view = o["diff"][:, :, :].rearrange("p t (u v) -> p (t u) v", v=VD)

            def square_o():
                dve.drain()
                dve.tensor_tensor(o_sq[:, :, :], heads_view, heads_view, ALU.mult)
                dve.drain()
                dve.tensor_reduce(o_rs[:, :], o_sq[:, :, :], AX, ALU.add)
                dve.drain()
                dve.tensor_scalar(o_ms[:, :], o_rs[:, :], 1.0 / VD, EPS, ALU.mult, ALU.add).then_inc(o_squares, 1)

            def norm_o(g):
                until(dve, o_roots, g + 2, passed)
                dve.reciprocal(o_rs[:, :], o_root[:, :])
                dve.drain()
                n = 2 * NT
                dve.tensor_tensor(o_sq[:, :, :], heads_view, o_rs[:, :].unsqueeze(2).to_broadcast([P, n, VD]), ALU.mult)
                dve.drain()
                dve.tensor_tensor(heads_view, o_sq[:, :, :], g_o[:, :].unsqueeze(1).to_broadcast([P, n, VD]), ALU.mult).then_inc(o_normed, 1)

            dve.wait_ge(small_in, 80)
            for i in range(2):
                dve.tensor_tensor_reduce(out=lam_junk[:, i, :], in0=lam_in[:, 2 * i, :], in1=lam_in[:, 2 * i + 1, :], scale=1.0,
                                         scalar=0.0, op0=ALU.mult, op1=ALU.add, accum_out=lam_sum[:, i:i + 1])
            dve.drain().then_inc(lam_summed, 1)
            dve.tensor_scalar(g_o[:, :], subln[:, :], 1.0 - LAM_INIT, None, ALU.mult)
            dve.wait_ge(lam_exped, 1)
            dve.tensor_scalar(neg_lam[:, :], lam_exp[:, 1:2], lam_exp[:, 0:1], -LAM_INIT, ALU.subtract, ALU.add)
            dve.wait_ge(dist_done, 1)
            dve.memset(dist[0:CHUNK, D - CHUNK:D], 1e36)
            dve.drain()
            for u in range(2):
                dve.tensor_scalar(bias[u][:, :], dist[:, :], -(2.0 ** (-8.0 * (u + 1) / HEADS)), None, ALU.mult)
            dve.drain()
            dve.sem_inc(shifted, 2 * MIXES)
            dve.sem_inc(maxed, JOBS)
            dve.sem_inc(mixed, MIXES)
            dve.sem_inc(o_taken, JOBS)
            dve.sem_inc(o_squares, 1)
            dve.sem_inc(o_normed, 1)
            if ex:
                ex.dve_start(dve)

            def pair(g, tile, half):
                maximum(g, 0)
                for i in range(JOBS):
                    if jobs[i][0] == "diff":
                        mix(g, i)
                    if i >= 2:
                        take_o(g, i - 2)
                    experts_beside("dve", dve, tile, half, i, 0)
                    if i + 1 < JOBS:
                        maximum(g, i + 1)
                    if i == LAST["diff"] + 2:
                        square_o()
                        for u in range(2):
                            dve.tensor_scalar(bias[u][:, :], bias[u][:, :], ALIBI_STEP, None, ALU.mult)
                    if i == LAST["diff"] + 3:
                        norm_o(g)
                    experts_beside("dve", dve, tile, half, i, 1)
                take_o(g, JOBS - 2)
                take_o(g, JOBS - 1)

            loop(dve, pair)


BRANCHES = 3
QUERY = 2 * P


def merge_branches(nc, a, s, mergedT, span, tag, ex=None, tile=None):
    GROUP = span.width
    HALF = BRANCHES * span.groups
    UNITS = 2 * HALF
    n_iter = DC // 2

    def done(g, n):
        return g * UNITS + (UNITS + n + 1)

    with ExitStack() as ctx:
        sb, psum, sem = tools(nc, ctx, tag)
        hT, oT = sb("hT", [P, DC, span.n]), sb("oT", [P, BRANCHES * 4, span.n])
        w_gate = [sb(f"w_gate{i}", [P, BRANCHES, DC, P]) for i in range(2)]
        w_br = [sb(f"w_br{i}", [P, BRANCHES, 4, P]) for i in range(2)]
        b_gate = sb("b_gate", [P, BRANCHES, DC])
        gate = [sb(f"gate{i}", [P, GROUP]) for i in range(2)]
        part, acc = sb("part", [P, GROUP]), sb("acc", [P, GROUP])
        ps_g = [psum(f"gates{i}", [P, 512]) for i in range(2)]
        ps_b = [psum(f"branch{i}", [P, 512]) for i in range(2)]
        passed = sem("loop_waits")
        h_in, o_in, b_in = sem("h_in"), sem("o_in"), sem("b_in")
        w_ready = [sem(f"w_ready{i}") for i in range(2)]
        projected, opened, gated = sem("projected"), sem("opened"), sem("gated")
        block = ctx.enter_context(nc.Block())

        def loop(eng, body):
            if ex:
                for g in range(n_iter):
                    body(g)
            else:
                with eng.Fori(0, n_iter) as g:
                    body(g)

        def experts_beside(kind, eng, g, n):
            if ex:
                beside(ex, kind, eng, tile, range(ATOMS), g * UNITS + n, n_iter * UNITS)

        @block.sync
        def _(sp):
            def load_weights(g, par):
                e = bass.ds(g * (2 * P) + par * P, P)
                for b in range(BRANCHES):
                    w = a["w_gate"][:, b * D:(b + 1) * D].rearrange("(c p) n -> p c n", p=P)
                    sp.dma_start(w_gate[par][:, b, :, :], w[:, :, e]).then_inc(w_ready[par], 16)
                for b, name in enumerate(("w_br_a", "w_br_b", "w_br_m")):
                    w = a[name].rearrange("(c p) n -> p c n", p=P)
                    sp.dma_start(w_br[par][:, b, :, :], w[:, :, e]).then_inc(w_ready[par], 16)

            def loads(g):
                for par in range(2):
                    until(sp, projected, done(g, (par + 1) * HALF - 1 - UNITS), passed)
                    load_weights(g, par)

            loop(sp, loads)

        @block.gpsimd
        def _(pool):
            pool.dma_start(b_gate[:, :, :], a["b_gate"].rearrange("p (b e) -> p b e", e=DC)).then_inc(b_in, 16)
            if ex:
                ex.pool_tile(pool, tile, range(HEADS))

        @block.tensor
        def _(pe):
            pe.sem_inc(projected, UNITS)
            pe.wait_ge(h_in, 16)
            pe.wait_ge(o_in, 16)

            def blocks(g):
                for n in range(UNITS):
                    par, t, b = n // HALF, n % HALF // BRANCHES, n % BRANCHES
                    if n % HALF == 0:
                        until(pe, w_ready[par], g * 96 + 96, passed)
                    tok = slice(t * GROUP, (t + 1) * GROUP)
                    until(pe, opened, done(g, n - 2), passed)
                    until(pe, gated, done(g, n - 2), passed)
                    for c in range(DC):
                        pe.matmul(ps_g[n % 2][:, 0:GROUP], w_gate[par][:, b, c, :], hT[:, c, tok], start=(c == 0), stop=(c == DC - 1))
                    for c in range(4):
                        last = pe.matmul(ps_b[n % 2][:, 0:GROUP], w_br[par][:, b, c, :], oT[:, 4 * b + c, tok], start=(c == 0), stop=(c == 3))
                    last.then_inc(projected, 1)
                    experts_beside("pe", pe, g, n)

            loop(pe, blocks)

        @block.scalar
        def _(act):
            act.dma_start(hT[:, :, :], s["hT"].rearrange("c p n -> p c n")[:, :, span.lo:span.hi]).then_inc(h_in, 16)
            act.dma_start(oT[:, :, :], s["oT"].rearrange("c p n -> p c n")[:, :, span.lo:span.hi]).then_inc(o_in, 16)
            act.wait_ge(b_in, 16)
            act.sem_inc(opened, UNITS)

            def blocks(g):
                for n in range(UNITS):
                    par, b = n // HALF, n % BRANCHES
                    experts_beside("act_diag", act, g, n)
                    until(act, gated, done(g, n - 2), passed)
                    until(act, projected, done(g, n), passed)
                    act.activation(gate[n % 2][:, :], ps_g[n % 2][:, 0:GROUP], ACT.Sigmoid,
                                   bias=b_gate[:, b, bass.ds(g * 2 + par, 1)]).then_inc(opened, 1)
                    experts_beside("act_rest", act, g, n)

            loop(act, blocks)

        @block.vector
        def _(dve):
            dve.sem_inc(gated, UNITS)

            def blocks(g):
                for n in range(UNITS):
                    par, t, b = n // HALF, n % HALF // BRANCHES, n % BRANCHES
                    until(dve, opened, done(g, n), passed)
                    dve.drain()
                    dst = acc if b == 0 else part
                    dve.tensor_tensor(dst[:, :], gate[n % 2][:, :], ps_b[n % 2][:, 0:GROUP], ALU.mult).then_inc(gated, 1)
                    if b:
                        dve.drain()
                        out = acc[:, :] if b == 1 else mergedT[:, bass.ds(g * 2 + par, 1), t * GROUP:(t + 1) * GROUP].rearrange("p c n -> p (c n)")
                        dve.tensor_tensor(out, acc[:, :], part[:, :], ALU.add)
                    experts_beside("dve", dve, g, n)

            loop(dve, blocks)


def project_out(nc, a, s, mergedT, h2T, span, tag, ex=None, tile=None, heads=None):
    rows, NT = span.rows, len(span.tiles)
    with ExitStack() as ctx:
        sb, psum, sem = tools(nc, ctx, tag)
        ident = sb("ident", [P, P])
        w_o = sb("w_o", [P, DC, D])
        g_ffn = sb("g_ffn", [P, D])
        xt = [sb(f"xt{i}", [P, D]) for i in range(2)]
        x1 = [sb(f"x1{i}", [P, D]) for i in range(2)]
        h2 = [sb(f"h2{i}", [P, D]) for i in range(2)]
        ms, root, rs = sb("ms", [P, 2]), sb("root", [P, 2]), sb("rs", [P, 2])
        ps_o = [psum(f"out{i}", [P, D]) for i in range(2)]
        ps_t = [psum(f"turn{i}", [P, 512]) for i in range(2)]
        made, w_in, g_in = sem("identity"), sem("w_in"), sem("g_in")
        x_in = [sem(f"x_in{i}") for i in range(2)]
        projected, added, squares, roots, normed = (sem(n) for n in ("projected", "added", "squares", "roots", "normed"))
        turned, t_copied = sem("turned"), sem("t_copied")
        rows_out = [sem(f"rows_out{i}") for i in range(2)]
        steps = range(heads.start * TOPK, heads.stop * TOPK) if ex else None
        block = ctx.enter_context(nc.Block())

        @block.gpsimd
        def _(pool):
            make_identity(pool, ident, made)
            if ex:
                ex.pool_tile(pool, tile, heads)

        @block.sync
        def _(sp):
            w = a["w_o"].rearrange("(c p) n -> p c n", p=P)
            for i in range(2):
                sp.dma_start(w_o[:, :, 512 * i:512 * i + 512], w[:, :, 512 * i:512 * i + 512]).then_inc(w_in, 16)
            sp.dma_start(g_ffn[:, :], a["norm_ffn"].to_broadcast([P, D])).then_inc(g_in, 16)

            def store(t):
                sp.wait_ge(normed, t + 1)
                own = slice(span.lo + t * P, span.lo + t * P + rows[t])
                sp.dma_start(s["x1"][own, :], x1[t % 2][0:rows[t], :]).then_inc(rows_out[t % 2], 16)
                sp.dma_start(s["h2"][own, :], h2[t % 2][0:rows[t], :]).then_inc(rows_out[t % 2], 16)

            for t in range(NT):
                if t >= 2:
                    sp.wait_ge(added, t - 1)
                sp.dma_start(xt[t % 2][0:rows[t], :], a["x_all"][span.lo + t * P:span.lo + t * P + rows[t], :]).then_inc(x_in[t % 2], 16)
                if t:
                    store(t - 1)
            store(NT - 1)
            for i in range(2):
                sp.wait_ge(rows_out[i], 32 * ((NT + 1 - i) // 2))

        @block.tensor
        def _(pe):
            def project(t):
                if t >= 2:
                    pe.wait_ge(added, t - 1)
                r = rows[t]
                for i in range(2):
                    for c in range(DC):
                        last = pe.matmul(ps_o[t % 2][0:r, 512 * i:512 * i + 512], mergedT[:, c, t * P:t * P + r],
                                         w_o[:, c, 512 * i:512 * i + 512], start=(c == 0), stop=(c == DC - 1))
                last.then_inc(projected, 1)

            pe.wait_ge(made, 2)
            pe.wait_ge(w_in, 32)
            project(0)
            for t in range(NT):
                if t + 1 < NT:
                    project(t + 1)
                pe.wait_ge(normed, t + 1)
                r = rows[t]
                for i in range(2):
                    if t or i >= 2:
                        pe.wait_ge(t_copied, 2 * t + i - 1)
                    for b in range(4):
                        c = 4 * i + b
                        last = pe.transpose(ps_t[i][:, b * P:b * P + r], h2[t % 2][0:r, c * P:(c + 1) * P], ident[0:r, 0:r])
                    last.then_inc(turned, 1)
                beside(ex, "pe", pe, tile, steps, t, NT)

        @block.scalar
        def _(act):
            def take_root(t):
                act.wait_ge(squares, t + 1)
                act.activation(root[0:rows[t], t % 2:t % 2 + 1], ms[0:rows[t], t % 2:t % 2 + 1], ACT.Sqrt).then_inc(roots, 1)

            for t in range(NT):
                take_root(t)
                r = rows[t]
                for i in range(2):
                    act.wait_ge(turned, 2 * t + i + 1)
                    act.activation(h2T[:, 4 * i:4 * i + 4, t * P:t * P + r],
                                   ps_t[i][:, :].rearrange("p (c n) -> p c n", n=P)[:, :, 0:r], ACT.Copy).then_inc(t_copied, 1)
                beside(ex, "act", act, tile, steps, t, NT)

        @block.vector
        def _(dve):
            dve.wait_ge(g_in, 16)
            for t in range(NT):
                r, p = rows[t], t % 2
                dve.wait_ge(x_in[p], 16 * (t // 2 + 1))
                if t >= 2:
                    dve.wait_ge(rows_out[p], 32 * (t // 2))
                    dve.wait_ge(turned, 2 * (t - 1))
                dve.wait_ge(projected, t + 1)
                dve.tensor_tensor(x1[p][0:r, :], ps_o[p][0:r, :], xt[p][0:r, :], ALU.add).then_inc(added, 1)
                dve.drain()
                dve.tensor_tensor_reduce(out=h2[p][0:r, :], in0=x1[p][0:r, :], in1=x1[p][0:r, :], scale=1.0 / D, scalar=EPS,
                                         op0=ALU.mult, op1=ALU.add, accum_out=ms[0:r, p:p + 1]).then_inc(squares, 1)
                dve.drain()
                dve.wait_ge(roots, t + 1)
                dve.reciprocal(rs[0:r, p:p + 1], root[0:r, p:p + 1])
                dve.drain()
                dve.scalar_tensor_tensor(out=h2[p][0:r, :], in0=x1[p][0:r, :], scalar=rs[0:r, p:p + 1], in1=g_ffn[0:r, :],
                                         op0=ALU.mult, op1=ALU.mult).then_inc(normed, 1)
                beside(ex, "dve", dve, tile, steps, t, NT)


def score_experts(nc, a, s, h2T, span, tag, ex=None, tile=None, heads=None):
    rows, NT, GROUP = span.rows, len(span.tiles), span.width
    HALF = 2 * span.groups
    SETS = 2 * HALF
    SCORES = 2 * NT
    n_iter = HEADS // 2

    def done(g, per, n):
        return g * per + (per + n + 1)

    with ExitStack() as ctx:
        sb, psum, sem = tools(nc, ctx, tag)
        w_q = [sb(f"w_q{i}", [P, DC, QUERY]) for i in range(2)]
        skT = [sb(f"skT{i}", [P, 2, P]) for i in range(2)]
        qT = [sb(f"qT{i}", [P, 2, span.n]) for i in range(2)]
        sc = [sb(f"sc{i}", [P, NT, QUERY]) for i in range(2)]
        ps_q = [psum(f"q{i}", [P, 512]) for i in range(2)]
        ps_s = [psum(f"s{i}", [P, 512]) for i in range(2)]
        passed = sem("loop_waits")
        w_ready = [sem(f"w_ready{i}") for i in range(2)]
        queried, q_copied, scored, s_copied = (sem(n) for n in ("queried", "q_copied", "scored", "s_copied"))
        sc_out = [sem(f"sc_out{i}") for i in range(2)]
        prompt_tiles = NT - span.sample
        first_tile = span.tiles[0]
        prompt_groups = s["sc"][0:KEY_TILES * HEADS, :, :].rearrange("(t h) p n -> p h t n", h=HEADS)
        sample_rows = s["sc"].rearrange("g p n -> (g p) n")
        block = ctx.enter_context(nc.Block())

        def loop(eng, body):
            if ex:
                for g in range(n_iter):
                    body(g)
            else:
                with eng.Fori(0, n_iter) as g:
                    body(g)

        def experts_beside(kind, eng, g, n):
            if ex:
                beside(ex, kind, eng, tile, range(heads.start * TOPK, heads.stop * TOPK), g * SETS + n, n_iter * SETS)

        @block.sync
        def _(sp):
            def load_weights(g, par):
                w = a["peer_wq"].rearrange("(c p) n -> p c n", p=P)
                sp.dma_start(w_q[par][:, :, :], w[:, :, bass.ds(g * (2 * QUERY) + par * QUERY, QUERY)]).then_inc(w_ready[par], 16)
                sp.dma_start(skT[par][:, :, :], s["skT"].rearrange("b d n -> d b n")[:, bass.ds(g * 4 + 2 * par, 2), :]).then_inc(w_ready[par], 16)

            def head_pair(g):
                for par in range(2):
                    until(sp, scored, done(g, SCORES, (par + 1) * NT - 1 - SCORES), passed)
                    load_weights(g, par)

            loop(sp, head_pair)

        @block.gpsimd
        def _(pool):
            if ex:
                ex.pool_tile(pool, tile, heads)

        @block.tensor
        def _(pe):
            pe.sem_inc(scored, SCORES)

            def head_pair(g):
                for par in range(2):
                    until(pe, w_ready[par], g * 32 + 32, passed)
                    for i in range(HALF):
                        n, j, t = par * HALF + i, i // span.groups, i % span.groups
                        until(pe, q_copied, done(g, SETS, n - 2), passed)
                        for c in range(DC):
                            last = pe.matmul(ps_q[n % 2][:, 0:GROUP], w_q[par][:, c, j * P:(j + 1) * P],
                                             h2T[:, c, t * GROUP:(t + 1) * GROUP], start=(c == 0), stop=(c == DC - 1))
                        last.then_inc(queried, 1)
                        experts_beside("pe", pe, g, n)
                    until(pe, q_copied, done(g, SETS, par * HALF + HALF - 1), passed)
                    for t in range(NT):
                        n = par * NT + t
                        until(pe, s_copied, done(g, SCORES, n - 2), passed)
                        for j in range(2):
                            last = pe.matmul(ps_s[n % 2][0:rows[t], j * P:(j + 1) * P], qT[par][:, j, t * P:t * P + rows[t]],
                                             skT[par][:, j, :], start=True, stop=True)
                        last.then_inc(scored, 1)

            loop(pe, head_pair)

        @block.scalar
        def _(act):
            act.sem_inc(q_copied, SETS)
            for i in range(2):
                act.sem_inc(sc_out[i], 16 * (1 + span.sample))

            def head_pair(g):
                for par in range(2):
                    until(act, scored, done(g, SCORES, (par + 1) * NT - 1 - SCORES), passed)
                    for i in range(HALF):
                        n, j, t = par * HALF + i, i // span.groups, i % span.groups
                        experts_beside("act_diag", act, g, n)
                        until(act, queried, g * SETS + (n + 1), passed)
                        act.activation(qT[par][:, j, t * GROUP:(t + 1) * GROUP], ps_q[n % 2][:, 0:GROUP], ACT.Copy).then_inc(q_copied, 1)
                        experts_beside("act_rest", act, g, n)
                    until(act, s_copied, done(g, SCORES, (par + 1) * NT - 1), passed)
                    dst = prompt_groups[:, bass.ds(g * 2 + par, 1), first_tile:first_tile + prompt_tiles, :].rearrange("p h t n -> p (h t) n")
                    act.dma_start(dst, sc[par][:, 0:prompt_tiles, :]).then_inc(sc_out[par], 16)
                    if span.sample:
                        row = (g * 2 + par) * DEC + KEY_TILES * HEADS * P
                        act.dma_start(sample_rows[bass.ds(row, DEC), :], sc[par][0:DEC, NT - 1, :]).then_inc(sc_out[par], 16)

            loop(act, head_pair)
            for i in range(2):
                act.wait_ge(sc_out[i], 16 * (1 + span.sample) * (n_iter + 1))

        @block.vector
        def _(dve):
            dve.sem_inc(s_copied, SCORES)

            def head_pair(g):
                for par in range(2):
                    for i in range(HALF):
                        experts_beside("dve", dve, g, par * HALF + i)
                    per = 16 * (1 + span.sample)
                    until(dve, sc_out[par], g * per + per, passed)
                    for t in range(NT):
                        n = par * NT + t
                        until(dve, scored, done(g, SCORES, n), passed)
                        dve.tensor_copy(sc[par][0:rows[t], t, :], ps_s[n % 2][0:rows[t], 0:QUERY]).then_inc(s_copied, 1)

            loop(dve, head_pair)


SLOTS_G = 8
PACK = P // DEC
PROMPT_GROUPS = KEY_TILES * HEADS
GROUPS_ALL = PROMPT_GROUPS + HEADS // PACK
RANK_AHEAD = 3
SAMPLE = KEY_TILES
RUNS = {0: len(FIRST.tiles), len(FIRST.tiles): TILES}
LOWEST = -3.0e38
DVE_SLOTS = (3, 7)
ON_DVE = [c for c in range(TOPK) if c % SLOTS_G in DVE_SLOTS]
ON_PE = [c for c in range(TOPK) if c % SLOTS_G not in DVE_SLOTS]


class Experts:

    def __init__(self, nc, ctx, a, s):
        self.nc, self.a, self.s = nc, a, s
        sb, psum, sem = tools(nc, ctx, "G")
        self.ident, self.fold = sb("ident", [P, P]), sb("fold", [P, DEC])
        self.h2, self.h2_next = sb("h2", [P, D]), sb("h2_next", [P, D])
        self.x1, self.y, self.acc, self.g_fin = sb("x1", [P, D]), sb("y", [P, D]), sb("acc", [P, D]), sb("g_fin", [P, D])
        self.u_rows = [sb(f"u_rows{i}", [P, D]) for i in range(SLOTS_G)]
        self.v_rows = [sb(f"v_rows{i}", [P, D]) for i in range(SLOTS_G)]
        self.sc = [sb(f"sc{i}", [P, 2, P]) for i in range(2)]
        self.rest = sb("rest", [P, 2, P])
        self.best1, self.pos1 = sb("best1", [P, 2, TOPK]), sb("pos1", [P, 2, TOPK], U32)
        self.pos1f = sb("pos1f", [P, 2, TOPK])
        self.cand = sb("cand", [P, TOPK, TOPK])
        self.cand_rest = sb("cand_rest", [P, TOPK, TOPK])
        self.best, self.sel = sb("best", [P, TOPK]), sb("sel", [P, TOPK], U32)
        self.part, self.partf = sb("part", [P, 2, TOPK], U32), sb("partf", [P, 2, TOPK])
        self.ranks = sb("ranks", [P, TOPK])
        self.hot = sb("hot", [P, 2 * TOPK, TOPK])
        self.key = sb("key", [P, 2, TOPK])
        self.nbest, self.esum, self.einv = sb("nbest", [P, 1]), sb("esum", [P, 1]), sb("einv", [P, 1])
        self.egate = sb("egate", [P, TOPK])
        self.idx = [sb(f"idx{h}", [P, TOPK], I32) for h in range(HEADS)]
        self.gates = [sb(f"gates{h}", [P, TOPK]) for h in range(HEADS)]
        self.dots = [sb(f"dots{i}", [P, TOPK]) for i in range(2)]
        self.gelus = [sb(f"gelus{i}", [P, TOPK]) for i in range(2)]
        self.weights = [sb(f"weights{i}", [P, TOPK]) for i in range(2)]
        self.diag = [sb(f"diag{i}", [P, P]) for i in range(4)]
        self.ms, self.root, self.rs = sb("ms", [P, 1]), sb("root", [P, 1]), sb("rs", [P, 1])
        self.ps_y = psum("y_sum", [P, D])

        self.passed = sem("loop_waits")
        self.made, self.ranks_made, self.fold_made = sem("identity"), sem("ranks_made"), sem("fold_made")
        self.g_in, self.h2_in, self.h2_copied, self.x1_in = sem("g_in"), sem("h2_in"), sem("h2_copied"), sem("x1_in")
        self.sc_in = [sem(f"sc_in{i}") for i in range(2)]
        self.u_in = [sem(f"u_in{i}") for i in range(SLOTS_G)]
        self.v_in = [sem(f"v_in{i}") for i in range(SLOTS_G)]
        self.scores_read, self.ranked = sem("scores_read"), sem("ranked")
        self.gate_max, self.gate_exped = sem("gate_max"), sem("gate_exped")
        self.dotted, self.group_dotted = sem("dotted"), sem("group_dotted")
        self.gelu_done, self.weighted = sem("gelu_done"), sem("weighted")
        self.diag_made, self.weighed, self.added = sem("diag_made"), sem("weighed"), sem("added")
        self.y_taken, self.squares, self.roots = sem("y_taken"), sem("squares"), sem("roots")
        self.y_ready, self.y_out = sem("y_ready"), sem("y_out")

    @staticmethod
    def last_of_run(t):
        return isinstance(t, int) and t + 1 in RUNS.values()

    def follows(self, t, h):
        heads = HEADS // PACK if isinstance(t, int) and t == SAMPLE else HEADS
        return not (self.last_of_run(t) and h == heads - 1)

    def ranks_group(self, t, h):
        if not isinstance(t, int) or t == SAMPLE:
            return not isinstance(t, int)
        end = GROUPS_ALL if t >= len(FIRST.tiles) else len(FIRST.tiles) * HEADS
        return t * HEADS + h + RANK_AHEAD < end

    @staticmethod
    def weighed_at(n, c):
        return n * len(ON_PE) + (len(ON_PE) + ON_PE.index(c) + 1)

    @staticmethod
    def added_at(n, c):
        return n * len(ON_DVE) + (len(ON_DVE) + ON_DVE.index(c) + 1)

    def pool_start(self, pool):
        make_identity(pool, self.ident, self.made)
        pool.iota(self.ranks[:, :], pattern=[[1, TOPK]], base=0, channel_multiplier=0,
                  allow_small_or_imprecise_dtypes=True).then_inc(self.ranks_made, 1)
        pool.dma_start(self.g_fin[:, :], self.a["norm_final"].to_broadcast([P, D])).then_inc(self.g_in, 16)
        self.pool_run(pool, 0)

    def gather(self, pool, buf, table, slot, c, signal):
        pool.indirect_dma_start(out=buf[:, :], out_offset=None, in_=table,
                                in_offset=bass.IndirectOffsetOnAxis(ap=self.idx[slot][:, c:c + 1], axis=0)).then_inc(signal, 16)

    def load_scores(self, pool, m, par):
        if not (isinstance(m, int) and m < 2):
            until(pool, self.scores_read, m - 1, self.passed)
        src = self.s["sc"][m, :, :] if isinstance(m, int) else self.s["sc"][bass.ds(m, 1), :, :].rearrange("g p n -> (g p) n")
        pool.dma_start(self.sc[par][:, :, :].rearrange("p j n -> p (j n)"), src).then_inc(self.sc_in[par], 16)

    def load_h2(self, pool, t):
        rows = self.s["h2"]
        if isinstance(t, int) and t == SAMPLE:
            for q in range(PACK):
                pool.dma_start(self.h2_next[DEC * q:DEC * (q + 1), :], rows[SEQ:TOK, :]).then_inc(self.h2_in, 16)
        else:
            own = slice(t * P, (t + 1) * P) if isinstance(t, int) else bass.ds(t * P, P)
            pool.dma_start(self.h2_next[:, :], rows[own, :]).then_inc(self.h2_in, 16)

    def pool_run(self, pool, t):
        n = t * HEADS
        for i in range(2):
            self.load_scores(pool, n + i, i % 2)
        if t:
            pool.wait_ge(self.h2_copied, t)
        self.load_h2(pool, t)
        pool.wait_ge(self.ranked, n + 1)
        for c in range(TOPK):
            if n or c >= SLOTS_G:
                pool.wait_ge(self.dotted, n * TOPK + c - SLOTS_G + 1)
            self.gather(pool, self.u_rows[c % SLOTS_G], self.a["peer_u"], 0, c, self.u_in[c % SLOTS_G])
        self.load_scores(pool, n + 2, 0)

    def pool_tile(self, pool, t, heads):
        sample = isinstance(t, int) and t == SAMPLE
        for h in heads:
            n = t * HEADS + h
            follow = self.follows(t, h)
            if self.ranks_group(t, h):
                self.load_scores(pool, n + RANK_AHEAD, (h + 1) % 2)
            if follow:
                until(pool, self.ranked, n + 2, self.passed)
            for c in range(TOPK):
                k = c % SLOTS_G
                count, signal = (self.added_at, self.added) if c in ON_DVE else (self.weighed_at, self.weighed)
                last_use = count(n, c - SLOTS_G) if c >= SLOTS_G else count(n - 1, c + SLOTS_G)
                until(pool, signal, last_use, self.passed)
                self.gather(pool, self.v_rows[k], self.a["peer_v"], h % HEADS, c, self.v_in[k])
                if follow:
                    until(pool, self.dotted, n * TOPK + (TOPK + c - SLOTS_G + 1), self.passed)
                    self.gather(pool, self.u_rows[k], self.a["peer_u"], (h + 1) % HEADS, c, self.u_in[k])
                if c == SLOTS_G and h == (0 if sample else 2):
                    until(pool, self.y_ready, t + 1, self.passed)
                    r = DEC if sample else P
                    before = slice(t * P, (t + 1) * P) if isinstance(t, int) else bass.ds(t * P, P)
                    own = slice(t * P, t * P + r) if isinstance(t, int) else bass.ds(t * P, P)
                    pool.dma_start(self.s["y"][before, :], self.y[:, :]).then_inc(self.y_out, 16)
                    pool.dma_start(self.x1[0:r, :], self.s["x1"][own, :]).then_inc(self.x1_in, 16)
                if c == SLOTS_G and h == 3 and not self.last_of_run(t):
                    until(pool, self.h2_copied, t + 1, self.passed)
                    self.load_h2(pool, t + 1)

    def rank(self, dve, m, par, slot, piece):
        sc, rest, best1, pos1, best, sel = self.sc[par], self.rest, self.best1, self.pos1, self.best, self.sel
        flat, flat_rest = (b[:, :, :].rearrange("p a b -> p (a b)") for b in (self.cand, self.cand_rest))
        if piece == 0:
            until(dve, self.sc_in[par], (m // 2) * 16 + 16 if isinstance(m, int) else m * 8 + (16 - 8 * par), self.passed)
            for j in range(2):
                dve.max(best1[:, j, 0:8], sc[:, j, :])
            dve.drain()
            for j in range(2):
                dve.max_index(pos1[:, j, 0:8], best1[:, j, 0:8], sc[:, j, :])
                dve.match_replace(rest[:, j, :], best1[:, j, 0:8], sc[:, j, :], LOWEST)
            dve.drain().then_inc(self.scores_read, 1)
        elif piece == 1:
            for j in range(2):
                dve.max(best1[:, j, 8:16], rest[:, j, :])
            dve.drain()
            for j in range(2):
                dve.max_index(pos1[:, j, 8:16], best1[:, j, 8:16], rest[:, j, :])
            dve.tensor_tensor(self.cand[:, :, :], best1[:, 0, :].unsqueeze(2).to_broadcast([P, TOPK, TOPK]),
                              best1[:, 1, :].unsqueeze(1).to_broadcast([P, TOPK, TOPK]), ALU.add)
            dve.drain()
            dve.tensor_copy(self.pos1f[:, :, :], pos1[:, :, :])
        elif piece == 2:
            dve.max(best[:, 0:8], flat)
            dve.drain()
            dve.max_index(sel[:, 0:8], best[:, 0:8], flat)
            dve.match_replace(flat_rest, best[:, 0:8], flat, LOWEST)
            dve.tensor_scalar(self.nbest[:, :], best[:, 0:1], -1.0, None, ALU.mult)
            dve.drain()
            dve.max(best[:, 8:16], flat_rest)
            dve.drain().then_inc(self.gate_max, 1)
            dve.max_index(sel[:, 8:16], best[:, 8:16], flat_rest)
        else:
            dve.drain()
            dve.tensor_scalar(self.part[:, 0, :], sel[:, :], 4, None, ALU.logical_shift_right)
            dve.tensor_scalar(self.part[:, 1, :], sel[:, :], TOPK - 1, None, ALU.bitwise_and)
            dve.drain()
            dve.tensor_copy(self.partf[:, :, :], self.part[:, :, :])
            dve.drain()
            hot = self.hot
            dve.tensor_tensor(hot[:, :, :], self.ranks[:, :].unsqueeze(1).to_broadcast([P, 2 * TOPK, TOPK]),
                              self.partf[:, :, :].rearrange("p j k -> p (j k)").unsqueeze(2).to_broadcast([P, 2 * TOPK, TOPK]), ALU.is_equal)
            dve.drain()
            for j in range(2):
                half = hot[:, j * TOPK:(j + 1) * TOPK, :]
                dve.tensor_tensor(half, half, self.pos1f[:, j, :].unsqueeze(1).to_broadcast([P, TOPK, TOPK]), ALU.mult)
            dve.drain()
            dve.tensor_reduce(self.key[:, :, :].rearrange("p j k -> p (j k)"), hot[:, :, :], AX, ALU.add)
            dve.drain()
            dve.scalar_tensor_tensor(out=self.idx[slot][:, :], in0=self.key[:, 0, :], scalar=float(P), in1=self.key[:, 1, :],
                                     op0=ALU.mult, op1=ALU.add).then_inc(self.ranked, 1)

    def gate(self, dve, m, slot):
        until(dve, self.gate_exped, m + 1, self.passed)
        dve.reciprocal(self.einv[:, :], self.esum[:, :])
        dve.drain()
        dve.tensor_scalar(self.gates[slot][:, :], self.egate[:, :], self.einv[:, 0:1], None, ALU.mult)

    def dot(self, dve, m, par, c):
        k = c % SLOTS_G
        until(dve, self.u_in[k], m * 32 + (c // SLOTS_G * 16 + 16), self.passed)
        dve.tensor_tensor_reduce(out=self.u_rows[k][:, :], in0=self.u_rows[k][:, :], in1=self.h2[:, :], scale=1.0, scalar=0.0,
                                 op0=ALU.mult, op1=ALU.add, accum_out=self.dots[par][:, c:c + 1]).then_inc(self.dotted, 1)
        if c == TOPK - 1:
            dve.drain().then_inc(self.group_dotted, 1)

    def copy_h2(self, dve, t):
        until(dve, self.h2_in, 16 * (t + 1) if not (isinstance(t, int) and t == SAMPLE) else 16 * (SAMPLE + PACK), self.passed)
        dve.drain()
        dve.tensor_copy(self.h2[:, :], self.h2_next[:, :]).then_inc(self.h2_copied, 1)
        dve.drain()

    def dve_start(self, dve):
        dve.wait_ge(self.made, 2)
        dve.wait_ge(self.ranks_made, 1)
        fold, ident = self.fold, self.ident
        dve.tensor_copy(fold[:, :], ident[:, 0:DEC])
        for q in range(1, PACK):
            dve.drain()
            dve.tensor_tensor(fold[:, :], fold[:, :], ident[:, DEC * q:DEC * (q + 1)], ALU.add)
        dve.memset(self.y[:, :], 0.0)
        dve.drain()
        dve.sem_inc(self.fold_made, 1)
        dve.sem_inc(self.y_ready, 1)
        dve.sem_inc(self.added, len(ON_DVE))
        dve.sem_inc(self.y_taken, 1)
        dve.wait_ge(self.g_in, 16)
        self.dve_run(dve, 0)

    def dve_run(self, dve, t):
        n = t * HEADS
        for m in range(2):
            for piece in range(4):
                self.rank(dve, n + m, m, m, piece)
            self.gate(dve, n + m, m)
        self.copy_h2(dve, t)
        for c in range(TOPK):
            self.dot(dve, n, 0, c)
        self.weigh(dve, n, 0, 0)
        for piece in range(4):
            self.rank(dve, n + 2, 0, 2, piece)
        self.gate(dve, n + 2, 2)

    def weigh(self, dve, m, par, slot):
        until(dve, self.gelu_done, m + 1, self.passed)
        until(dve, self.diag_made, (m + 1) * len(ON_PE), self.passed)
        dve.drain()
        dve.tensor_tensor(self.weights[par][:, :], self.gelus[par][:, :], self.gates[slot][:, :], ALU.mult).then_inc(self.weighted, 1)

    def dve_step(self, dve, t, h, c):
        n, par = t * HEADS + h, h % 2
        if self.ranks_group(t, h) and c % 3 == 2 and c < 12:
            if c == 2:
                until(dve, self.weighed, (n + 1) * len(ON_PE), self.passed)
            self.rank(dve, n + RANK_AHEAD, (h + 1) % 2, (h + RANK_AHEAD) % HEADS, c // 3)
        if self.follows(t, h):
            if h == HEADS - 1 and c == 0:
                self.copy_h2(dve, t + 1)
            self.dot(dve, n + 1, (h + 1) % 2, c)
        if c in ON_DVE:
            k = c % SLOTS_G
            until(dve, self.v_in[k], n * 32 + (c // SLOTS_G * 16 + 16), self.passed)
            dve.drain()
            weight = self.weights[par][:, c:c + 1]
            if h == 0 and c == ON_DVE[0]:
                dve.tensor_scalar(self.acc[:, :], self.v_rows[k][:, :], weight, None, ALU.mult).then_inc(self.added, 1)
            else:
                dve.scalar_tensor_tensor(out=self.acc[:, :], in0=self.v_rows[k][:, :], scalar=weight, in1=self.acc[:, :],
                                         op0=ALU.mult, op1=ALU.add).then_inc(self.added, 1)
        if c == TOPK - 1 and self.follows(t, h):
            self.weigh(dve, n + 1, (h + 1) % 2, (h + 1) % HEADS)
        if c == TOPK - 1 and self.ranks_group(t, h):
            self.gate(dve, n + RANK_AHEAD, (h + RANK_AHEAD) % HEADS)

    def dve_finish(self, dve, t):
        sample = isinstance(t, int) and t == SAMPLE
        r = DEC if sample else P
        x1, y = self.x1, self.y
        if sample:
            dve.wait_ge(self.weighed, (GROUPS_ALL + 1) * len(ON_PE) + 1)
        else:
            until(dve, self.weighed, self.weighed_at(t * HEADS + (HEADS - 1), ON_PE[-1]), self.passed)
        until(dve, self.x1_in, t * 16 + 16, self.passed)
        dve.tensor_tensor(x1[0:r, :], self.ps_y[0:r, :], x1[0:r, :], ALU.add).then_inc(self.y_taken, 1)
        dve.drain()
        if not sample:
            dve.tensor_tensor(x1[:, :], x1[:, :], self.acc[:, :], ALU.add)
            dve.drain()
        until(dve, self.y_out, t * 16 + 16, self.passed)
        dve.tensor_tensor_reduce(out=y[0:r, :], in0=x1[0:r, :], in1=x1[0:r, :], scale=1.0 / D, scalar=EPS,
                                 op0=ALU.mult, op1=ALU.add, accum_out=self.ms[0:r, :])
        dve.drain().then_inc(self.squares, 1)
        until(dve, self.roots, t + 1, self.passed)
        dve.reciprocal(self.rs[0:r, :], self.root[0:r, :])
        dve.drain()
        dve.scalar_tensor_tensor(out=y[0:r, :], in0=x1[0:r, :], scalar=self.rs[0:r, 0:1], in1=self.g_fin[0:r, :],
                                 op0=ALU.mult, op1=ALU.mult).then_inc(self.y_ready, 1)

    def gate_exp(self, act, m):
        until(act, self.gate_max, m + 1, self.passed)
        act.activation(self.egate[:, :], self.best[:, :], ACT.Exp, bias=self.nbest[:, 0:1], accum_out=self.esum[:, 0:1]).then_inc(self.gate_exped, 1)

    def gelu(self, act, m, par):
        until(act, self.group_dotted, m + 1, self.passed)
        act.activation(self.gelus[par][:, :], self.dots[par][:, :], ACT.Gelu).then_inc(self.gelu_done, 1)

    def act_start(self, act):
        act.wait_ge(self.made, 2)
        act.sem_inc(self.diag_made, 2 * len(ON_PE))
        self.act_run(act, 0)

    def act_run(self, act, t):
        n = t * HEADS
        self.gate_exp(act, n)
        self.gate_exp(act, n + 1)
        self.gelu(act, n, 0)
        self.gate_exp(act, n + 2)

    def act_diag(self, act, t, h, c):
        n = t * HEADS + h
        if c in ON_PE:
            i = ON_PE.index(c)
            sample = isinstance(t, int) and t == SAMPLE
            matrix, width = (self.fold, DEC) if sample else (self.ident, P)
            if i == 0:
                until(act, self.weighted, n + 1, self.passed)
                if sample:
                    act.wait_ge(self.fold_made, 1)
            until(act, self.weighed, n * len(ON_PE) + (len(ON_PE) + i - 3), self.passed)
            act.activation(self.diag[i % 4][:, 0:width], matrix[:, 0:width], ACT.Copy,
                           scale=self.weights[h % 2][:, c:c + 1]).then_inc(self.diag_made, 1)

    def act_rest(self, act, t, h, c):
        n = t * HEADS + h
        if c == 10 and self.ranks_group(t, h):
            self.gate_exp(act, n + RANK_AHEAD)
        if c == TOPK - 1 and self.follows(t, h):
            self.gelu(act, n + 1, (h + 1) % 2)

    def act_finish(self, act, t):
        r = DEC if isinstance(t, int) and t == SAMPLE else P
        until(act, self.squares, t + 1, self.passed)
        act.activation(self.root[0:r, :], self.ms[0:r, :], ACT.Sqrt).then_inc(self.roots, 1)

    def pe_start(self, pe):
        pe.sem_inc(self.weighed, len(ON_PE))

    def pe_step(self, pe, t, h, c):
        if c not in ON_PE:
            return
        n, k, i = t * HEADS + h, c % SLOTS_G, ON_PE.index(c)
        sample = isinstance(t, int) and t == SAMPLE
        r = DEC if sample else P
        if h == 0 and i == 0:
            until(pe, self.y_taken, t + 1, self.passed)
        until(pe, self.v_in[k], n * 32 + (c // SLOTS_G * 16 + 16), self.passed)
        until(pe, self.diag_made, n * len(ON_PE) + (2 * len(ON_PE) + i + 1), self.passed)
        for half in range(2):
            cols = slice(512 * half, 512 * (half + 1))
            last = pe.matmul(self.ps_y[0:r, cols], self.diag[i % 4][:, 0:r], self.v_rows[k][:, cols],
                             start=(h == 0 and i == 0), stop=(not sample and h == HEADS - 1 and c == ON_PE[-1]))
        last.then_inc(self.weighed, 1)

    def pe_finish(self, pe, t):
        if isinstance(t, int) and t == SAMPLE:
            pe.wait_ge(self.added, self.added_at(GROUPS_ALL - 1, ON_DVE[-1]))
            for half in range(2):
                cols = slice(512 * half, 512 * (half + 1))
                last = pe.matmul(self.ps_y[0:DEC, cols], self.fold[:, :], self.acc[:, cols], start=False, stop=True)
            last.then_inc(self.weighed, 1)

    def atom(self, kind, eng, t, k):
        parts = {"pe": (self.pe_step, self.pe_finish), "dve": (self.dve_step, self.dve_finish),
                 "act": (self.act_diag, self.act_rest, self.act_finish),
                 "act_diag": (self.act_diag,), "act_rest": (self.act_rest, self.act_finish)}[kind]
        last = k == (TOPK * HEADS // PACK if isinstance(t, int) and t == SAMPLE else ATOMS) - 1
        for part in parts:
            if part not in (self.pe_finish, self.dve_finish, self.act_finish):
                part(eng, t, k // TOPK, k % TOPK)
            elif last:
                part(eng, t)

    def second_run(self):
        first, loops = len(FIRST.tiles), KEY_TILES - 1 - len(FIRST.tiles)
        with self.nc.Block() as block:
            def tiles(kind, eng):
                with eng.Fori(0, loops) as i:
                    for k in range(ATOMS):
                        self.atom(kind, eng, i + first, k)
                for k in range(ATOMS):
                    self.atom(kind, eng, KEY_TILES - 1, k)
                for k in range(TOPK * HEADS // PACK):
                    self.atom(kind, eng, SAMPLE, k)

            @block.gpsimd
            def _(pool):
                self.pool_run(pool, first)
                with pool.Fori(0, loops) as i:
                    self.pool_tile(pool, i + first, range(HEADS))
                self.pool_tile(pool, KEY_TILES - 1, range(HEADS))
                self.pool_tile(pool, SAMPLE, range(HEADS // PACK))
                pool.wait_ge(self.y_ready, SAMPLE + 2)
                pool.dma_start(self.s["y"][P + SEQ:P + TOK, :], self.y[0:DEC, :]).then_inc(self.y_out, 16)
                pool.wait_ge(self.y_out, 16 * (SAMPLE + 2))

            @block.vector
            def _(dve):
                self.dve_run(dve, first)
                tiles("dve", dve)

            @block.scalar
            def _(act):
                self.act_run(act, first)
                tiles("act", act)

            @block.tensor
            def _(pe):
                tiles("pe", pe)


def build(nc, a, outs):
    s = dict(outs)
    for name, shape in (("hT", (DC, P, ROWS)), ("vm", (KEYS, BR)), ("kT", (HEADS, QK, KEYS)), ("qT", (HEADS, QK, ROWS)),
                        ("dkT", (4, P, KEYS)), ("dqT", (4, P, ROWS)), ("mqT", (MEM_HEADS, P, ROWS)),
                        ("mkT", (2, MEM_HEADS, P, MEM)), ("oT", (3 * BR // P, P, ROWS)), ("skT", (2 * HEADS, P, P)),
                        ("x1", (ROWS, D)), ("h2", (ROWS, D)), ("h2T", (DC, P, ROWS)), ("sc", (66, P, 2 * P))):
        s[name] = nc.dram_tensor(f"scratch_{name}", shape, F32, kind="Internal").ap()
    project_inputs(nc, a, s)
    cached_and_memory_keys(nc, a, s)
    attention(nc, a, s, FIRST, "C1")
    with ExitStack() as ctx:
        mergedT = ctx.enter_context(nc.sbuf_tensor("mergedT1", [P, DC, FIRST.n], F32))
        merge_branches(nc, a, s, mergedT, FIRST, "D1")
        h2T = ctx.enter_context(nc.sbuf_tensor("h2T1", [P, DC, FIRST.n], F32))
        project_out(nc, a, s, mergedT, h2T, FIRST, "E1")
        score_experts(nc, a, s, h2T, FIRST, "F1")
    with ExitStack() as experts_ctx:
        ex = Experts(nc, experts_ctx, a, s)
        attention(nc, a, s, SECOND, "C2", ex)
        with ExitStack() as ctx:
            mergedT = ctx.enter_context(nc.sbuf_tensor("mergedT2", [P, DC, SECOND.n], F32))
            merge_branches(nc, a, s, mergedT, SECOND, "D2", ex, 2)
            h2T = ctx.enter_context(nc.sbuf_tensor("h2T2", [P, DC, SECOND.n], F32))
            project_out(nc, a, s, mergedT, h2T, SECOND, "E2", ex, 3, range(0, 3))
            score_experts(nc, a, s, h2T, SECOND, "F2", ex, 3, range(3, HEADS))
        ex.second_run()


_WEIGHTS = ["norm_mix", "w_in", "mla_q_norm", "w_uq", "mla_kv_norm", "w_uk", "w_uv", "diff_lq1", "diff_lk1",
            "diff_lq2", "diff_lk2", "diff_subln", "norm_mem", "w_mem_kv", "w_br_a", "w_br_b", "w_br_m", "w_gate",
            "b_gate", "w_o", "norm_ffn", "peer_wq", "peer_subkeys", "peer_u", "peer_v", "norm_final",
            "cache_mla_ckv", "cache_mla_krope", "cache_diff_k", "cache_diff_v", "cache_mem_k", "cache_mem_v",
            "mem_prompt"]


def rotary_table():
    half = ROPE // 2
    pos = np.concatenate([np.arange(SEQ), PAST + np.arange(PAD_ROWS - SEQ)]).astype(np.float32)
    inv = (1.0 / (np.float32(10000.0) ** (np.arange(half, dtype=np.float32) / np.float32(half)))).astype(np.float32)
    ang = pos[:, None] * inv[None, :]
    return np.concatenate([np.cos(ang), np.sin(ang)], axis=-1).astype(np.float32)


def kernel(**inputs):
    import concourse.bacc as bacc
    from concourse.bass_utils import run_bass_kernel_spmd as run

    nc = bacc.Bacc("TRN2", target_bir_lowering=False, num_devices=1)
    arrays, a = {}, {}

    def take(name, array):
        arrays[f"in_{name}"] = array
        a[name] = nc.dram_tensor(f"in_{name}", array.shape, F32, kind="ExternalInput").ap()

    x_all = np.zeros((PAD_ROWS, D), np.float32)
    x_all[0:SEQ] = inputs["x_prompt"][0]
    x_all[SEQ:TOK] = inputs["x_sample"][0]
    take("x_all", x_all)
    take("cos_sin", rotary_table())
    for name in _WEIGHTS:
        w = np.ascontiguousarray(inputs[name])
        if name == "peer_subkeys":
            w = w.reshape(2 * HEADS * P, P)
        elif name == "b_gate":
            w = np.ascontiguousarray(w.reshape(-1, P).T)
        elif name.startswith("cache"):
            w = w.reshape(w.shape[2], -1)
        elif w.ndim == 3:
            w = w[0]
        elif w.ndim == 1:
            w = w.reshape(1, -1)
        take(name, w)

    outs = {name: nc.dram_tensor(f"out_{name}", shape, F32, kind="ExternalOutput").ap() for name, shape in
            (("y", (P + TOK, D)), ("ckv", (ROWS, KV_LORA)), ("krope", (ROWS, ROPE)), ("dk", (ROWS, BR)), ("dv", (ROWS, BR)),
             ("mk", (MEM, BR)), ("mv", (MEM, BR)))}
    build(nc, a, outs)
    got = run(nc, [arrays], core_ids=[0]).results[0]

    def rows(name, lo, hi, *shape):
        return got[f"out_{name}"][lo:hi].reshape(*shape)

    prompt, sample = (1, 1, SEQ), (1, 1, DEC)
    return (rows("y", P, P + SEQ, 1, SEQ, D), rows("y", P + SEQ, P + TOK, 1, DEC, D),
            rows("ckv", 0, SEQ, *prompt, KV_LORA), rows("krope", 0, SEQ, *prompt, ROPE),
            rows("dk", 0, SEQ, *prompt, HEADS, VD), rows("dv", 0, SEQ, *prompt, HEADS, VD),
            rows("mk", 0, MEM, 1, 1, MEM, MEM_HEADS, MDH), rows("mv", 0, MEM, 1, 1, MEM, MEM_HEADS, MDH),
            rows("ckv", SEQ, TOK, *sample, KV_LORA), rows("krope", SEQ, TOK, *sample, ROPE),
            rows("dk", SEQ, TOK, *sample, HEADS, VD), rows("dv", SEQ, TOK, *sample, HEADS, VD))
```

```python
from contextlib import ExitStack

import numpy as np

import concourse.bass as bass
from concourse import mybir

F32 = mybir.dt.float32
I32 = mybir.dt.int32
U32 = mybir.dt.uint32
ALU = mybir.AluOpType
ACT = mybir.ActivationFunctionType
AX = mybir.AxisListType.X

P = 128
D = 1024
DC = D // P
SEQ, DEC, PAST = 1024, 32, 128
TOK = SEQ + DEC
TILES = -(-TOK // P)
ROWS = TILES * P
PAD_ROWS = ROWS + 2 * P
CACHE = ROWS
KEYS = ROWS + PAST
MEM = 256
EPS = 1e-6
HEADS = 8
NOPE, ROPE, VD = 64, 32, 64
QK = NOPE + ROPE
Q_LORA, KV_LORA = 384, 256
BR = 512
DDH = 32
MEM_HEADS, MDH = 4, 128
MLA_SCALE = QK ** -0.5
DIFF_SCALE = DDH ** -0.5
MEM_SCALE = MDH ** -0.5
CHUNK = 64
TOPK = 16
Z_CUTS = [0, Q_LORA, Q_LORA + KV_LORA + ROPE]
Z_CUTS += [Z_CUTS[-1] + BR * (i + 1) for i in range(4)]
Z_COLS = list(zip(Z_CUTS[:-1], Z_CUTS[1:]))
IN_W = Z_CUTS[-1]


def until(eng, sem, value, passed):
    eng.wait_ge(sem, value)
    if not isinstance(value, int):
        eng.sem_inc(passed, 1)


def clear(nc, sems):
    with nc.Block() as block:
        @block.gpsimd
        def _(pool):
            nc.clear_and_free_semaphores(sems)


def tools(nc, ctx, tag):
    sems = []
    ctx.callback(clear, nc, sems)

    def sb(name, shape, dt=F32):
        return ctx.enter_context(nc.sbuf_tensor(f"{tag}_{name}", shape, dt))

    def psum(name, shape):
        return ctx.enter_context(nc.psum_tensor(f"{tag}_{name}", shape, F32))

    def sem(name):
        sems.append(nc.alloc_semaphore(name=f"{tag}_{name}"))
        return sems[-1]
    return sb, psum, sem


def beside(ex, kind, eng, tile, heads, i, of, half=None):
    if ex:
        groups = len(heads)
        q = next(q for q in range(groups) if i < of * (q + 1) // groups)
        first, last = of * q // groups, of * (q + 1) // groups
        share = range(TOPK * (i - first) // (last - first), TOPK * (i - first + 1) // (last - first))
        if half is not None:
            share = (share[:len(share) // 2], share[len(share) // 2:])[half]
        for c in share:
            ex.atom(kind, eng, tile, heads[q], c)


def make_identity(pool, ident, made):
    pool.memset(ident[:, :], 0.0).then_inc(made, 1)
    pool.wait_ge(made, 1)
    pool.affine_select(out=ident[:, :], in_=ident[:, :], compare_op=ALU.not_equal, fill=1.0, base=0,
                       pattern=[[-1, P]], channel_multiplier=1).then_inc(made, 1)


def project_inputs(nc, a, s):
    MMS, TURNS = 10, 11
    with ExitStack() as ctx:
        sb, psum, sem = tools(nc, ctx, "A")
        ident = sb("ident", [P, P])
        w_in = sb("w_in", [P, DC, IN_W])
        w_uq = sb("w_uq", [P, Q_LORA // P, HEADS * QK])
        w_uk = sb("w_uk", [P, KV_LORA // P, BR])
        w_uv = sb("w_uv", [P, KV_LORA // P, BR])
        g_mix, g_q, g_kv = sb("g_mix", [P, D]), sb("g_q", [P, Q_LORA]), sb("g_kv", [P, KV_LORA])
        xt = [sb(f"xt{i}", [P, D]) for i in range(2)]
        cs = [sb(f"cs{i}", [P, ROPE]) for i in range(2)]
        junk = sb("junk", [P, D])
        xn = sb("xn", [P, D])
        hT = [sb(f"hT{i}", [P, DC, P]) for i in range(2)]
        ms, root, rs = sb("ms", [P, 4]), sb("root", [P, 4]), sb("rs", [P, 4])
        cq, kv = sb("cq", [P, Q_LORA]), sb("kv", [P, KV_LORA + ROPE])
        cqn, kvn, krr = sb("cqn", [P, Q_LORA]), sb("kvn", [P, KV_LORA]), sb("krr", [P, ROPE])
        cqT, kvT = sb("cqT", [P, Q_LORA]), sb("kvT", [P, KV_LORA])
        dq = [sb(f"dq{i}", [P, BR]) for i in range(2)]
        dk = [sb(f"dk{i}", [P, BR]) for i in range(2)]
        dv = [sb(f"dv{i}", [P, BR]) for i in range(2)]
        mq = [sb(f"mq{i}", [P, BR]) for i in range(2)]
        q_sb, k_sb, v_sb = sb("q_sb", [P, HEADS, QK]), sb("k_sb", [P, HEADS, QK]), sb("v_sb", [P, BR])
        rot = sb("rot", [P, 4, HEADS, ROPE // 2])
        kT, qT = sb("kT", [P, HEADS, P]), sb("qT", [P, HEADS, P])
        dkT, dqT, mqT = sb("dkT", [P, 4, P]), sb("dqT", [P, 4, P]), sb("mqT", [P, 4, P])
        ps_t = [psum(f"turn{i}", [P, 512]) for i in range(2)]
        ps_m = [psum(f"mm{i}", [P, 512]) for i in range(4)]

        made, passed = sem("identity"), sem("loop_waits")
        w_z = [sem(f"w_in{i}") for i in range(6)]
        w_up, gains = sem("w_up"), sem("gains")
        x_in = [sem(f"x_in{i}") for i in range(2)]
        cs_in = [sem(f"cs_in{i}") for i in range(2)]
        squares, roots, normed = sem("squares"), sem("roots"), sem("normed")
        turned, t_copied = sem("turned"), sem("t_copied")
        mm_done, m_copied = sem("mm_done"), sem("m_copied")
        heads_ready, latents_done, roped = sem("heads_ready"), sem("latents_done"), sem("q_roped")
        v_out, kv_out = sem("v_out"), sem("kv_out")
        h_out = [sem(f"h_out{i}") for i in range(2)]
        d_out = [sem(f"d_out{i}") for i in range(2)]
        t_out = {k: sem(f"{k}_out") for k in ("kT", "qT", "dkT", "dqT", "mqT")}
        block = ctx.enter_context(nc.Block())

        @block.gpsimd
        def _(pool):
            make_identity(pool, ident, made)
            for j in range(2):
                pool.dma_start(xt[j][:, :], a["x_all"][j * P:(j + 1) * P, :]).then_inc(x_in[j], 16)
                pool.dma_start(cs[j][:, :], a["cos_sin"][j * P:(j + 1) * P, :]).then_inc(cs_in[j], 16)
            until(pool, normed, 1, passed)
            pool.dma_start(xt[0][:, :], a["x_all"][2 * P:3 * P, :]).then_inc(x_in[0], 16)
            with pool.Fori(0, TILES // 2) as g:
                for par in range(2):
                    j = g * 2 + par
                    until(pool, roped, j + 1, passed)
                    pool.dma_start(cs[par][:, :], a["cos_sin"][bass.ds(j * P + 2 * P, P), :]).then_inc(cs_in[par], 16)
                    until(pool, normed, j + 2, passed)
                    pool.dma_start(xt[1 - par][:, :], a["x_all"][bass.ds(j * P + 3 * P, P), :]).then_inc(x_in[1 - par], 16)

        @block.sync
        def _(sp):
            for w, name in ((g_mix, "norm_mix"), (g_q, "mla_q_norm"), (g_kv, "mla_kv_norm")):
                sp.dma_start(w[:, :], a[name].to_broadcast(list(w.shape))).then_inc(gains, 16)
            w_view = a["w_in"].rearrange("(c p) n -> p c n", p=P)
            for i, (lo, hi) in enumerate(Z_COLS):
                sp.dma_start(w_in[:, :, lo:hi], w_view[:, :, lo:hi]).then_inc(w_z[i], 16)
            for w, name in ((w_uq, "w_uq"), (w_uk, "w_uk"), (w_uv, "w_uv")):
                sp.dma_start(w[:, :, :], a[name].rearrange("(c p) n -> p c n", p=P)).then_inc(w_up, 16)

            def rows(t):
                return slice(t * P, (t + 1) * P) if isinstance(t, int) else bass.ds(t * P, P)

            def store_projected(t, par, mm0, tn0):
                until(sp, t_copied, tn0 + 2, passed)
                sp.dma_start(s["hT"].rearrange("c p n -> p c n")[:, :, rows(t)], hT[par][:, :, :]).then_inc(h_out[par], 16)
                until(sp, latents_done, t + 1, passed)
                sp.dma_start(s["ckv"][rows(t), :], kvn[:, :]).then_inc(kv_out, 16)
                sp.dma_start(s["krope"][rows(t), :], krr[:, :]).then_inc(kv_out, 16)
                until(sp, m_copied, mm0 + 5, passed)
                sp.dma_start(s["dk"][rows(t), :], dk[par][:, :]).then_inc(d_out[par], 16)
                sp.dma_start(s["dv"][rows(t), :], dv[par][:, :]).then_inc(d_out[par], 16)

            def store_values(t):
                until(sp, m_copied, t * MMS + 10, passed)
                sp.dma_start(s["vm"][rows(t), :], v_sb[:, :]).then_inc(v_out, 16)

            def store_turned(t):
                for n, (name, buf, top) in {5: ("kT", kT, QK), 7: ("qT", qT, QK), 8: ("dkT", dkT, P),
                                            9: ("dqT", dqT, P), 10: ("mqT", mqT, P)}.items():
                    until(sp, t_copied, t * TURNS + (2 + n + 1), passed)
                    sp.dma_start(s[name].rearrange("c p n -> p c n")[:, :, rows(t)], buf[0:top, :, :]).then_inc(t_out[name], 16)

            store_projected(0, 0, 0, 0)
            with sp.Fori(0, TILES // 2) as g:
                for par in range(2):
                    j = g * 2 + par
                    store_values(j)
                    store_projected(j + 1, 1 - par, j * MMS + 10, j * TURNS + 4)
                    store_turned(j)
            store_values(TILES - 1)
            store_turned(TILES - 1)
            sp.wait_ge(v_out, 16 * TILES)
            sp.wait_ge(kv_out, 32 * TILES)
            for i in range(2):
                sp.wait_ge(h_out[i], 16 * ((TILES + 1 - i) // 2))
                sp.wait_ge(d_out[i], 32 * ((TILES + 1 - i) // 2))
            for q in t_out.values():
                sp.wait_ge(q, 16 * TILES)

        @block.tensor
        def _(pe):
            def turn(n, bank, blocks, top):
                if not (isinstance(n, int) and n < 2):
                    until(pe, t_copied, n - 1, passed)
                for b, src in enumerate(blocks):
                    last = pe.transpose(ps_t[bank][0:top, b * P:(b + 1) * P], src, ident[:, :])
                last.then_inc(turned, 1)

            def product(n, bank, lhs, w, lo, hi):
                if not (isinstance(n, int) and n < 4):
                    until(pe, m_copied, n - 3, passed)
                for c in range(len(lhs)):
                    last = pe.matmul(ps_m[bank][:, 0:hi - lo], lhs[c], w[:, c, lo:hi], start=(c == 0),
                                     stop=(c == len(lhs) - 1))
                last.then_inc(mm_done, 1)

            def chunks(buf, lo, hi):
                return [buf[:, c * P:(c + 1) * P] for c in range(lo, hi)]

            def turn_h(n, bank):
                turn(n, bank, chunks(xn, 0, 4), P)
                turn(n + 1, 1 - bank, chunks(xn, 4, 8), P)

            def project(n, bank, par, first):
                for i, (lo, hi) in enumerate(Z_COLS):
                    if first:
                        pe.wait_ge(w_z[i], 16)
                    product(n + i, (bank + i) % 4, [hT[par][:, c, :] for c in range(DC)], w_in, lo, hi)

            def latents(j, par):
                until(pe, normed, j + 2, passed)
                turn(j * TURNS + 2, par, chunks(cqn, 0, 3), P)
                turn(j * TURNS + 3, 1 - par, chunks(kvn, 0, 2), P)

            def ups(j, par):
                n, bank = j * MMS + 6, (2 + 2 * par) % 4
                until(pe, t_copied, j * TURNS + 4, passed)
                product(n, bank, chunks(cqT, 0, 3), w_uq, 0, 512)
                product(n + 1, (bank + 1) % 4, chunks(cqT, 0, 3), w_uq, 512, HEADS * QK)
                product(n + 2, (bank + 2) % 4, chunks(kvT, 0, 2), w_uk, 0, BR)
                product(n + 3, (bank + 3) % 4, chunks(kvT, 0, 2), w_uv, 0, BR)

            def turn_heads(j, par):
                until(pe, heads_ready, j + 1, passed)
                n, bank = j * TURNS + 6, par
                for i, (buf, h) in enumerate(((k_sb, 0), (k_sb, 4), (q_sb, 0), (q_sb, 4))):
                    turn(n + i, (bank + i) % 2, [buf[:, h + b, :] for b in range(4)], QK)
                for i, buf in enumerate((dk[par], dq[par], mq[par])):
                    turn(n + 4 + i, (bank + i) % 2, chunks(buf, 0, 4), P)

            pe.wait_ge(made, 2)
            pe.wait_ge(normed, 1)
            turn_h(0, 0)
            pe.wait_ge(t_copied, 2)
            project(0, 0, 0, True)
            pe.wait_ge(w_up, 48)
            with pe.Fori(0, TILES // 2) as g:
                for par in range(2):
                    j = g * 2 + par
                    latents(j, par)
                    turn_h(j * TURNS + 4, par)
                    ups(j, par)
                    until(pe, t_copied, j * TURNS + 6, passed)
                    project(j * MMS + 10, (2 + 2 * par) % 4, 1 - par, False)
                    turn_heads(j, par)
            j = TILES - 1
            latents(j, 0)
            turn_h(j * TURNS + 4, 0)
            ups(j, 0)
            turn_heads(j, 0)

        @block.scalar
        def _(act):
            def copy(n, bank, dst, width, top, guard=None):
                until(act, turned, n + 1, passed)
                if guard is not None and not (isinstance(guard[1], int) and guard[1] <= 0):
                    until(act, guard[0], guard[1], passed)
                act.activation(dst, ps_t[bank][0:top, 0:width], ACT.Copy).then_inc(t_copied, 1)

            def take_root(n):
                until(act, squares, n, passed)
                act.activation(root[:, :], ms[:, :], ACT.Sqrt).then_inc(roots, 1)

            def flat(buf, lo, hi, top):
                return buf[0:top, lo:hi, :].rearrange("p c n -> p (c n)")

            def copy_h(n, bank, par, guard=None):
                copy(n, bank, flat(hT[par], 0, 4, P), 512, P, guard)
                copy(n + 1, 1 - bank, flat(hT[par], 4, 8, P), 512, P)

            def copy_heads(j, par):
                n, w = j * TURNS + 6, j * 16
                for i, (buf, h, name) in enumerate(((kT, 0, "kT"), (kT, 4, "kT"), (qT, 0, "qT"), (qT, 4, "qT"))):
                    copy(n + i, (par + i) % 2, flat(buf, h, h + 4, QK), 512, QK, (t_out[name], w))
                for i, (buf, name) in enumerate(((dkT, "dkT"), (dqT, "dqT"), (mqT, "mqT"))):
                    copy(n + 4 + i, (par + i) % 2, flat(buf, 0, 4, P), 512, P, (t_out[name], w))

            take_root(1)
            copy_h(0, 0, 0)
            take_root(2)

            def step(g, par, follow, guard=True):
                j = g * 2 + par
                copy(j * TURNS + 2, par, cqT[:, :], Q_LORA, P)
                copy(j * TURNS + 3, 1 - par, kvT[:, :], KV_LORA, P)
                copy_h(j * TURNS + 4, par, 1 - par, (h_out[1 - par], (g + par) * 16))
                if follow:
                    take_root(j + 3)
                copy_heads(j, par)

            for par in range(2):
                step(0, par, True)
            with act.Fori(0, TILES // 2 - 1) as g:
                for par in range(2):
                    step(g + 1, par, True)
            step(TILES // 2, 0, False)

        @block.vector
        def _(dve):
            def evacuate(n, bank, dst, width, scale=None):
                until(dve, mm_done, n + 1, passed)
                src = ps_m[bank][:, 0:width]
                if scale is None:
                    dve.tensor_copy(dst, src).then_inc(m_copied, 1)
                else:
                    dve.tensor_scalar(dst, src, scale, None, ALU.mult).then_inc(m_copied, 1)

            def square(col, src, width):
                dve.tensor_tensor_reduce(out=junk[:, 0:width], in0=src, in1=src, scale=1.0 / width, scalar=EPS,
                                         op0=ALU.mult, op1=ALU.add, accum_out=ms[:, col:col + 1])

            def rotate(x, x_out, table, heads):
                half = ROPE // 2
                x1, x2 = x[:, :, 0:half], x[:, :, half:ROPE]
                cos = table[:, 0:half].unsqueeze(1).to_broadcast([P, heads, half])
                sin = table[:, half:ROPE].unsqueeze(1).to_broadcast([P, heads, half])
                for i, (u, w) in enumerate(((x1, cos), (x2, sin), (x2, cos), (x1, sin))):
                    dve.tensor_tensor(rot[:, i, 0:heads, :], u, w, ALU.mult)
                dve.drain()
                dve.tensor_tensor(x_out[:, :, 0:half], rot[:, 0, 0:heads, :], rot[:, 1, 0:heads, :], ALU.subtract)
                dve.tensor_tensor(x_out[:, :, half:ROPE], rot[:, 2, 0:heads, :], rot[:, 3, 0:heads, :], ALU.add)
                dve.drain()

            def norm_x(src):
                dve.scalar_tensor_tensor(out=xn[:, :], in0=src[:, :], scalar=rs[:, 2:3], in1=g_mix[:, :],
                                         op0=ALU.mult, op1=ALU.mult).then_inc(normed, 1)

            def take_z(n, bank, t, par, cs_count, x_count, d_guard, kv_guard):
                evacuate(n, bank, cq[:, :], Q_LORA)
                evacuate(n + 1, (bank + 1) % 4, kv[:, :], KV_LORA + ROPE)
                until(dve, x_in[1 - par], x_count, passed)
                dve.drain()
                square(0, cq[:, :], Q_LORA)
                dve.drain()
                square(1, kv[:, 0:KV_LORA], KV_LORA)
                dve.drain()
                square(2, xt[1 - par][:, :], D)
                dve.drain().then_inc(squares, 1)
                until(dve, cs_in[par], cs_count, passed)
                if kv_guard is not None:
                    until(dve, kv_out, kv_guard, passed)
                rotate(kv[:, KV_LORA:].unsqueeze(1), krr[:, :].unsqueeze(1), cs[par], 1)
                until(dve, roots, t + 2, passed)
                dve.reciprocal(rs[:, :], root[:, :])
                dve.drain()
                dve.scalar_tensor_tensor(out=cqn[:, :], in0=cq[:, :], scalar=rs[:, 0:1], in1=g_q[:, :],
                                         op0=ALU.mult, op1=ALU.mult)
                dve.scalar_tensor_tensor(out=kvn[:, :], in0=kv[:, 0:KV_LORA], scalar=rs[:, 1:2], in1=g_kv[:, :],
                                         op0=ALU.mult, op1=ALU.mult).then_inc(latents_done, 1)
                norm_x(xt[1 - par])
                if d_guard is not None:
                    until(dve, d_out[par], d_guard, passed)
                evacuate(n + 2, (bank + 2) % 4, dq[par][:, :], BR, DIFF_SCALE)
                evacuate(n + 3, (bank + 3) % 4, dk[par][:, :], BR)
                evacuate(n + 4, bank, dv[par][:, :], BR)
                evacuate(n + 5, (bank + 1) % 4, mq[par][:, :], BR, MEM_SCALE)

            def take_heads(j, par, guard):
                n, bank = j * MMS + 6, (2 + 2 * par) % 4
                q_flat = q_sb[:, :, :].rearrange("p h d -> p (h d)")
                evacuate(n, bank, q_flat[:, 0:512], 512, MLA_SCALE)
                evacuate(n + 1, (bank + 1) % 4, q_flat[:, 512:], HEADS * QK - 512, MLA_SCALE)
                until(dve, mm_done, n + 3, passed)
                dve.tensor_copy(k_sb[:, :, 0:NOPE],
                                ps_m[(bank + 2) % 4][:, :].rearrange("p (h d) -> p h d", d=NOPE)).then_inc(m_copied, 1)
                if guard:
                    until(dve, v_out, j * 16, passed)
                evacuate(n + 3, (bank + 3) % 4, v_sb[:, :], BR)
                dve.tensor_copy(k_sb[:, :, NOPE:], krr[:, :].unsqueeze(1).to_broadcast([P, HEADS, ROPE]))
                dve.drain()
                rotate(q_sb[:, :, NOPE:], q_sb[:, :, NOPE:], cs[par], HEADS)
                dve.sem_inc(roped, 1)
                dve.sem_inc(heads_ready, 1)

            dve.memset(ms[:, :], 1.0)
            dve.memset(junk[:, :], 0.0)
            dve.drain()
            dve.wait_ge(gains, 48)
            dve.wait_ge(x_in[0], 16)
            square(2, xt[0][:, :], D)
            dve.drain().then_inc(squares, 1)
            dve.wait_ge(roots, 1)
            dve.reciprocal(rs[:, :], root[:, :])
            dve.drain()
            norm_x(xt[0])
            take_z(0, 0, 0, 0, 16, 16, None, None)

            def step(g, par, first):
                j = g * 2 + par
                take_heads(j, par, not (first and par == 0))
                take_z(j * MMS + 10, (2 + 2 * par) % 4, j + 1, 1 - par, (g + par) * 16 + 16, (g * 16) + 32,
                       None if first and par == 0 else (g + par) * 32, j * 32 + 32)

            for par in range(2):
                step(0, par, True)
            with dve.Fori(0, TILES // 2 - 1) as g:
                for par in range(2):
                    step(g + 1, par, False)
            take_heads(TILES - 1, 0, True)


def cached_and_memory_keys(nc, a, s):
    with ExitStack() as ctx:
        sb, psum, sem = tools(nc, ctx, "B")
        ident = sb("ident", [P, P])
        w_uk, w_uv = sb("w_uk", [P, KV_LORA // P, BR]), sb("w_uv", [P, KV_LORA // P, BR])
        w_kv = sb("w_kv", [P, DC, 2 * BR])
        g_mem = sb("g_mem", [P, D])
        cmk = sb("cmk", [P, 2, BR])
        cdk, ckv, ckr = sb("cdk", [P, BR]), sb("ckv", [P, KV_LORA]), sb("ckr", [P, ROPE])
        sub = sb("sub", [P, 2 * HEADS, P])
        mem, mn = sb("mem", [P, 2, D]), sb("mn", [P, 2, D])
        ms, root, rs = sb("ms", [P, 2]), sb("root", [P, 2]), sb("rs", [P, 2])
        memT = sb("memT", [P, 2, DC, P])
        ckvT = sb("ckvT", [P, KV_LORA])
        cmkT, mkT = sb("cmkT", [P, MEM_HEADS, MEM]), sb("mkT", [P, MEM_HEADS, MEM])
        cdkT, subT = sb("cdkT", [P, 4, P]), sb("subT", [P, 2 * HEADS, P])
        k_sb, v_sb, kT = sb("k_sb", [P, HEADS, QK]), sb("v_sb", [P, BR]), sb("kT", [P, HEADS, P])
        mk, mv = sb("mk", [P, 2, BR]), sb("mv", [P, 2, BR])
        ps_t = [psum(f"turn{i}", [P, 512]) for i in range(2)]
        ps_m = [psum(f"mm{i}", [P, 512]) for i in range(4)]
        made = sem("identity")
        small_in, mem_in, w_in_sem, sub_in = sem("small_in"), sem("mem_in"), sem("w_in"), sem("sub_in")
        squares, roots, normed = sem("squares"), sem("roots"), sem("normed")
        turned, t_copied, mm_done, m_copied = sem("turned"), sem("t_copied"), sem("mm_done"), sem("m_copied")
        keys_ready, stored = sem("keys_ready"), sem("stored")
        block = ctx.enter_context(nc.Block())

        @block.gpsimd
        def _(pool):
            make_identity(pool, ident, made)

        @block.sync
        def _(sp):
            two = "(m p) n -> p m n"
            sp.dma_start(cmk[:, :, :], a["cache_mem_k"].rearrange(two, p=P)).then_inc(small_in, 16)
            sp.dma_start(cdk[:, :], a["cache_diff_k"]).then_inc(small_in, 16)
            sp.dma_start(ckv[:, :], a["cache_mla_ckv"]).then_inc(small_in, 16)
            sp.dma_start(ckr[:, :], a["cache_mla_krope"]).then_inc(small_in, 16)
            sp.dma_start(w_uk[:, :, :], a["w_uk"].rearrange("(c p) n -> p c n", p=P)).then_inc(small_in, 16)
            sp.dma_start(w_uv[:, :, :], a["w_uv"].rearrange("(c p) n -> p c n", p=P)).then_inc(small_in, 16)
            sp.dma_start(mem[:, :, :], a["mem_prompt"].rearrange(two, p=P)).then_inc(mem_in, 16)
            sp.dma_start(g_mem[:, :], a["norm_mem"].to_broadcast([P, D])).then_inc(mem_in, 16)
            sp.dma_start(sub[:, :, :], a["peer_subkeys"].rearrange("(b n) d -> n b d", n=P)).then_inc(sub_in, 16)
            sp.dma_start(w_kv[:, :, :], a["w_mem_kv"].rearrange("(c p) n -> p c n", p=P)).then_inc(w_in_sem, 16)
            cache = slice(CACHE, CACHE + PAST)
            sp.wait_ge(t_copied, 3)
            sp.dma_start(s["mkT"][1].rearrange("h p n -> p h n"), cmkT[:, :, :]).then_inc(stored, 16)
            sp.dma_start(s["dkT"].rearrange("c p n -> p c n")[:, :, cache], cdkT[:, :, :]).then_inc(stored, 16)
            sp.wait_ge(m_copied, 2)
            sp.dma_start(s["vm"][cache, :], v_sb[:, :]).then_inc(stored, 16)
            sp.wait_ge(t_copied, 14)
            sp.dma_start(s["kT"].rearrange("c p n -> p c n")[:, :, cache], kT[0:QK, :, :]).then_inc(stored, 16)
            sp.wait_ge(m_copied, 6)
            sp.dma_start(s["mk"].rearrange(two, p=P), mk[:, :, :]).then_inc(stored, 16)
            sp.dma_start(s["mv"].rearrange(two, p=P), mv[:, :, :]).then_inc(stored, 16)
            sp.wait_ge(t_copied, 16)
            sp.dma_start(s["mkT"][0].rearrange("h p n -> p h n"), mkT[:, :, :]).then_inc(stored, 16)
            sp.dma_start(s["skT"].rearrange("b d n -> d b n"), subT[:, :, :]).then_inc(stored, 16)
            sp.wait_ge(stored, 16 * 8)

        @block.tensor
        def _(pe):
            count = {"turn": 0, "mm": 0}

            def turn(blocks, top=P):
                n = count["turn"]
                if n >= 2:
                    pe.wait_ge(t_copied, n - 1)
                for b, src in enumerate(blocks):
                    last = pe.transpose(ps_t[n % 2][0:top, b * P:(b + 1) * P], src, ident[:, :])
                last.then_inc(turned, 1)
                count["turn"] += 1

            def product(lhs, w, lo):
                n = count["mm"]
                if n >= 4:
                    pe.wait_ge(m_copied, n - 3)
                for c in range(len(lhs)):
                    last = pe.matmul(ps_m[n % 4][:, :], lhs[c], w[:, c, lo:lo + BR], start=(c == 0),
                                     stop=(c == len(lhs) - 1))
                last.then_inc(mm_done, 1)
                count["mm"] += 1

            pe.wait_ge(made, 2)
            pe.wait_ge(small_in, 96)
            for m in range(2):
                turn([cmk[:, m, h * P:(h + 1) * P] for h in range(4)])
            turn([cdk[:, h * P:(h + 1) * P] for h in range(4)])
            turn([ckv[:, c * P:(c + 1) * P] for c in range(2)])
            pe.wait_ge(sub_in, 16)
            for i in range(4):
                turn([sub[:, 4 * i + b, :] for b in range(4)])
            latent = [ckvT[:, c * P:(c + 1) * P] for c in range(2)]
            product(latent, w_uk, 0)
            product(latent, w_uv, 0)
            pe.wait_ge(normed, 2)
            for m in range(2):
                for i in range(2):
                    turn([mn[:, m, (4 * i + b) * P:(4 * i + b + 1) * P] for b in range(4)])
            pe.wait_ge(keys_ready, 1)
            for i in range(2):
                turn([k_sb[:, 4 * i + b, :] for b in range(4)], QK)
            pe.wait_ge(w_in_sem, 16)
            for m in range(2):
                pe.wait_ge(t_copied, 10 + 2 * m)
                for i in range(2):
                    product([memT[:, m, c, :] for c in range(DC)], w_kv, i * BR)
            for m in range(2):
                pe.wait_ge(m_copied, 3 + 2 * m)
                turn([mk[:, m, h * P:(h + 1) * P] for h in range(4)])

        @block.scalar
        def _(act):
            act.wait_ge(squares, 1)
            act.activation(root[:, :], ms[:, :], ACT.Sqrt).then_inc(roots, 1)
            count = [0]

            def copy(dst, width, top=P):
                n = count[0]
                act.wait_ge(turned, n + 1)
                src = ps_t[n % 2][0:top, 0:width]
                if len(dst.shape) == 3:
                    src = src.rearrange("p (c n) -> p c n", n=P)
                act.activation(dst, src, ACT.Copy).then_inc(t_copied, 1)
                count[0] += 1

            for m in range(2):
                copy(cmkT[:, :, m * P:(m + 1) * P], 512)
            copy(cdkT[:, :, :], 512)
            copy(ckvT[:, :], KV_LORA)
            for i in range(4):
                copy(subT[:, 4 * i:4 * i + 4, :], 512)
            for m in range(2):
                for i in range(2):
                    copy(memT[:, m, 4 * i:4 * i + 4, :], 512)
            for i in range(2):
                copy(kT[0:QK, 4 * i:4 * i + 4, :], 512, QK)
            for m in range(2):
                copy(mkT[:, :, m * P:(m + 1) * P], 512)

        @block.vector
        def _(dve):
            dve.wait_ge(mem_in, 32)
            for m in range(2):
                dve.tensor_tensor_reduce(out=mn[:, m, :], in0=mem[:, m, :], in1=mem[:, m, :], scale=1.0 / D, scalar=EPS,
                                         op0=ALU.mult, op1=ALU.add, accum_out=ms[:, m:m + 1])
            dve.drain().then_inc(squares, 1)
            dve.wait_ge(roots, 1)
            dve.reciprocal(rs[:, :], root[:, :])
            dve.drain()
            for m in range(2):
                dve.scalar_tensor_tensor(out=mn[:, m, :], in0=mem[:, m, :], scalar=rs[:, m:m + 1], in1=g_mem[:, :],
                                         op0=ALU.mult, op1=ALU.mult).then_inc(normed, 1)
            dve.wait_ge(mm_done, 1)
            dve.tensor_copy(k_sb[:, :, 0:NOPE], ps_m[0][:, :].rearrange("p (h d) -> p h d", d=NOPE)).then_inc(m_copied, 1)
            dve.wait_ge(small_in, 96)
            dve.tensor_copy(k_sb[:, :, NOPE:], ckr[:, :].unsqueeze(1).to_broadcast([P, HEADS, ROPE]))
            dve.drain().then_inc(keys_ready, 1)
            for n, dst in enumerate((v_sb[:, :], mk[:, 0, :], mv[:, 0, :], mk[:, 1, :], mv[:, 1, :])):
                dve.wait_ge(mm_done, n + 2)
                dve.tensor_copy(dst, ps_m[(n + 1) % 4][:, :]).then_inc(m_copied, 1)


KEY_TILES = SEQ // P
SAMPLE_KEYS = PAST + DEC
LAM_INIT = 0.8 - 0.6
PAIRS = HEADS // 2
ALIBI_STEP = 2.0 ** (-8.0 * 2 / HEADS)


class Span:

    def __init__(self, tiles, groups):
        self.tiles = tiles
        self.lo = tiles[0] * P
        self.hi = min(TOK, (tiles[-1] + 1) * P)
        self.n = self.hi - self.lo
        self.groups = groups
        self.width = self.n // groups
        self.sample = self.hi == TOK
        self.keys = SEQ if self.sample else self.hi
        self.rows = [min(P, TOK - t * P) for t in tiles]


SPANS = [Span(list(range(lo, hi)), 1) for lo, hi in ((0, 2), (2, 5), (5, TILES))]


def attention_jobs(span, blocks):
    jobs, slot, group = [], 0, 0
    for kind, heads in (("mla", 2), ("diff", 2), ("mem", 1)):
        for u in range(heads):
            for t in span.tiles:
                keys = MEM if kind == "mem" else (t + 1) * P if t < KEY_TILES else SAMPLE_KEYS
                jobs.append((kind, u, t, keys, slot, group))
                slot += 2 if kind == "diff" else 1
                group += -(-keys // (blocks * P))
    return jobs, slot, group


def attention(nc, a, s, span, tag, ex=None, tiles=None):
    BLOCKS = 4
    BANKS = 1 if ex else 2
    jobs, SLOTS, GROUPS = attention_jobs(span, BLOCKS)
    JOBS = len(jobs)
    NT = len(span.tiles)
    O_GROUPS = -(-NT // BLOCKS)
    TURNS = GROUPS + 3 * O_GROUPS
    MIXES = 2 * NT
    LAST = {k: max(i for i, j in enumerate(jobs) if j[0] == k) for k in ("mla", "diff", "mem")}
    WIDTH = {"mla": VD, "diff": VD, "mem": MDH}

    def done(g, per, n):
        return g * per + (per + n + 1)

    with ExitStack() as ctx:
        sb, psum, sem = tools(nc, ctx, tag)
        ident = sb("ident", [P, P])
        MEMS = 1 + span.sample
        KW = span.keys + (SAMPLE_KEYS if span.sample else 0)
        VT = span.keys // P + (2 if span.sample else 0)
        bias = [sb(f"bias{u}", [P, D]) for u in range(2)]
        q_mla = [sb(f"q_mla{u}", [P, NT * P]) for u in range(2)]
        k_mla = [sb(f"k_mla{u}", [P, KW]) for u in range(2)]
        v_mla = sb("v_mla", [P, VT, P])
        q_diff, k_diff = sb("q_diff", [P, NT * P]), sb("k_diff", [P, KW])
        v_diff = sb("v_diff", [P, VT, P])
        q_mem, k_mem, v_mem = sb("q_mem", [P, NT * P]), sb("k_mem", [P, 2, MEM]), sb("v_mem", [P, 2, 2, P])
        shifted_s = [sb(f"shifted{i}", [P, D]) for i in range(2)]
        probs = [sb(f"probs{i}", [P, D]) for i in range(2)]
        pT = [sb(f"pT{i}", [P, D]) for i in range(2)]
        o = {k: sb(f"o_{k}", [P, NT, P]) for k in ("mla", "diff", "mem")}
        o_sq = sb("o_sq", [P, NT * 2, VD])
        oT = {k: sb(f"oT_{k}", [P, NT, P]) for k in ("mla", "diff", "mem")}
        o_ms, o_root, o_rs = (sb(n, [P, 2 * NT]) for n in ("o_ms", "o_root", "o_rs"))
        top = sb("top", [P, 8])
        ntop = sb("ntop", [P, 8])
        sums = sb("sums", [P, 8])
        inv, coef = sb("inv", [P, 8]), sb("coef", [P, 8])
        lam_in = sb("lam_in", [P, 4, DDH])
        lam_junk, lam_sum, lam_exp = sb("lam_junk", [P, 2, DDH]), sb("lam_sum", [P, 2]), sb("lam_exp", [P, 2])
        neg_lam = sb("neg_lam", [P, 1])
        subln, g_o = sb("subln", [P, VD]), sb("g_o", [P, VD])
        ps_s = [psum(f"scores{i}", [P, D]) for i in range(2)]
        ps_t = [psum(f"turn{i}", [P, 512]) for i in range(BANKS)]
        ps_o = [psum(f"o{i}", [P, 512]) for i in range(BANKS)]
        steps, dist = shifted_s[0][:, :].bitcast(I32), probs[0]

        K_IN = 48 if span.sample else 16
        made, passed = sem("identity"), sem("loop_waits")
        iota_done, dist_done, small_in, lam_summed, lam_exped = (sem(n) for n in (
            "iota_done", "dist_done", "small_in", "lam_summed", "lam_exped"))
        in_mla = [sem(f"in_mla{u}") for u in range(2)]
        in_vmla, in_diff, in_mem = sem("in_vmla"), sem("in_diff"), sem("in_mem")
        scored, maxed, shifted, exped = sem("scored"), sem("maxed"), sem("shifted"), sem("exped")
        mixed, turned, t_copied = sem("mixed"), sem("turned"), sem("t_copied")
        pv_done, o_taken = sem("pv_done"), sem("o_taken")
        o_squares, o_roots, o_normed, oT_out = sem("o_squares"), sem("o_roots"), sem("o_normed"), sem("oT_out")

        def loop(eng, body):
            if not ex:
                with eng.Fori(0, PAIRS) as g:
                    body(g, None, None)
            elif len(tiles) == 1:
                per = HEADS // PAIRS
                for g in range(PAIRS):
                    body(g, tiles[0], range(g * per, (g + 1) * per))
            else:
                per = HEADS // 2
                with eng.Fori(0, PAIRS // 2) as t:
                    for half in range(2):
                        body(t * 2 + half, t + tiles[0], range(half * per, (half + 1) * per))

        def experts_beside(kind, eng, tile, heads, i, share=None):
            beside(ex, kind, eng, tile, heads, i, JOBS, share)

        block = ctx.enter_context(nc.Block())

        @block.sync
        def _(sp):
            for i, name in enumerate(("diff_lq1", "diff_lk1", "diff_lq2", "diff_lk2")):
                sp.dma_start(lam_in[:, i, :], a[name].to_broadcast([P, DDH])).then_inc(small_in, 16)
            sp.dma_start(subln[:, :], a["diff_subln"].to_broadcast([P, VD])).then_inc(small_in, 16)

            def tiles(src):
                return src.rearrange("(t p) n -> p t n", p=P)

            def load_keys(buf, top_row, src, c, signal):
                view = src.rearrange("c p n -> p c n")[:, bass.ds(c, 1), :]
                parts = [(0, 0, span.keys)] + [(SEQ, CACHE, PAST), (SEQ + PAST, SEQ, DEC)] * span.sample
                for lo, src_lo, n in parts:
                    sp.dma_start(buf[0:top_row, lo:lo + n].unsqueeze(1), view[:, :, src_lo:src_lo + n]).then_inc(signal, 16)

            def load_values(buf, rows, cache, g, signal):
                cols = bass.ds(g * P, P)
                sp.dma_start(buf[:, 0:span.keys // P, :], tiles(rows[0:span.keys, :])[:, :, cols]).then_inc(signal, 16)
                if span.sample:
                    sp.dma_start(buf[:, KEY_TILES, :], cache[:, cols]).then_inc(signal, 16)
                    sp.dma_start(buf[0:DEC, KEY_TILES + 1, :], rows[SEQ:TOK, cols]).then_inc(signal, 16)

            q_cols = slice(span.lo, span.lo + NT * P)

            def loads(g, tile, heads):
                for u in range(2):
                    last = max(j[4] for j in jobs if j[0] == "mla" and j[1] == u)
                    until(sp, scored, done(g, SLOTS, last - SLOTS), passed)
                    view = s["qT"].rearrange("c p n -> p c n")[:, bass.ds(g * 2 + u, 1), q_cols]
                    sp.dma_start(q_mla[u][0:QK, :].unsqueeze(1), view).then_inc(in_mla[u], 16)
                    load_keys(k_mla[u], QK, s["kT"], g * 2 + u, in_mla[u])
                until(sp, pv_done, done(g, JOBS, LAST["mla"] - JOBS), passed)
                load_values(v_mla, s["vm"], s["vm"][CACHE:CACHE + PAST, :], g, in_vmla)
                until(sp, pv_done, done(g, JOBS, LAST["diff"] - JOBS), passed)
                sp.dma_start(q_diff[:, :].unsqueeze(1), s["dqT"].rearrange("c p n -> p c n")[:, bass.ds(g, 1), q_cols]).then_inc(in_diff, 16)
                load_keys(k_diff, P, s["dkT"], g, in_diff)
                load_values(v_diff, s["dv"], a["cache_diff_v"], g, in_diff)
                until(sp, pv_done, done(g, JOBS, LAST["mem"] - JOBS), passed)
                sp.dma_start(q_mem[:, :].unsqueeze(1), s["mqT"].rearrange("c p n -> p c n")[:, bass.ds(g, 1), q_cols]).then_inc(in_mem, 16)
                for m, v in enumerate((s["mv"], a["cache_mem_v"])[0:MEMS]):
                    sp.dma_start(k_mem[:, m, :].unsqueeze(1), s["mkT"][m].rearrange("h p n -> p h n")[:, bass.ds(g, 1), :]).then_inc(in_mem, 16)
                    sp.dma_start(v_mem[:, m, :, :], tiles(v)[:, :, bass.ds(g * P, P)]).then_inc(in_mem, 16)

            loop(sp, loads)

        @block.gpsimd
        def _(pool):
            make_identity(pool, ident, made)
            pool.iota(steps, pattern=[[1, D]], base=P - D, channel_multiplier=-1).then_inc(iota_done, 1)
            if ex:
                if tiles[0] == 0:
                    ex.pool_start(pool)
                if len(tiles) == 1:
                    ex.pool_tile(pool, tiles[0], range(HEADS))
                else:
                    with pool.Fori(0, len(tiles)) as t:
                        ex.pool_tile(pool, t + tiles[0], range(HEADS))

        @block.tensor
        def _(pe):
            def free_slot(g, k):
                if k < 2:
                    until(pe, exped, done(g, SLOTS, -1), passed)
                elif 2 * NT <= k - 2 < 6 * NT:
                    until(pe, shifted, done(g, 2 * MIXES, k - 2 - 2 * NT), passed)
                else:
                    until(pe, exped, done(g, SLOTS, k - 2), passed)

            def scores(g, i):
                kind, u, t, keys, slot, _ = jobs[i]
                if t == span.tiles[0]:
                    per, signal = {"mla": (16 + K_IN, in_mla[u]), "diff": (16 + K_IN + K_IN, in_diff),
                                   "mem": (16 + 32 * MEMS, in_mem)}[kind]
                    until(pe, signal, g * per + per, passed)
                q = slice(t * P - span.lo, (t + 1) * P - span.lo)
                lo = 0 if t < KEY_TILES else SEQ
                for m in range(2 if kind == "diff" else 1):
                    free_slot(g, slot + m)
                    out = ps_s[(slot + m) % 2]
                    for c in range(0, keys, 512):
                        n = min(512, keys - c)
                        if kind == "mla":
                            lhs, rhs = q_mla[u][0:QK, q], k_mla[u][0:QK, lo + c:lo + c + n]
                        elif kind == "diff":
                            part = slice(DDH * (2 * u + m), DDH * (2 * u + m + 1))
                            lhs, rhs = q_diff[part, q], k_diff[part, lo + c:lo + c + n]
                        else:
                            lhs, rhs = q_mem[:, q], k_mem[:, int(t == TILES - 1), :]
                        last = pe.matmul(out[:, c:c + n], lhs, rhs, start=True, stop=True)
                    last.then_inc(scored, 1)

            def bank_free(g, n):
                until(pe, t_copied, done(g, TURNS, n - BANKS if n >= BANKS else -1), passed)

            def turn(g, i):
                kind, u, t, keys, slot, group = jobs[i]
                if kind == "diff":
                    until(pe, mixed, done(g, MIXES, i - 2 * NT), passed)
                else:
                    until(pe, exped, done(g, SLOTS, slot), passed)
                for n, c in enumerate(range(0, keys, BLOCKS * P)):
                    bank_free(g, group + n)
                    for b in range(c, min(keys, c + BLOCKS * P), P):
                        w = min(P, keys - b)
                        last = pe.transpose(ps_t[(group + n) % BANKS][0:w, b - c:b - c + P], probs[slot % 2][:, b:b + w], ident[:, :])
                    last.then_inc(turned, 1)

            def weigh(g, i):
                kind, u, t, keys, _, group = jobs[i]
                if kind == "mla" and i == 0:
                    until(pe, in_vmla, g * K_IN + K_IN, passed)
                until(pe, t_copied, done(g, TURNS, group + (keys - 1) // (BLOCKS * P)), passed)
                until(pe, o_taken, done(g, JOBS, i - BANKS if i >= BANKS else -1), passed)
                blocks = -(-keys // P)
                for b in range(blocks):
                    w = min(P, keys - b * P)
                    if kind == "mem":
                        v = v_mem[:, int(t == TILES - 1), b, :]
                    else:
                        tile = b if t < KEY_TILES else KEY_TILES + b
                        v = (v_mla if kind == "mla" else v_diff)[0:w, tile, VD * u:VD * (u + 1)]
                    last = pe.matmul(ps_o[i % BANKS][:, 0:WIDTH[kind]], pT[i % 2][0:w, b * P:(b + 1) * P], v,
                                     start=(b == 0), stop=(b == blocks - 1))
                last.then_inc(pv_done, 1)

            def turn_o(g):
                for n, kind in enumerate(("mla", "diff", "mem")):
                    if kind == "diff":
                        until(pe, o_normed, g + 2, passed)
                    else:
                        until(pe, o_taken, done(g, JOBS, LAST[kind]), passed)
                    for c in range(O_GROUPS):
                        group = GROUPS + O_GROUPS * n + c
                        bank_free(g, group)
                        for b in range(BLOCKS * c, min(BLOCKS * c + BLOCKS, NT)):
                            last = pe.transpose(ps_t[group % BANKS][:, (b - BLOCKS * c) * P:(b - BLOCKS * c + 1) * P], o[kind][:, b, :], ident[:, :])
                        last.then_inc(turned, 1)

            pe.wait_ge(made, 2)
            pe.sem_inc(scored, SLOTS)
            pe.sem_inc(turned, TURNS)
            pe.sem_inc(pv_done, JOBS)
            if ex and tiles[0] == 0:
                ex.pe_start(pe)

            def pair(g, tile, heads):
                scores(g, 0)
                for i in range(JOBS):
                    if i + 1 < JOBS:
                        scores(g, i + 1)
                    experts_beside("pe", pe, tile, heads, i, 0)
                    turn(g, i)
                    experts_beside("pe", pe, tile, heads, i, 1)
                    if i >= 1:
                        weigh(g, i - 1)
                weigh(g, JOBS - 1)
                turn_o(g)

            loop(pe, pair)

        @block.scalar
        def _(act):
            def exp(g, i):
                kind, _, _, keys, slot, _ = jobs[i]
                until(act, maxed, done(g, JOBS, i), passed)
                for m in range(2 if kind == "diff" else 1):
                    col = 2 * (i % 4) + m
                    src = shifted_s[m] if kind == "diff" else ps_s[slot % 2]
                    act.activation(probs[(slot + m) % 2][:, 0:keys], src[:, 0:keys], ACT.Exp, bias=ntop[:, col:col + 1],
                                   accum_out=sums[:, col:col + 1]).then_inc(exped, 1)

            def copy(g, i):
                _, _, _, keys, _, group = jobs[i]
                until(act, pv_done, done(g, JOBS, i - 2 if i >= 2 else -1), passed)
                for n, c in enumerate(range(0, keys, BLOCKS * P)):
                    until(act, turned, done(g, TURNS, group + n), passed)
                    full = min(keys, c + BLOCKS * P) // P * P - c
                    bank = ps_t[(group + n) % BANKS]
                    if full:
                        last = act.activation(pT[i % 2][:, c:c + full], bank[:, 0:full], ACT.Copy)
                    if (keys - c) % P and keys - c < BLOCKS * P:
                        w = (keys - c) % P
                        last = act.activation(pT[i % 2][0:w, c + full:c + full + P], bank[0:w, full:full + P], ACT.Copy)
                    last.then_inc(t_copied, 1)

            act.wait_ge(iota_done, 1)
            act.activation(dist[:, :], steps, ACT.Abs).then_inc(dist_done, 1)
            act.wait_ge(lam_summed, 1)
            act.activation(lam_exp[:, :], lam_sum[:, :], ACT.Exp).then_inc(lam_exped, 1)
            act.sem_inc(exped, SLOTS)
            act.sem_inc(t_copied, TURNS)
            act.sem_inc(o_roots, 1)
            act.sem_inc(oT_out, 48)
            if ex and tiles[0] == 0:
                ex.act_start(act)

            def pair(g, tile, heads):
                exp(g, 0)
                for i in range(JOBS):
                    experts_beside("act_diag", act, tile, heads, i)
                    copy(g, i)
                    if i + 1 < JOBS:
                        exp(g, i + 1)
                    if i == LAST["diff"] + 2:
                        until(act, o_squares, g + 2, passed)
                        act.activation(o_root[:, :], o_ms[:, :], ACT.Sqrt).then_inc(o_roots, 1)
                    experts_beside("act_rest", act, tile, heads, i)
                until(act, oT_out, g * 48 + 48, passed)
                for n, kind in enumerate(("mla", "diff", "mem")):
                    for c in range(O_GROUPS):
                        group = GROUPS + O_GROUPS * n + c
                        until(act, turned, done(g, TURNS, group), passed)
                        k = min(BLOCKS, NT - BLOCKS * c)
                        act.activation(oT[kind][:, BLOCKS * c:BLOCKS * c + k, :].rearrange("p t n -> p (t n)"),
                                       ps_t[group % BANKS][:, 0:k * P], ACT.Copy).then_inc(t_copied, 1)
                    until(act, t_copied, done(g, TURNS, group), passed)
                    view = s["oT"].rearrange("c p n -> p c n")[:, bass.ds(g + PAIRS * n, 1), span.lo:span.lo + NT * P]
                    act.dma_start(view, oT[kind][:, :, :].rearrange("p t n -> p (t n)").unsqueeze(1)).then_inc(oT_out, 16)

            loop(act, pair)
            act.wait_ge(oT_out, 48 * (PAIRS + 1))

        @block.vector
        def _(dve):
            def maximum(g, i):
                kind, u, t, keys, slot, _ = jobs[i]
                col = 2 * (i % 4)
                until(dve, scored, done(g, SLOTS, slot), passed)
                if kind == "diff":
                    for m in range(2):
                        if m:
                            until(dve, scored, done(g, SLOTS, slot + 1), passed)
                        lo = D - P - t * P if t < KEY_TILES else D - P - PAST
                        dve.tensor_tensor_reduce(out=shifted_s[m][:, 0:keys], in0=ps_s[m][:, 0:keys],
                                                 in1=bias[u][:, lo:lo + keys], scale=1.0, scalar=-3.0e38,
                                                 op0=ALU.add, op1=ALU.max, accum_out=top[:, col + m:col + m + 1]).then_inc(shifted, 1)
                    dve.drain()
                    dve.tensor_scalar(ntop[:, col:col + 2], top[:, col:col + 2], -1.0, None, ALU.mult).then_inc(maxed, 1)
                    return
                if kind == "mla" and t < KEY_TILES:
                    dve.memset(ps_s[slot % 2][0:CHUNK, keys - CHUNK:keys], -1e30)
                    dve.drain()
                dve.tensor_reduce(ntop[:, col:col + 1], ps_s[slot % 2][:, 0:keys], AX, ALU.max, negate=True).then_inc(maxed, 1)

            def mix(g, i):
                col, slot = 2 * (i % 4), jobs[i][4]
                until(dve, exped, done(g, SLOTS, slot + 1), passed)
                dve.reciprocal(inv[:, col:col + 2], sums[:, col:col + 2])
                dve.drain()
                dve.tensor_scalar(coef[:, col:col + 1], inv[:, col + 1:col + 2], sums[:, col:col + 1], neg_lam[:, 0:1], ALU.mult, ALU.mult)
                dve.drain()
                keys = jobs[i][3]
                dve.scalar_tensor_tensor(out=probs[0][:, 0:keys], in0=probs[1][:, 0:keys], scalar=coef[:, col:col + 1],
                                         in1=probs[0][:, 0:keys], op0=ALU.mult, op1=ALU.add).then_inc(mixed, 1)

            def take_o(g, i):
                kind, u, t, _, _, _ = jobs[i]
                col = 2 * (i % 4)
                until(dve, pv_done, done(g, JOBS, i), passed)
                if kind != "diff":
                    dve.reciprocal(inv[:, col:col + 1], sums[:, col:col + 1])
                    dve.drain()
                lo = 0 if kind == "mem" else VD * u
                dve.tensor_scalar(o[kind][:, t - span.tiles[0], lo:lo + WIDTH[kind]], ps_o[i % BANKS][:, 0:WIDTH[kind]],
                                  inv[:, col:col + 1], None, ALU.mult).then_inc(o_taken, 1)

            heads_view = o["diff"][:, :, :].rearrange("p t (u v) -> p (t u) v", v=VD)

            def square_o():
                dve.drain()
                dve.tensor_tensor(o_sq[:, :, :], heads_view, heads_view, ALU.mult)
                dve.drain()
                dve.tensor_reduce(o_rs[:, :], o_sq[:, :, :], AX, ALU.add)
                dve.drain()
                dve.tensor_scalar(o_ms[:, :], o_rs[:, :], 1.0 / VD, EPS, ALU.mult, ALU.add).then_inc(o_squares, 1)

            def norm_o(g):
                until(dve, o_roots, g + 2, passed)
                dve.reciprocal(o_rs[:, :], o_root[:, :])
                dve.drain()
                n = 2 * NT
                dve.tensor_tensor(o_sq[:, :, :], heads_view, o_rs[:, :].unsqueeze(2).to_broadcast([P, n, VD]), ALU.mult)
                dve.drain()
                dve.tensor_tensor(heads_view, o_sq[:, :, :], g_o[:, :].unsqueeze(1).to_broadcast([P, n, VD]), ALU.mult).then_inc(o_normed, 1)

            dve.wait_ge(small_in, 80)
            for i in range(2):
                dve.tensor_tensor_reduce(out=lam_junk[:, i, :], in0=lam_in[:, 2 * i, :], in1=lam_in[:, 2 * i + 1, :], scale=1.0,
                                         scalar=0.0, op0=ALU.mult, op1=ALU.add, accum_out=lam_sum[:, i:i + 1])
            dve.drain().then_inc(lam_summed, 1)
            dve.tensor_scalar(g_o[:, :], subln[:, :], 1.0 - LAM_INIT, None, ALU.mult)
            dve.wait_ge(lam_exped, 1)
            dve.tensor_scalar(neg_lam[:, :], lam_exp[:, 1:2], lam_exp[:, 0:1], -LAM_INIT, ALU.subtract, ALU.add)
            dve.wait_ge(dist_done, 1)
            dve.memset(dist[0:CHUNK, D - CHUNK:D], 1e36)
            dve.drain()
            for u in range(2):
                dve.tensor_scalar(bias[u][:, :], dist[:, :], -(2.0 ** (-8.0 * (u + 1) / HEADS)), None, ALU.mult)
            dve.drain()
            dve.sem_inc(shifted, 2 * MIXES)
            dve.sem_inc(maxed, JOBS)
            dve.sem_inc(mixed, MIXES)
            dve.sem_inc(o_taken, JOBS)
            dve.sem_inc(o_squares, 1)
            dve.sem_inc(o_normed, 1)
            if ex and tiles[0] == 0:
                ex.dve_start(dve)

            def pair(g, tile, heads):
                maximum(g, 0)
                for i in range(JOBS):
                    if jobs[i][0] == "diff":
                        mix(g, i)
                    if i >= 2:
                        take_o(g, i - 2)
                    experts_beside("dve", dve, tile, heads, i, 0)
                    if i + 1 < JOBS:
                        maximum(g, i + 1)
                    if i == LAST["diff"] + 2:
                        square_o()
                        for u in range(2):
                            dve.tensor_scalar(bias[u][:, :], bias[u][:, :], ALIBI_STEP, None, ALU.mult)
                    if i == LAST["diff"] + 3:
                        norm_o(g)
                    experts_beside("dve", dve, tile, heads, i, 1)
                take_o(g, JOBS - 2)
                take_o(g, JOBS - 1)
                if LAST["diff"] + 3 >= JOBS:
                    norm_o(g)

            loop(dve, pair)


BRANCHES = 3
QUERY = 2 * P


def merge_branches(nc, a, s, mergedT, span, tag, ex=None, tile=None, heads=None):
    GROUP = span.n
    UNITS = 2 * BRANCHES
    n_iter = DC // 2

    def done(g, n):
        return g * UNITS + (UNITS + n + 1)

    with ExitStack() as ctx:
        sb, psum, sem = tools(nc, ctx, tag)
        hT, oT = sb("hT", [P, DC, span.n]), sb("oT", [P, BRANCHES * 4, span.n])
        w_gate = [sb(f"w_gate{b}", [P, DC, 2 * P]) for b in range(BRANCHES)]
        w_br = [sb(f"w_br{b}", [P, 4, 2 * P]) for b in range(BRANCHES)]
        b_gate = sb("b_gate", [P, BRANCHES, DC])
        gate = [sb(f"gate{i}", [P, GROUP]) for i in range(2)]
        part, acc = sb("part", [P, GROUP]), [sb(f"acc{i}", [P, GROUP]) for i in range(2)]
        ps_g = [psum(f"gates{i}", [P, 512]) for i in range(2)]
        ps_b = [psum(f"branch{i}", [P, 512]) for i in range(2)]
        passed = sem("loop_waits")
        h_in, o_in, b_in = sem("h_in"), sem("o_in"), sem("b_in")
        w_ready = [sem(f"w_ready{b}") for b in range(BRANCHES)]
        projected, opened, gated = sem("projected"), sem("opened"), sem("gated")
        block = ctx.enter_context(nc.Block())

        def loop(eng, body):
            if ex:
                for g in range(n_iter):
                    body(g)
            else:
                with eng.Fori(0, n_iter) as g:
                    body(g)

        def experts_beside(kind, eng, g, n):
            beside(ex, kind, eng, tile, heads, g * UNITS + n, n_iter * UNITS)

        @block.sync
        def _(sp):
            def loads(g):
                cols = bass.ds(g * (2 * P), 2 * P)
                for b, name in enumerate(("w_br_a", "w_br_b", "w_br_m")):
                    until(sp, projected, done(g, 2 * b + 1 - UNITS), passed)
                    w = a["w_gate"][:, b * D:(b + 1) * D].rearrange("(c p) n -> p c n", p=P)
                    sp.dma_start(w_gate[b][:, :, :], w[:, :, cols]).then_inc(w_ready[b], 16)
                    w = a[name].rearrange("(c p) n -> p c n", p=P)
                    sp.dma_start(w_br[b][:, :, :], w[:, :, cols]).then_inc(w_ready[b], 16)

            loop(sp, loads)

        @block.gpsimd
        def _(pool):
            pool.dma_start(b_gate[:, :, :], a["b_gate"].rearrange("p (b e) -> p b e", e=DC)).then_inc(b_in, 16)
            if ex:
                ex.pool_tile(pool, tile, heads)

        @block.tensor
        def _(pe):
            pe.sem_inc(projected, UNITS)
            pe.wait_ge(h_in, 16)
            pe.wait_ge(o_in, 16)

            def blocks(g):
                for n in range(UNITS):
                    b, par = n // 2, n % 2
                    block = slice(par * P, (par + 1) * P)
                    if par == 0:
                        until(pe, w_ready[b], g * 32 + 32, passed)
                    until(pe, opened, done(g, n - 2), passed)
                    until(pe, gated, done(g, n - 2), passed)
                    for c in range(DC):
                        pe.matmul(ps_g[n % 2][:, 0:GROUP], w_gate[b][:, c, block], hT[:, c, :], start=(c == 0), stop=(c == DC - 1))
                    for c in range(4):
                        last = pe.matmul(ps_b[n % 2][:, 0:GROUP], w_br[b][:, c, block], oT[:, 4 * b + c, :], start=(c == 0), stop=(c == 3))
                    last.then_inc(projected, 1)
                    experts_beside("pe", pe, g, n)

            loop(pe, blocks)

        @block.scalar
        def _(act):
            act.dma_start(hT[:, :, :], s["hT"].rearrange("c p n -> p c n")[:, :, span.lo:span.hi]).then_inc(h_in, 16)
            act.dma_start(oT[:, :, :], s["oT"].rearrange("c p n -> p c n")[:, :, span.lo:span.hi]).then_inc(o_in, 16)
            act.wait_ge(b_in, 16)
            act.sem_inc(opened, UNITS)

            def blocks(g):
                for n in range(UNITS):
                    b, par = n // 2, n % 2
                    experts_beside("act_diag", act, g, n)
                    until(act, gated, done(g, n - 2), passed)
                    until(act, projected, done(g, n), passed)
                    act.activation(gate[n % 2][:, :], ps_g[n % 2][:, 0:GROUP], ACT.Sigmoid,
                                   bias=b_gate[:, b, bass.ds(g * 2 + par, 1)]).then_inc(opened, 1)
                    experts_beside("act_rest", act, g, n)

            loop(act, blocks)

        @block.vector
        def _(dve):
            dve.sem_inc(gated, UNITS)

            def blocks(g):
                for n in range(UNITS):
                    b, par = n // 2, n % 2
                    until(dve, opened, done(g, n), passed)
                    dve.drain()
                    dst = acc[par] if b == 0 else part
                    dve.tensor_tensor(dst[:, :], gate[n % 2][:, :], ps_b[n % 2][:, 0:GROUP], ALU.mult).then_inc(gated, 1)
                    if b:
                        dve.drain()
                        out = acc[par][:, :] if b == 1 else mergedT[:, bass.ds(g * 2 + par, 1), :].rearrange("p c n -> p (c n)")
                        dve.tensor_tensor(out, acc[par][:, :], part[:, :], ALU.add)
                    experts_beside("dve", dve, g, n)

            loop(dve, blocks)


def project_out(nc, a, s, mergedT, h2T, span, tag, ex=None, tile=None, heads=None):
    rows, NT = span.rows, len(span.tiles)
    with ExitStack() as ctx:
        sb, psum, sem = tools(nc, ctx, tag)
        ident = sb("ident", [P, P])
        w_o = sb("w_o", [P, DC, D])
        g_ffn = sb("g_ffn", [P, D])
        xt = [sb(f"xt{i}", [P, D]) for i in range(2)]
        x1 = [sb(f"x1{i}", [P, D]) for i in range(2)]
        h2 = [sb(f"h2{i}", [P, D]) for i in range(2)]
        ms, root, rs = sb("ms", [P, 2]), sb("root", [P, 2]), sb("rs", [P, 2])
        ps_o = [psum(f"out{i}", [P, D]) for i in range(2)]
        ps_t = [psum(f"turn{i}", [P, 512]) for i in range(2)]
        made, w_in, g_in = sem("identity"), sem("w_in"), sem("g_in")
        x_in = [sem(f"x_in{i}") for i in range(2)]
        projected, added, squares, roots, normed = (sem(n) for n in ("projected", "added", "squares", "roots", "normed"))
        turned, t_copied = sem("turned"), sem("t_copied")
        rows_out = [sem(f"rows_out{i}") for i in range(2)]
        block = ctx.enter_context(nc.Block())

        @block.gpsimd
        def _(pool):
            make_identity(pool, ident, made)
            if ex:
                ex.pool_tile(pool, tile, heads)

        @block.sync
        def _(sp):
            w = a["w_o"].rearrange("(c p) n -> p c n", p=P)
            for i in range(2):
                sp.dma_start(w_o[:, :, 512 * i:512 * i + 512], w[:, :, 512 * i:512 * i + 512]).then_inc(w_in, 16)
            sp.dma_start(g_ffn[:, :], a["norm_ffn"].to_broadcast([P, D])).then_inc(g_in, 16)

            def store(t):
                sp.wait_ge(normed, t + 1)
                own = slice(span.lo + t * P, span.lo + t * P + rows[t])
                sp.dma_start(s["x1"][own, :], x1[t % 2][0:rows[t], :]).then_inc(rows_out[t % 2], 16)
                sp.dma_start(s["h2"][own, :], h2[t % 2][0:rows[t], :]).then_inc(rows_out[t % 2], 16)

            for t in range(NT):
                if t >= 2:
                    sp.wait_ge(added, t - 1)
                sp.dma_start(xt[t % 2][0:rows[t], :], a["x_all"][span.lo + t * P:span.lo + t * P + rows[t], :]).then_inc(x_in[t % 2], 16)
                if t:
                    store(t - 1)
            store(NT - 1)
            for i in range(2):
                sp.wait_ge(rows_out[i], 32 * ((NT + 1 - i) // 2))

        @block.tensor
        def _(pe):
            def project(t):
                if t >= 2:
                    pe.wait_ge(added, t - 1)
                r = rows[t]
                for i in range(2):
                    for c in range(DC):
                        last = pe.matmul(ps_o[t % 2][0:r, 512 * i:512 * i + 512], mergedT[:, c, t * P:t * P + r],
                                         w_o[:, c, 512 * i:512 * i + 512], start=(c == 0), stop=(c == DC - 1))
                last.then_inc(projected, 1)

            pe.wait_ge(made, 2)
            pe.wait_ge(w_in, 32)
            project(0)
            for t in range(NT):
                if t + 1 < NT:
                    project(t + 1)
                pe.wait_ge(normed, t + 1)
                r = rows[t]
                for i in range(2):
                    if t or i >= 2:
                        pe.wait_ge(t_copied, 2 * t + i - 1)
                    for b in range(4):
                        c = 4 * i + b
                        last = pe.transpose(ps_t[i][:, b * P:b * P + r], h2[t % 2][0:r, c * P:(c + 1) * P], ident[0:r, 0:r])
                    last.then_inc(turned, 1)
                beside(ex, "pe", pe, tile, heads, t, NT)

        @block.scalar
        def _(act):
            def take_root(t):
                act.wait_ge(squares, t + 1)
                act.activation(root[0:rows[t], t % 2:t % 2 + 1], ms[0:rows[t], t % 2:t % 2 + 1], ACT.Sqrt).then_inc(roots, 1)

            for t in range(NT):
                take_root(t)
                r = rows[t]
                for i in range(2):
                    act.wait_ge(turned, 2 * t + i + 1)
                    act.activation(h2T[:, 4 * i:4 * i + 4, t * P:t * P + r],
                                   ps_t[i][:, :].rearrange("p (c n) -> p c n", n=P)[:, :, 0:r], ACT.Copy).then_inc(t_copied, 1)
                beside(ex, "act", act, tile, heads, t, NT)

        @block.vector
        def _(dve):
            dve.wait_ge(g_in, 16)
            for t in range(NT):
                r, p = rows[t], t % 2
                dve.wait_ge(x_in[p], 16 * (t // 2 + 1))
                if t >= 2:
                    dve.wait_ge(rows_out[p], 32 * (t // 2))
                    dve.wait_ge(turned, 2 * (t - 1))
                dve.wait_ge(projected, t + 1)
                dve.tensor_tensor(x1[p][0:r, :], ps_o[p][0:r, :], xt[p][0:r, :], ALU.add).then_inc(added, 1)
                dve.drain()
                dve.tensor_tensor_reduce(out=h2[p][0:r, :], in0=x1[p][0:r, :], in1=x1[p][0:r, :], scale=1.0 / D, scalar=EPS,
                                         op0=ALU.mult, op1=ALU.add, accum_out=ms[0:r, p:p + 1]).then_inc(squares, 1)
                dve.drain()
                dve.wait_ge(roots, t + 1)
                dve.reciprocal(rs[0:r, p:p + 1], root[0:r, p:p + 1])
                dve.drain()
                dve.scalar_tensor_tensor(out=h2[p][0:r, :], in0=x1[p][0:r, :], scalar=rs[0:r, p:p + 1], in1=g_ffn[0:r, :],
                                         op0=ALU.mult, op1=ALU.mult).then_inc(normed, 1)
                beside(ex, "dve", dve, tile, heads, t, NT)


def score_experts(nc, a, s, h2T, span, tag, ex=None, tile=None, heads=None):
    rows, NT, GROUP = span.rows, len(span.tiles), span.width
    HALF = 2 * span.groups
    SETS = 2 * HALF
    SCORES = 2 * NT
    n_iter = HEADS // 2

    def done(g, per, n):
        return g * per + (per + n + 1)

    with ExitStack() as ctx:
        sb, psum, sem = tools(nc, ctx, tag)
        w_q = [sb(f"w_q{i}", [P, DC, QUERY]) for i in range(2)]
        skT = [sb(f"skT{i}", [P, 2, P]) for i in range(2)]
        qT = [sb(f"qT{i}", [P, 2, span.n]) for i in range(2)]
        sc = [sb(f"sc{i}", [P, NT, QUERY]) for i in range(2)]
        ps_q = [psum(f"q{i}", [P, 512]) for i in range(2)]
        ps_s = [psum(f"s{i}", [P, 512]) for i in range(2)]
        passed = sem("loop_waits")
        w_ready = [sem(f"w_ready{i}") for i in range(2)]
        queried, q_copied, scored, s_copied = (sem(n) for n in ("queried", "q_copied", "scored", "s_copied"))
        sc_out = [sem(f"sc_out{i}") for i in range(2)]
        prompt_tiles = NT - span.sample
        first_tile = span.tiles[0]
        prompt_groups = s["sc"][0:KEY_TILES * HEADS, :, :].rearrange("(t h) p n -> p h t n", h=HEADS)
        sample_rows = s["sc"].rearrange("g p n -> (g p) n")
        block = ctx.enter_context(nc.Block())

        def loop(eng, body):
            if ex:
                for g in range(n_iter):
                    body(g)
            else:
                with eng.Fori(0, n_iter) as g:
                    body(g)

        def experts_beside(kind, eng, g, n):
            beside(ex, kind, eng, tile, heads, g * SETS + n, n_iter * SETS)

        @block.sync
        def _(sp):
            def load_weights(g, par):
                w = a["peer_wq"].rearrange("(c p) n -> p c n", p=P)
                sp.dma_start(w_q[par][:, :, :], w[:, :, bass.ds(g * (2 * QUERY) + par * QUERY, QUERY)]).then_inc(w_ready[par], 16)
                sp.dma_start(skT[par][:, :, :], s["skT"].rearrange("b d n -> d b n")[:, bass.ds(g * 4 + 2 * par, 2), :]).then_inc(w_ready[par], 16)

            def head_pair(g):
                for par in range(2):
                    until(sp, scored, done(g, SCORES, (par + 1) * NT - 1 - SCORES), passed)
                    load_weights(g, par)

            loop(sp, head_pair)

        @block.gpsimd
        def _(pool):
            def scores_stored(pool, h):
                pool.wait_ge(sc_out[h % 2], 16 * (1 + span.sample) * (h // 2 + 2))

            if ex:
                ex.pool_tile(pool, tile, heads, scores_stored)

        @block.tensor
        def _(pe):
            pe.sem_inc(scored, SCORES)

            def head_pair(g):
                for par in range(2):
                    until(pe, w_ready[par], g * 32 + 32, passed)
                    for i in range(HALF):
                        n, j, t = par * HALF + i, i // span.groups, i % span.groups
                        until(pe, q_copied, done(g, SETS, n - 2), passed)
                        for c in range(DC):
                            last = pe.matmul(ps_q[n % 2][:, 0:GROUP], w_q[par][:, c, j * P:(j + 1) * P],
                                             h2T[:, c, t * GROUP:(t + 1) * GROUP], start=(c == 0), stop=(c == DC - 1))
                        last.then_inc(queried, 1)
                        experts_beside("pe", pe, g, n)
                    until(pe, q_copied, done(g, SETS, par * HALF + HALF - 1), passed)
                    for t in range(NT):
                        n = par * NT + t
                        until(pe, s_copied, done(g, SCORES, n - 2), passed)
                        for j in range(2):
                            last = pe.matmul(ps_s[n % 2][0:rows[t], j * P:(j + 1) * P], qT[par][:, j, t * P:t * P + rows[t]],
                                             skT[par][:, j, :], start=True, stop=True)
                        last.then_inc(scored, 1)

            loop(pe, head_pair)

        @block.scalar
        def _(act):
            act.sem_inc(q_copied, SETS)
            for i in range(2):
                act.sem_inc(sc_out[i], 16 * (1 + span.sample))

            def head_pair(g):
                for par in range(2):
                    until(act, scored, done(g, SCORES, (par + 1) * NT - 1 - SCORES), passed)
                    for i in range(HALF):
                        n, j, t = par * HALF + i, i // span.groups, i % span.groups
                        experts_beside("act_diag", act, g, n)
                        until(act, queried, g * SETS + (n + 1), passed)
                        act.activation(qT[par][:, j, t * GROUP:(t + 1) * GROUP], ps_q[n % 2][:, 0:GROUP], ACT.Copy).then_inc(q_copied, 1)
                        experts_beside("act_rest", act, g, n)
                    until(act, s_copied, done(g, SCORES, (par + 1) * NT - 1), passed)
                    dst = prompt_groups[:, bass.ds(g * 2 + par, 1), first_tile:first_tile + prompt_tiles, :].rearrange("p h t n -> p (h t) n")
                    act.dma_start(dst, sc[par][:, 0:prompt_tiles, :]).then_inc(sc_out[par], 16)
                    if span.sample:
                        row = (g * 2 + par) * DEC + KEY_TILES * HEADS * P
                        act.dma_start(sample_rows[bass.ds(row, DEC), :], sc[par][0:DEC, NT - 1, :]).then_inc(sc_out[par], 16)

            loop(act, head_pair)
            for i in range(2):
                act.wait_ge(sc_out[i], 16 * (1 + span.sample) * (n_iter + 1))

        @block.vector
        def _(dve):
            dve.sem_inc(s_copied, SCORES)

            def head_pair(g):
                for par in range(2):
                    for i in range(HALF):
                        experts_beside("dve", dve, g, par * HALF + i)
                    per = 16 * (1 + span.sample)
                    until(dve, sc_out[par], g * per + per, passed)
                    for t in range(NT):
                        n = par * NT + t
                        until(dve, scored, done(g, SCORES, n), passed)
                        dve.tensor_copy(sc[par][0:rows[t], t, :], ps_s[n % 2][0:rows[t], 0:QUERY]).then_inc(s_copied, 1)

            loop(dve, head_pair)


SLOTS_G = 8
PACK = P // DEC
PROMPT_GROUPS = KEY_TILES * HEADS
GROUPS_ALL = PROMPT_GROUPS + HEADS // PACK
RANK_AHEAD = 3
SAMPLE = KEY_TILES
LAST_TILES = [span.tiles[-1] for span in SPANS[:-1]]
LOWEST = -3.0e38
DIAGS = 4


class Split:

    def __init__(self, dve_slots):
        self.on_dve = [c for c in range(TOPK) if c % SLOTS_G in dve_slots]
        self.on_pe = [c for c in range(TOPK) if c % SLOTS_G not in dve_slots]
        self.side = {"on_dve": self.on_dve, "on_pe": self.on_pe}


COMMON = Split((3, 7))
DENSE = Split((1, 3, 5, 7))


class Experts:

    def __init__(self, nc, ctx, a, s):
        self.nc, self.a, self.s = nc, a, s
        sb, psum, sem = tools(nc, ctx, "G")
        self.ident, self.fold = sb("ident", [P, P]), sb("fold", [P, DEC])
        self.h2, self.h2_next = sb("h2", [P, D]), sb("h2_next", [P, D])
        self.x1, self.y, self.acc, self.g_fin = sb("x1", [P, D]), sb("y", [P, D]), sb("acc", [P, D]), sb("g_fin", [P, D])
        self.u_rows = [sb(f"u_rows{i}", [P, D]) for i in range(SLOTS_G)]
        self.v_rows = [sb(f"v_rows{i}", [P, D]) for i in range(SLOTS_G)]
        self.sc = [sb(f"sc{i}", [P, 2, P]) for i in range(2)]
        self.rest = sb("rest", [P, 2, P])
        self.best1, self.pos1 = sb("best1", [P, 2, TOPK]), sb("pos1", [P, 2, TOPK], U32)
        self.pos1f = sb("pos1f", [P, 2, TOPK])
        self.cand = sb("cand", [P, TOPK, TOPK])
        self.cand_rest = sb("cand_rest", [P, TOPK, TOPK])
        self.best, self.sel = sb("best", [P, TOPK]), sb("sel", [P, TOPK], U32)
        self.part, self.partf = sb("part", [P, 2, TOPK], U32), sb("partf", [P, 2, TOPK])
        self.ranks = sb("ranks", [P, TOPK])
        self.hot = sb("hot", [P, 2 * TOPK, TOPK])
        self.key = sb("key", [P, 2, TOPK])
        self.nbest, self.esum, self.einv = sb("nbest", [P, 1]), sb("esum", [P, 1]), sb("einv", [P, 1])
        self.egate = sb("egate", [P, TOPK])
        self.idx = [sb(f"idx{h}", [P, TOPK], I32) for h in range(HEADS)]
        self.gates = [sb(f"gates{h}", [P, TOPK]) for h in range(HEADS)]
        self.dots = [sb(f"dots{i}", [P, TOPK]) for i in range(2)]
        self.gelus = [sb(f"gelus{i}", [P, TOPK]) for i in range(2)]
        self.weights = [sb(f"weights{i}", [P, TOPK]) for i in range(2)]
        self.diag = [sb(f"diag{i}", [P, P]) for i in range(DIAGS)]
        self.ms, self.root, self.rs = sb("ms", [P, 1]), sb("root", [P, 1]), sb("rs", [P, 1])
        self.ps_y = psum("y_sum", [P, D])

        self.passed = sem("loop_waits")
        self.made, self.ranks_made, self.fold_made = sem("identity"), sem("ranks_made"), sem("fold_made")
        self.g_in, self.h2_in, self.h2_copied, self.x1_in = sem("g_in"), sem("h2_in"), sem("h2_copied"), sem("x1_in")
        self.sc_in = [sem(f"sc_in{i}") for i in range(2)]
        self.u_in = [sem(f"u_in{i}") for i in range(SLOTS_G)]
        self.v_in = [sem(f"v_in{i}") for i in range(SLOTS_G)]
        self.scores_read, self.ranked = sem("scores_read"), sem("ranked")
        self.gate_max, self.gate_exped = sem("gate_max"), sem("gate_exped")
        self.dotted, self.group_dotted = sem("dotted"), sem("group_dotted")
        self.gelu_done, self.weighted = sem("gelu_done"), sem("weighted")
        self.diag_made, self.weighed, self.added = sem("diag_made"), sem("weighed"), sem("added")
        self.y_taken, self.squares, self.roots = sem("y_taken"), sem("squares"), sem("roots")
        self.y_ready, self.y_out = sem("y_ready"), sem("y_out")

    @staticmethod
    def follows(t, h):
        return not (isinstance(t, int) and t == SAMPLE and h == HEADS // PACK - 1)

    @staticmethod
    def rankings(t, h):
        if isinstance(t, int) and t in LAST_TILES and h > HEADS - 1 - RANK_AHEAD:
            return {5: [], 6: [(2, (2, 5, 8, 11), 10, 15)],
                    7: [(2, (0, 1, 2, 3), 4, 5), (3, (6, 8, 10, 12), 14, 15)]}[h]
        if isinstance(t, int) and t * HEADS + h + RANK_AHEAD >= GROUPS_ALL:
            return []
        return [(RANK_AHEAD, (2, 5, 8, 11), 10, 15)]

    @staticmethod
    def split(t):
        return DENSE if isinstance(t, int) and t in LAST_TILES else COMMON

    def before(self, side, t, h):
        common, own = len(COMMON.side[side]), len(self.split(t).side[side])
        dense = sum(tile < t for tile in LAST_TILES) if isinstance(t, int) else self.dense_before
        more = dense * HEADS * (len(DENSE.side[side]) - common)
        return t * (HEADS * common) + (more + h * own)

    def at(self, side, t, h, c):
        experts = self.split(t).side[side]
        place = experts.index(c) if c >= 0 else experts.index(c + TOPK) - len(experts)
        return self.before(side, t, h) + (len(COMMON.side[side]) + place + 1)

    def pool_start(self, pool):
        make_identity(pool, self.ident, self.made)
        pool.iota(self.ranks[:, :], pattern=[[1, TOPK]], base=0, channel_multiplier=0,
                  allow_small_or_imprecise_dtypes=True).then_inc(self.ranks_made, 1)
        pool.dma_start(self.g_fin[:, :], self.a["norm_final"].to_broadcast([P, D])).then_inc(self.g_in, 16)
        for m in range(2):
            self.load_scores(pool, m, m)
        self.load_h2(pool, 0)
        pool.wait_ge(self.ranked, 1)
        for c in range(TOPK):
            if c >= SLOTS_G:
                pool.wait_ge(self.dotted, c - SLOTS_G + 1)
            self.gather(pool, self.u_rows[c % SLOTS_G], self.a["peer_u"], 0, c, self.u_in[c % SLOTS_G])
        self.load_scores(pool, 2, 0)

    def gather(self, pool, buf, table, slot, c, signal):
        pool.indirect_dma_start(out=buf[:, :], out_offset=None, in_=table,
                                in_offset=bass.IndirectOffsetOnAxis(ap=self.idx[slot][:, c:c + 1], axis=0)).then_inc(signal, 16)

    def load_scores(self, pool, m, par):
        if not (isinstance(m, int) and m < 2):
            until(pool, self.scores_read, m - 1, self.passed)
        src = self.s["sc"][m, :, :] if isinstance(m, int) else self.s["sc"][bass.ds(m, 1), :, :].rearrange("g p n -> (g p) n")
        pool.dma_start(self.sc[par][:, :, :].rearrange("p j n -> p (j n)"), src).then_inc(self.sc_in[par], 16)

    def load_h2(self, pool, t):
        rows = self.s["h2"]
        if isinstance(t, int) and t == SAMPLE:
            for q in range(PACK):
                pool.dma_start(self.h2_next[DEC * q:DEC * (q + 1), :], rows[SEQ:TOK, :]).then_inc(self.h2_in, 16)
        else:
            own = slice(t * P, (t + 1) * P) if isinstance(t, int) else bass.ds(t * P, P)
            pool.dma_start(self.h2_next[:, :], rows[own, :]).then_inc(self.h2_in, 16)

    def pool_tile(self, pool, t, heads, scores_stored=None):
        sample = isinstance(t, int) and t == SAMPLE
        for h in heads:
            n = t * HEADS + h
            follow = self.follows(t, h)
            for ahead, *_ in self.rankings(t, h):
                if isinstance(t, int) and t in LAST_TILES and h + ahead >= HEADS:
                    scores_stored(pool, h + ahead - HEADS)
                self.load_scores(pool, n + ahead, (h + ahead) % 2)
            if follow:
                until(pool, self.ranked, n + 2, self.passed)
            for c in range(TOPK):
                k = c % SLOTS_G
                side, signal = ("on_dve", self.added) if c in self.split(t).on_dve else ("on_pe", self.weighed)
                until(pool, signal, self.at(side, t, h, c - SLOTS_G), self.passed)
                self.gather(pool, self.v_rows[k], self.a["peer_v"], h % HEADS, c, self.v_in[k])
                if follow:
                    until(pool, self.dotted, n * TOPK + (TOPK + c - SLOTS_G + 1), self.passed)
                    self.gather(pool, self.u_rows[k], self.a["peer_u"], (h + 1) % HEADS, c, self.u_in[k])
                if c == SLOTS_G and h == (0 if sample else 2):
                    until(pool, self.y_ready, t + 1, self.passed)
                    r = DEC if sample else P
                    before = slice(t * P, (t + 1) * P) if isinstance(t, int) else bass.ds(t * P, P)
                    own = slice(t * P, t * P + r) if isinstance(t, int) else bass.ds(t * P, P)
                    pool.dma_start(self.s["y"][before, :], self.y[:, :]).then_inc(self.y_out, 16)
                    pool.dma_start(self.x1[0:r, :], self.s["x1"][own, :]).then_inc(self.x1_in, 16)
                if c == SLOTS_G and h == (6 if isinstance(t, int) and t in LAST_TILES else 3):
                    until(pool, self.h2_copied, t + 1, self.passed)
                    self.load_h2(pool, t + 1)

    def rank(self, dve, m, par, slot, piece):
        sc, rest, best1, pos1, best, sel = self.sc[par], self.rest, self.best1, self.pos1, self.best, self.sel
        flat, flat_rest = (b[:, :, :].rearrange("p a b -> p (a b)") for b in (self.cand, self.cand_rest))
        if piece == 0:
            until(dve, self.sc_in[par], (m // 2) * 16 + 16 if isinstance(m, int) else m * 8 + (16 - 8 * par), self.passed)
            for j in range(2):
                dve.max(best1[:, j, 0:8], sc[:, j, :])
            dve.drain()
            for j in range(2):
                dve.max_index(pos1[:, j, 0:8], best1[:, j, 0:8], sc[:, j, :])
                dve.match_replace(rest[:, j, :], best1[:, j, 0:8], sc[:, j, :], LOWEST)
            dve.drain().then_inc(self.scores_read, 1)
        elif piece == 1:
            for j in range(2):
                dve.max(best1[:, j, 8:16], rest[:, j, :])
            dve.drain()
            for j in range(2):
                dve.max_index(pos1[:, j, 8:16], best1[:, j, 8:16], rest[:, j, :])
            dve.tensor_tensor(self.cand[:, :, :], best1[:, 0, :].unsqueeze(2).to_broadcast([P, TOPK, TOPK]),
                              best1[:, 1, :].unsqueeze(1).to_broadcast([P, TOPK, TOPK]), ALU.add)
            dve.drain()
            dve.tensor_copy(self.pos1f[:, :, :], pos1[:, :, :])
        elif piece == 2:
            dve.max(best[:, 0:8], flat)
            dve.drain()
            dve.max_index(sel[:, 0:8], best[:, 0:8], flat)
            dve.match_replace(flat_rest, best[:, 0:8], flat, LOWEST)
            dve.tensor_scalar(self.nbest[:, :], best[:, 0:1], -1.0, None, ALU.mult)
            dve.drain()
            dve.max(best[:, 8:16], flat_rest)
            dve.drain().then_inc(self.gate_max, 1)
            dve.max_index(sel[:, 8:16], best[:, 8:16], flat_rest)
        else:
            dve.drain()
            dve.tensor_scalar(self.part[:, 0, :], sel[:, :], 4, None, ALU.logical_shift_right)
            dve.tensor_scalar(self.part[:, 1, :], sel[:, :], TOPK - 1, None, ALU.bitwise_and)
            dve.drain()
            dve.tensor_copy(self.partf[:, :, :], self.part[:, :, :])
            dve.drain()
            hot = self.hot
            dve.tensor_tensor(hot[:, :, :], self.ranks[:, :].unsqueeze(1).to_broadcast([P, 2 * TOPK, TOPK]),
                              self.partf[:, :, :].rearrange("p j k -> p (j k)").unsqueeze(2).to_broadcast([P, 2 * TOPK, TOPK]), ALU.is_equal)
            dve.drain()
            for j in range(2):
                half = hot[:, j * TOPK:(j + 1) * TOPK, :]
                dve.tensor_tensor(half, half, self.pos1f[:, j, :].unsqueeze(1).to_broadcast([P, TOPK, TOPK]), ALU.mult)
            dve.drain()
            dve.tensor_reduce(self.key[:, :, :].rearrange("p j k -> p (j k)"), hot[:, :, :], AX, ALU.add)
            dve.drain()
            dve.scalar_tensor_tensor(out=self.idx[slot][:, :], in0=self.key[:, 0, :], scalar=float(P), in1=self.key[:, 1, :],
                                     op0=ALU.mult, op1=ALU.add).then_inc(self.ranked, 1)

    def gate(self, dve, m, slot):
        until(dve, self.gate_exped, m + 1, self.passed)
        dve.reciprocal(self.einv[:, :], self.esum[:, :])
        dve.drain()
        dve.tensor_scalar(self.gates[slot][:, :], self.egate[:, :], self.einv[:, 0:1], None, ALU.mult)

    def dot(self, dve, m, par, c):
        k = c % SLOTS_G
        until(dve, self.u_in[k], m * 32 + (c // SLOTS_G * 16 + 16), self.passed)
        dve.tensor_tensor_reduce(out=self.u_rows[k][:, :], in0=self.u_rows[k][:, :], in1=self.h2[:, :], scale=1.0, scalar=0.0,
                                 op0=ALU.mult, op1=ALU.add, accum_out=self.dots[par][:, c:c + 1]).then_inc(self.dotted, 1)
        if c == TOPK - 1:
            dve.drain().then_inc(self.group_dotted, 1)

    def copy_h2(self, dve, t):
        until(dve, self.h2_in, 16 * (t + 1) if not (isinstance(t, int) and t == SAMPLE) else 16 * (SAMPLE + PACK), self.passed)
        dve.drain()
        dve.tensor_copy(self.h2[:, :], self.h2_next[:, :]).then_inc(self.h2_copied, 1)
        dve.drain()

    def dve_start(self, dve):
        dve.wait_ge(self.made, 2)
        dve.wait_ge(self.ranks_made, 1)
        fold, ident = self.fold, self.ident
        dve.tensor_copy(fold[:, :], ident[:, 0:DEC])
        for q in range(1, PACK):
            dve.drain()
            dve.tensor_tensor(fold[:, :], fold[:, :], ident[:, DEC * q:DEC * (q + 1)], ALU.add)
        dve.memset(self.y[:, :], 0.0)
        dve.drain()
        dve.sem_inc(self.fold_made, 1)
        dve.sem_inc(self.y_ready, 1)
        dve.sem_inc(self.added, len(COMMON.on_dve))
        dve.sem_inc(self.y_taken, 1)
        dve.wait_ge(self.g_in, 16)
        for m in range(2):
            for piece in range(4):
                self.rank(dve, m, m, m, piece)
            self.gate(dve, m, m)
        self.copy_h2(dve, 0)
        for c in range(TOPK):
            self.dot(dve, 0, 0, c)
        self.weigh(dve, 0, 0, 0, 0)
        for piece in range(4):
            self.rank(dve, 2, 0, 2, piece)
        self.gate(dve, 2, 2)

    def weigh(self, dve, m, par, slot, diags):
        until(dve, self.gelu_done, m + 1, self.passed)
        until(dve, self.diag_made, diags + 2 * len(COMMON.on_pe), self.passed)
        dve.drain()
        dve.tensor_tensor(self.weights[par][:, :], self.gelus[par][:, :], self.gates[slot][:, :], ALU.mult).then_inc(self.weighted, 1)

    def dve_step(self, dve, t, h, c):
        n, par = t * HEADS + h, h % 2
        for ahead, pieces, _, _ in self.rankings(t, h):
            if c in pieces:
                if c == pieces[0]:
                    until(dve, self.weighed, self.before("on_pe", t, h) + len(COMMON.on_pe), self.passed)
                self.rank(dve, n + ahead, (h + ahead) % 2, (h + ahead) % HEADS, pieces.index(c))
        if self.follows(t, h):
            if h == HEADS - 1 and c == 0:
                self.copy_h2(dve, t + 1)
            self.dot(dve, n + 1, (h + 1) % 2, c)
        if c in self.split(t).on_dve:
            k = c % SLOTS_G
            until(dve, self.v_in[k], n * 32 + (c // SLOTS_G * 16 + 16), self.passed)
            dve.drain()
            weight = self.weights[par][:, c:c + 1]
            if h == 0 and c == self.split(t).on_dve[0]:
                dve.tensor_scalar(self.acc[:, :], self.v_rows[k][:, :], weight, None, ALU.mult).then_inc(self.added, 1)
            else:
                dve.scalar_tensor_tensor(out=self.acc[:, :], in0=self.v_rows[k][:, :], scalar=weight, in1=self.acc[:, :],
                                         op0=ALU.mult, op1=ALU.add).then_inc(self.added, 1)
        if c == TOPK - 1 and self.follows(t, h):
            self.weigh(dve, n + 1, (h + 1) % 2, (h + 1) % HEADS, self.before("on_pe", t, h))
        for ahead, _, _, gate_at in self.rankings(t, h):
            if c == gate_at:
                self.gate(dve, n + ahead, (h + ahead) % HEADS)

    def dve_finish(self, dve, t):
        sample = isinstance(t, int) and t == SAMPLE
        r = DEC if sample else P
        x1, y = self.x1, self.y
        if sample:
            dve.wait_ge(self.weighed, self.at("on_pe", t, HEADS // PACK - 1, COMMON.on_pe[-1]) + 1)
        else:
            until(dve, self.weighed, self.at("on_pe", t, HEADS - 1, self.split(t).on_pe[-1]), self.passed)
        until(dve, self.x1_in, t * 16 + 16, self.passed)
        dve.tensor_tensor(x1[0:r, :], self.ps_y[0:r, :], x1[0:r, :], ALU.add).then_inc(self.y_taken, 1)
        dve.drain()
        if not sample:
            dve.tensor_tensor(x1[:, :], x1[:, :], self.acc[:, :], ALU.add)
            dve.drain()
        until(dve, self.y_out, t * 16 + 16, self.passed)
        dve.tensor_tensor_reduce(out=y[0:r, :], in0=x1[0:r, :], in1=x1[0:r, :], scale=1.0 / D, scalar=EPS,
                                 op0=ALU.mult, op1=ALU.add, accum_out=self.ms[0:r, :])
        dve.drain().then_inc(self.squares, 1)
        until(dve, self.roots, t + 1, self.passed)
        dve.reciprocal(self.rs[0:r, :], self.root[0:r, :])
        dve.drain()
        dve.scalar_tensor_tensor(out=y[0:r, :], in0=x1[0:r, :], scalar=self.rs[0:r, 0:1], in1=self.g_fin[0:r, :],
                                 op0=ALU.mult, op1=ALU.mult).then_inc(self.y_ready, 1)

    def gate_exp(self, act, m):
        until(act, self.gate_max, m + 1, self.passed)
        act.activation(self.egate[:, :], self.best[:, :], ACT.Exp, bias=self.nbest[:, 0:1], accum_out=self.esum[:, 0:1]).then_inc(self.gate_exped, 1)

    def gelu(self, act, m, par):
        until(act, self.group_dotted, m + 1, self.passed)
        act.activation(self.gelus[par][:, :], self.dots[par][:, :], ACT.Gelu).then_inc(self.gelu_done, 1)

    def act_start(self, act):
        act.wait_ge(self.made, 2)
        act.sem_inc(self.diag_made, 2 * len(COMMON.on_pe))
        self.gate_exp(act, 0)
        self.gate_exp(act, 1)
        self.gelu(act, 0, 0)
        self.gate_exp(act, 2)

    def act_diag(self, act, t, h, c):
        n = t * HEADS + h
        if c in self.split(t).on_pe:
            i = self.split(t).on_pe.index(c)
            sample = isinstance(t, int) and t == SAMPLE
            matrix, width = (self.fold, DEC) if sample else (self.ident, P)
            if i == 0:
                until(act, self.weighted, n + 1, self.passed)
                if sample:
                    act.wait_ge(self.fold_made, 1)
            until(act, self.weighed, self.before("on_pe", t, h) + (len(COMMON.on_pe) + i + 1 - DIAGS), self.passed)
            act.activation(self.diag[i % DIAGS][:, 0:width], matrix[:, 0:width], ACT.Copy,
                           scale=self.weights[h % 2][:, c:c + 1]).then_inc(self.diag_made, 1)

    def act_rest(self, act, t, h, c):
        n = t * HEADS + h
        for ahead, _, exp_at, _ in self.rankings(t, h):
            if c == exp_at:
                self.gate_exp(act, n + ahead)
        if c == TOPK - 1 and self.follows(t, h):
            self.gelu(act, n + 1, (h + 1) % 2)

    def act_finish(self, act, t):
        r = DEC if isinstance(t, int) and t == SAMPLE else P
        until(act, self.squares, t + 1, self.passed)
        act.activation(self.root[0:r, :], self.ms[0:r, :], ACT.Sqrt).then_inc(self.roots, 1)

    def pe_start(self, pe):
        pe.sem_inc(self.weighed, len(COMMON.on_pe))

    def pe_step(self, pe, t, h, c):
        on_pe = self.split(t).on_pe
        if c not in on_pe:
            return
        n, k, i = t * HEADS + h, c % SLOTS_G, on_pe.index(c)
        sample = isinstance(t, int) and t == SAMPLE
        r = DEC if sample else P
        if h == 0 and i == 0:
            until(pe, self.y_taken, t + 1, self.passed)
        until(pe, self.v_in[k], n * 32 + (c // SLOTS_G * 16 + 16), self.passed)
        until(pe, self.diag_made, self.before("on_pe", t, h) + (2 * len(COMMON.on_pe) + i + 1), self.passed)
        for half in range(2):
            cols = slice(512 * half, 512 * (half + 1))
            last = pe.matmul(self.ps_y[0:r, cols], self.diag[i % DIAGS][:, 0:r], self.v_rows[k][:, cols],
                             start=(h == 0 and i == 0), stop=(not sample and h == HEADS - 1 and c == on_pe[-1]))
        last.then_inc(self.weighed, 1)

    def pe_finish(self, pe, t):
        if isinstance(t, int) and t == SAMPLE:
            pe.wait_ge(self.added, self.at("on_dve", t, HEADS // PACK - 1, COMMON.on_dve[-1]))
            for half in range(2):
                cols = slice(512 * half, 512 * (half + 1))
                last = pe.matmul(self.ps_y[0:DEC, cols], self.fold[:, :], self.acc[:, cols], start=False, stop=True)
            last.then_inc(self.weighed, 1)

    def atom(self, kind, eng, t, h, c):
        parts = {"pe": (self.pe_step, self.pe_finish), "dve": (self.dve_step, self.dve_finish),
                 "act": (self.act_diag, self.act_rest, self.act_finish),
                 "act_diag": (self.act_diag,), "act_rest": (self.act_rest, self.act_finish)}[kind]
        groups = HEADS // PACK if isinstance(t, int) and t == SAMPLE else HEADS
        last = h == groups - 1 and c == TOPK - 1
        for part in parts:
            if part not in (self.pe_finish, self.dve_finish, self.act_finish):
                part(eng, t, h, c)
            elif last:
                part(eng, t)

    def last_run(self):
        first, loops = SPANS[-1].tiles[0], KEY_TILES - 1 - SPANS[-1].tiles[0]
        with self.nc.Block() as block:
            def steps(kind, eng, t, heads):
                for h in range(heads):
                    for c in range(TOPK):
                        self.atom(kind, eng, t, h, c)

            def tiles(kind, eng):
                with eng.Fori(0, loops) as i:
                    steps(kind, eng, i + first, HEADS)
                steps(kind, eng, KEY_TILES - 1, HEADS)
                steps(kind, eng, SAMPLE, HEADS // PACK)

            @block.gpsimd
            def _(pool):
                with pool.Fori(0, loops) as i:
                    self.pool_tile(pool, i + first, range(HEADS))
                self.pool_tile(pool, KEY_TILES - 1, range(HEADS))
                self.pool_tile(pool, SAMPLE, range(HEADS // PACK))
                pool.wait_ge(self.y_ready, SAMPLE + 2)
                pool.dma_start(self.s["y"][P + SEQ:P + TOK, :], self.y[0:DEC, :]).then_inc(self.y_out, 16)
                pool.wait_ge(self.y_out, 16 * (SAMPLE + 2))

            @block.vector
            def _(dve):
                tiles("dve", dve)

            @block.scalar
            def _(act):
                tiles("act", act)

            @block.tensor
            def _(pe):
                tiles("pe", pe)


def build(nc, a, outs):
    s = dict(outs)
    for name, shape in (("hT", (DC, P, ROWS)), ("vm", (KEYS, BR)), ("kT", (HEADS, QK, KEYS)), ("qT", (HEADS, QK, ROWS)),
                        ("dkT", (4, P, KEYS)), ("dqT", (4, P, ROWS)), ("mqT", (MEM_HEADS, P, ROWS)),
                        ("mkT", (2, MEM_HEADS, P, MEM)), ("oT", (3 * BR // P, P, ROWS)), ("skT", (2 * HEADS, P, P)),
                        ("x1", (ROWS, D)), ("h2", (ROWS, D)), ("h2T", (DC, P, ROWS)), ("sc", (66, P, 2 * P))):
        s[name] = nc.dram_tensor(f"scratch_{name}", shape, F32, kind="Internal").ap()
    project_inputs(nc, a, s)
    cached_and_memory_keys(nc, a, s)
    attention(nc, a, s, SPANS[0], "C0")
    with ExitStack() as ctx:
        mergedT = ctx.enter_context(nc.sbuf_tensor("mergedT0", [P, DC, SPANS[0].n], F32))
        merge_branches(nc, a, s, mergedT, SPANS[0], "D0")
        h2T = ctx.enter_context(nc.sbuf_tensor("h2T0", [P, DC, SPANS[0].n], F32))
        project_out(nc, a, s, mergedT, h2T, SPANS[0], "E0")
        score_experts(nc, a, s, h2T, SPANS[0], "F0")
    with ExitStack() as experts_ctx:
        ex = Experts(nc, experts_ctx, a, s)
        for i, span in enumerate(SPANS[1:], 1):
            *first, last = SPANS[i - 1].tiles
            ex.dense_before = i - 1
            attention(nc, a, s, span, f"C{i}", ex, first)
            with ExitStack() as ctx:
                mergedT = ctx.enter_context(nc.sbuf_tensor(f"mergedT{i}", [P, DC, span.n], F32))
                merge_branches(nc, a, s, mergedT, span, f"D{i}", ex, last, range(0, 4))
                h2T = ctx.enter_context(nc.sbuf_tensor(f"h2T{i}", [P, DC, span.n], F32))
                project_out(nc, a, s, mergedT, h2T, span, f"E{i}", ex, last, range(4, 5))
                score_experts(nc, a, s, h2T, span, f"F{i}", ex, last, range(5, HEADS))
        ex.dense_before = len(LAST_TILES)
        ex.last_run()


_WEIGHTS = ["norm_mix", "w_in", "mla_q_norm", "w_uq", "mla_kv_norm", "w_uk", "w_uv", "diff_lq1", "diff_lk1",
            "diff_lq2", "diff_lk2", "diff_subln", "norm_mem", "w_mem_kv", "w_br_a", "w_br_b", "w_br_m", "w_gate",
            "b_gate", "w_o", "norm_ffn", "peer_wq", "peer_subkeys", "peer_u", "peer_v", "norm_final",
            "cache_mla_ckv", "cache_mla_krope", "cache_diff_k", "cache_diff_v", "cache_mem_k", "cache_mem_v",
            "mem_prompt"]


def rotary_table():
    half = ROPE // 2
    pos = np.concatenate([np.arange(SEQ), PAST + np.arange(PAD_ROWS - SEQ)]).astype(np.float32)
    inv = (1.0 / (np.float32(10000.0) ** (np.arange(half, dtype=np.float32) / np.float32(half)))).astype(np.float32)
    ang = pos[:, None] * inv[None, :]
    return np.concatenate([np.cos(ang), np.sin(ang)], axis=-1).astype(np.float32)


def kernel(**inputs):
    import concourse.bacc as bacc
    from concourse.bass_utils import run_bass_kernel_spmd as run

    nc = bacc.Bacc("TRN2", target_bir_lowering=False, num_devices=1)
    arrays, a = {}, {}

    def take(name, array):
        arrays[f"in_{name}"] = array
        a[name] = nc.dram_tensor(f"in_{name}", array.shape, F32, kind="ExternalInput").ap()

    x_all = np.zeros((PAD_ROWS, D), np.float32)
    x_all[0:SEQ] = inputs["x_prompt"][0]
    x_all[SEQ:TOK] = inputs["x_sample"][0]
    take("x_all", x_all)
    take("cos_sin", rotary_table())
    for name in _WEIGHTS:
        w = np.ascontiguousarray(inputs[name])
        if name == "peer_subkeys":
            w = w.reshape(2 * HEADS * P, P)
        elif name == "b_gate":
            w = np.ascontiguousarray(w.reshape(-1, P).T)
        elif name.startswith("cache"):
            w = w.reshape(w.shape[2], -1)
        elif w.ndim == 3:
            w = w[0]
        elif w.ndim == 1:
            w = w.reshape(1, -1)
        take(name, w)

    outs = {name: nc.dram_tensor(f"out_{name}", shape, F32, kind="ExternalOutput").ap() for name, shape in
            (("y", (P + TOK, D)), ("ckv", (ROWS, KV_LORA)), ("krope", (ROWS, ROPE)), ("dk", (ROWS, BR)), ("dv", (ROWS, BR)),
             ("mk", (MEM, BR)), ("mv", (MEM, BR)))}
    build(nc, a, outs)
    got = run(nc, [arrays], core_ids=[0]).results[0]

    def rows(name, lo, hi, *shape):
        return got[f"out_{name}"][lo:hi].reshape(*shape)

    prompt, sample = (1, 1, SEQ), (1, 1, DEC)
    return (rows("y", P, P + SEQ, 1, SEQ, D), rows("y", P + SEQ, P + TOK, 1, DEC, D),
            rows("ckv", 0, SEQ, *prompt, KV_LORA), rows("krope", 0, SEQ, *prompt, ROPE),
            rows("dk", 0, SEQ, *prompt, HEADS, VD), rows("dv", 0, SEQ, *prompt, HEADS, VD),
            rows("mk", 0, MEM, 1, 1, MEM, MEM_HEADS, MDH), rows("mv", 0, MEM, 1, 1, MEM, MEM_HEADS, MDH),
            rows("ckv", SEQ, TOK, *sample, KV_LORA), rows("krope", SEQ, TOK, *sample, ROPE),
            rows("dk", SEQ, TOK, *sample, HEADS, VD), rows("dv", SEQ, TOK, *sample, HEADS, VD))
```
